# Optimizing a Trainium2 kernel written in Bass

```python
import math
import jax, jax.numpy as jnp
from jax import lax
import numpy as np

D_MODEL = 2048
BATCH = 1
SEQ = 1024
DEPTH = 1

CHUNK = 64
EPS = 1e-6

S5_WIDTH = D_MODEL // 2
S5_GROUP = 16
S5_GROUPS = S5_WIDTH // S5_GROUP
S5_STATE = 64
S5_DT_MIN = 1e-3
S5_DT_MAX = 1e-1

RET_HEADS = 8
RET_WIDTH = D_MODEL // 2
RET_V_HEAD = RET_WIDTH // RET_HEADS
RET_QK_HEAD = RET_V_HEAD // 2
RET_QK = RET_HEADS * RET_QK_HEAD
ROPE_BASE = 10000.0

COL_SIZES = (S5_WIDTH, S5_WIDTH, RET_QK, RET_QK, RET_WIDTH, RET_WIDTH, D_MODEL, D_MODEL)
IN_COLS = 2 * S5_WIDTH + 2 * RET_QK + 2 * RET_WIDTH + 2 * D_MODEL
SPLIT_IDX = (S5_WIDTH,
             2 * S5_WIDTH,
             2 * S5_WIDTH + RET_QK,
             2 * S5_WIDTH + 2 * RET_QK,
             2 * S5_WIDTH + 2 * RET_QK + RET_WIDTH,
             2 * S5_WIDTH + 2 * RET_QK + 2 * RET_WIDTH,
             2 * S5_WIDTH + 2 * RET_QK + 2 * RET_WIDTH + D_MODEL)

kernel_name = "hybrid_s5_retention_gated_block"

def rms_norm(x, gain):
    xf = x.astype(jnp.float32)
    y = xf * lax.rsqrt(jnp.mean(xf * xf, axis=-1, keepdims=True) + EPS)
    return (y * gain.astype(jnp.float32)).astype(x.dtype)

def s5_mixer(u, lam_re, lam_im, log_step, b_re, b_im, c_re, c_im, d_skip, w_glu, b_glu):
    bsz, seq, _ = u.shape
    f32 = jnp.float32
    uf = u.astype(f32).reshape(bsz, seq, S5_GROUPS, S5_GROUP)
    lr = lam_re.astype(f32)
    li = lam_im.astype(f32)
    step = jnp.exp(log_step.astype(f32))[:, None]
    mag = jnp.exp(lr * step)
    ang = li * step
    ab_re = mag * jnp.cos(ang)
    ab_im = mag * jnp.sin(ang)
    den = lr * lr + li * li
    nr = ab_re - 1.0
    f_re = (nr * lr + ab_im * li) / den
    f_im = (ab_im * lr - nr * li) / den
    br = b_re.astype(f32)
    bi = b_im.astype(f32)
    bb_re = f_re[..., None] * br - f_im[..., None] * bi
    bb_im = f_re[..., None] * bi + f_im[..., None] * br
    bu_re = jnp.einsum('blgh,gph->blgp', uf, bb_re)
    bu_im = jnp.einsum('blgh,gph->blgp', uf, bb_im)
    a_re = jnp.broadcast_to(ab_re, bu_re.shape)
    a_im = jnp.broadcast_to(ab_im, bu_re.shape)

    def combine(e1, e2):
        a1r, a1i, b1r, b1i = e1
        a2r, a2i, b2r, b2i = e2
        return (a2r * a1r - a2i * a1i,
                a2r * a1i + a2i * a1r,
                a2r * b1r - a2i * b1i + b2r,
                a2r * b1i + a2i * b1r + b2i)

    _, _, xr, xi = lax.associative_scan(combine, (a_re, a_im, bu_re, bu_im), axis=1)
    y = (jnp.einsum('blgp,ghp->blgh', xr, c_re.astype(f32))
         - jnp.einsum('blgp,ghp->blgh', xi, c_im.astype(f32))
         + d_skip.astype(f32).reshape(S5_GROUPS, S5_GROUP) * uf)
    y = y.reshape(bsz, seq, S5_WIDTH)
    g = jax.nn.gelu(y)
    out = g * jax.nn.sigmoid(g @ w_glu.astype(f32) + b_glu.astype(f32))
    return out.astype(u.dtype)

def rotary(t, seq):
    d = t.shape[-1]
    inv = ROPE_BASE ** (-jnp.arange(0, d, 2, dtype=jnp.float32) / d)
    pos = jnp.arange(seq, dtype=jnp.float32)
    angle = pos[:, None] * inv[None, :]
    cos = jnp.cos(angle)[None, :, None, :]
    sin = jnp.sin(angle)[None, :, None, :]
    t1, t2 = t[..., : d // 2], t[..., d // 2:]
    return jnp.concatenate([t1 * cos - t2 * sin, t1 * sin + t2 * cos], axis=-1)

def retention(q, k, v):
    bsz, seq, _ = q.shape
    f32 = jnp.float32
    n = seq // CHUNK
    qh = rotary(q.astype(f32).reshape(bsz, seq, RET_HEADS, RET_QK_HEAD), seq)
    kh = rotary(k.astype(f32).reshape(bsz, seq, RET_HEADS, RET_QK_HEAD), seq) * (RET_QK_HEAD ** -0.5)
    vh = v.astype(f32).reshape(bsz, seq, RET_HEADS, RET_V_HEAD)
    qc = qh.reshape(bsz, n, CHUNK, RET_HEADS, RET_QK_HEAD)
    kc = kh.reshape(bsz, n, CHUNK, RET_HEADS, RET_QK_HEAD)
    vc = vh.reshape(bsz, n, CHUNK, RET_HEADS, RET_V_HEAD)
    log_g = jnp.log1p(-jnp.exp2(-5.0 - jnp.arange(RET_HEADS, dtype=f32)))
    idx = jnp.arange(CHUNK, dtype=f32)
    dmat = jnp.exp(jnp.abs(idx[:, None] - idx[None, :])[None] * log_g[:, None, None])
    scores = jnp.einsum('bnihd,bnjhd->bnhij', qc, kc) * dmat
    inner = jnp.einsum('bnhij,bnjhe->bnihe', scores, vc)
    zeta = jnp.exp((CHUNK - 1.0 - idx)[None, :] * log_g[:, None])
    kv = jnp.einsum('bnjhd,hj,bnjhe->bnhde', kc, zeta, vc)
    chunk_decay = jnp.exp(CHUNK * log_g)[None, :, None, None]

    def step(state, kv_i):
        return state * chunk_decay + kv_i, state

    init = jnp.zeros((bsz, RET_HEADS, RET_QK_HEAD, RET_V_HEAD), f32)
    _, prev = lax.scan(step, init, jnp.moveaxis(kv, 1, 0))
    prev = jnp.moveaxis(prev, 0, 1)
    xi = jnp.exp((idx + 1.0)[None, :] * log_g[:, None])
    cross = jnp.einsum('bnihd,bnhde,hi->bnihe', qc, prev, xi)
    o = (inner + cross).reshape(bsz, seq, RET_HEADS, RET_V_HEAD)
    o = o * lax.rsqrt(jnp.mean(o * o, axis=-1, keepdims=True) + EPS)
    return o.reshape(bsz, seq, RET_WIDTH).astype(q.dtype)

def setup_inputs(seed: int = 0) -> dict:
    key = jax.random.key(seed)
    ks = jax.random.split(key, 20)
    f32 = jnp.float32
    nrm = lambda k, s: jax.random.normal(k, s, f32)
    x = nrm(ks[0], (BATCH, SEQ, D_MODEL))
    norm_pre = 1.0 + 0.01 * nrm(ks[1], (DEPTH, D_MODEL))
    w_in = nrm(ks[2], (DEPTH, D_MODEL, IN_COLS)) * D_MODEL ** -0.5
    lam_re = -0.5 + 0.01 * nrm(ks[3], (DEPTH, S5_GROUPS, S5_STATE))
    lam_im = (math.pi * jnp.arange(S5_STATE, dtype=f32))[None, None, :] + 0.01 * nrm(ks[4], (DEPTH, S5_GROUPS, S5_STATE))
    log_step = jax.random.uniform(ks[5], (DEPTH, S5_GROUPS), f32, math.log(S5_DT_MIN), math.log(S5_DT_MAX))
    s5_b_re = nrm(ks[6], (DEPTH, S5_GROUPS, S5_STATE, S5_GROUP)) * (2 * S5_GROUP) ** -0.5
    s5_b_im = nrm(ks[7], (DEPTH, S5_GROUPS, S5_STATE, S5_GROUP)) * (2 * S5_GROUP) ** -0.5
    s5_c_re = nrm(ks[8], (DEPTH, S5_GROUPS, S5_GROUP, S5_STATE)) * (2 * S5_STATE) ** -0.5
    s5_c_im = nrm(ks[9], (DEPTH, S5_GROUPS, S5_GROUP, S5_STATE)) * (2 * S5_STATE) ** -0.5
    s5_d = nrm(ks[10], (DEPTH, S5_WIDTH))
    w_glu = nrm(ks[11], (DEPTH, S5_WIDTH, S5_WIDTH)) * S5_WIDTH ** -0.5
    b_glu = 0.01 * nrm(ks[12], (DEPTH, S5_WIDTH))
    w_proj_s5 = nrm(ks[13], (DEPTH, S5_WIDTH, D_MODEL)) * S5_WIDTH ** -0.5
    w_proj_ret = nrm(ks[14], (DEPTH, RET_WIDTH, D_MODEL)) * RET_WIDTH ** -0.5
    w_out = nrm(ks[15], (DEPTH, D_MODEL, D_MODEL)) * D_MODEL ** -0.5
    norm_post = 1.0 + 0.01 * nrm(ks[16], (DEPTH, D_MODEL))
    return {"x": x, "norm_pre": norm_pre, "w_in": w_in, "lam_re": lam_re, "lam_im": lam_im,
            "log_step": log_step, "s5_b_re": s5_b_re, "s5_b_im": s5_b_im, "s5_c_re": s5_c_re,
            "s5_c_im": s5_c_im, "s5_d": s5_d, "w_glu": w_glu, "b_glu": b_glu,
            "w_proj_s5": w_proj_s5, "w_proj_ret": w_proj_ret, "w_out": w_out, "norm_post": norm_post}

def reference(x, norm_pre, w_in, lam_re, lam_im, log_step, s5_b_re, s5_b_im, s5_c_re, s5_c_im,
              s5_d, w_glu, b_glu, w_proj_s5, w_proj_ret, w_out, norm_post):
    for l in range(DEPTH):
        h = rms_norm(x, norm_pre[l])
        proj = h @ w_in[l]
        u_s, z_s, q, k, v, z_r, gl_s, gl_r = jnp.split(proj, SPLIT_IDX, axis=-1)
        y_s = s5_mixer(u_s, lam_re[l], lam_im[l], log_step[l], s5_b_re[l], s5_b_im[l],
                       s5_c_re[l], s5_c_im[l], s5_d[l], w_glu[l], b_glu[l]) * jax.nn.silu(z_s)
        y_r = retention(q, k, v) * jax.nn.silu(z_r)
        m = (jax.nn.sigmoid(gl_s) * (y_s @ w_proj_s5[l])
             + jax.nn.sigmoid(gl_r) * (y_r @ w_proj_ret[l]))
        x = x + rms_norm(m @ w_out[l], norm_post[l])
    return x


_drawn_inputs = setup_inputs


def setup_inputs(seed=0):
    import zlib

    import numpy as np

    out = dict(_drawn_inputs(seed))
    spreads = {}
    factors = {'norm_pre': 10.707,
     'lam_re': 64.0,
     'lam_im': 17.397,
     'log_step': 18.164,
     's5_b_re': 34.561,
     's5_b_im': 33.483,
     's5_c_re': 34.828,
     's5_c_im': 35.524,
     'b_glu': 28.37,
     'norm_post': 46.858}
    for name, (base, spread) in spreads.items():
        noise = np.random.default_rng([zlib.crc32(name.encode()), seed]).standard_normal(out[name].shape)
        drawn = base * np.exp(spread * noise) if base else spread * noise
        out[name] = __import__('jax').numpy.asarray(drawn.astype(out[name].dtype))
    for name, factor in factors.items():
        out[name] = (out[name] * factor).astype(out[name].dtype)
    return out
```

```python
import math
from contextlib import ExitStack

import numpy as np

import concourse.bass as bass
from concourse import mybir

F32 = mybir.dt.float32
F32R = mybir.dt.float32r
I32 = mybir.dt.int32
ALU = mybir.AluOpType
ACT = mybir.ActivationFunctionType
AX_X = mybir.AxisListType.X

P = 128
D_MODEL = 2048
SEQ = 1024
CHUNK = 64
EPS = 1e-6
S5_WIDTH = D_MODEL // 2
GROUP = 16
GROUPS = S5_WIDTH // GROUP
STATE = 64
HEADS = 8
V_HEAD = S5_WIDTH // HEADS
QK_HEAD = V_HEAD // 2
ROPE_BASE = 10000.0

PASSES = 2
TOK = SEQ // PASSES
KT_IN = D_MODEL // P
KT_MID = S5_WIDTH // P
COLS = 512
STEP = 8
STEPS = TOK // STEP
BLOCK = 128
BLOCKS = TOK // BLOCK

SLOTS = 4
Q_U, Q_ZS, Q_GLU, Q_Q, Q_K, Q_V, Q_ZR, Q_S, Q_R, Q_OUT = 0, 8, 16, 20, 24, 28, 36, 44, 68, 92
QUADS = 108
Q_MERGE = 6
MERGES = D_MODEL // COLS
B_U, B_ZS, B_GLU, B_QK, B_V, B_ZR, B_S, B_R, B_OUT = 0, 1, 2, 3, 4, 5, 6, 10, 14
BLOCKS_SET = 16
START = 1
CONSTS = 5


def build_program(nc, x, xT, wstream, gain_in, gain_out, b_glu, lam_re, lam_im, log_step,
                  b_ri, b_ir, c_ri, c_ir, d_rep, signs, eye, ones, dmat, zeta, xi,
                  gdec, rope, mats, out):
    with ExitStack() as ctx:
        def sb(name, shape, dt=F32):
            return ctx.enter_context(nc.sbuf_tensor(name, shape, dt))

        def sem(name):
            return ctx.enter_context(nc.semaphore(name))

        raw = sb("raw", [P, SLOTS, COLS])
        w_hi = sb("w_hi", [P, SLOTS, COLS], F32R)
        w_lo = sb("w_lo", [P, SLOTS, COLS], F32R)
        h_hi = sb("h_hi", [P, KT_IN, TOK], F32R)
        h_lo = sb("h_lo", [P, KT_IN, TOK], F32R)
        y_hi = sb("y_hi", [P, KT_MID, TOK], F32R)
        y_lo = sb("y_lo", [P, KT_MID, TOK], F32R)
        R2, R3, R4 = 8192, 8192 + 4160, 8192 + 4160 + 4096
        work = sb("work", [P, R4 + 2048])
        tmp = sb("tmp", [P, 2, TOK])
        ident = sb("ident", [P, P])
        ones_sb = sb("ones_sb", [P, P])
        gain_sb = sb("gain_sb", [P, KT_IN])
        bglu_sb = sb("bglu_sb", [P, KT_MID])
        gdec_sb = sb("gdec_sb", [P, 4])
        eps_sb = sb("eps_sb", [P, 1])
        scan_re = sb("scan_re", [P, 2, 32])
        scan_im = sb("scan_im", [P, 2, 32])
        carry = sb("carry", [P, 2, 32])
        scan_t = sb("scan_t", [P, 2, 2, 32])
        ret_state = sb("ret_state", [P, 4, V_HEAD])
        ssq = sb("ssq", [P, 4, 4])
        rstd_out = sb("rstd_out", [P, 4])
        psum = ctx.enter_context(nc.psum_tensor("psum", [P, 8, COLS], F32))

        def area(a, n):
            return work[:, a:a + n]

        u_tok = area(0, 4096).rearrange("p (g q h) -> p g q h", g=GROUPS, q=4)
        mat_ring = area(0, 4096).rearrange("p (s m n) -> p s m n", s=2, m=2)
        q_t = area(0, 2048).rearrange("p (a n) -> p a n", a=4)
        k_t = area(2048, 2048).rearrange("p (a n) -> p a n", a=4)
        m_t = area(0, 8192).rearrange("p (k n) -> p k n", k=KT_IN)
        o_row = area(0, 8192).rearrange("p (i n) -> p i n", i=4)
        u_step = area(4096, 4096).rearrange("p (g c) -> p g c", g=GROUPS)
        v_row = area(4096, 4096).rearrange("p (i n) -> p i n", i=4)
        sq_sum = area(R2 + 2048, TOK)
        rstd_in = area(R2 + 2560, TOK)
        state = area(R2, 4160).rearrange("p (c r k) -> p c r k", c=STEPS + 1, r=2)
        rope_sb = area(R2, 1024).rearrange("p (s n) -> p s n", s=2)
        z_r = area(R2, 4096).rearrange("p (k n) -> p k n", k=KT_MID)
        gain_row = area(R2, 2048)
        m2_ring = area(R3, 4096).rearrange("p (s n) -> p s n", s=4)
        z_s = area(R3, 4096).rearrange("p (k n) -> p k n", k=KT_MID)
        o_t = area(R3, 1024).rearrange("p (h a n) -> p h a n", h=2, a=4)
        o_sq = area(R3 + 1024, 1024).rearrange("p (h a n) -> p h a n", h=2, a=4)
        dmat_sb = area(R3 + 2048, 1024).rearrange("p (h n) -> p h n", h=2)
        zeta_sb = area(R3 + 3072, 512)
        xi_sb = area(R3 + 3584, 512)
        x_ring = area(R3, 4096).rearrange("p (s n) -> p s n", s=2)
        xt_ring = area(R4, 2048).rearrange("p (s n) -> p s n", s=4)
        sc_ring = area(R4, 1024).rearrange("p (s g c) -> p s g c", s=2, g=8)
        y_row = work[0:STEPS, R4 + 1024:R4 + 2048].rearrange("p (t n) -> p t n", t=STEP)
        gate = area(R4, 2048).rearrange("p (s n) -> p s n", s=4)
        s_dec = area(R4, 1024).rearrange("p (h n) -> p h n", h=2)
        q_xi = area(R4 + 1024, 512).rearrange("p (a n) -> p a n", a=4)
        k_zeta = area(R4 + 1536, 512)

        raw_loaded = [sem(f"raw_loaded{s}") for s in range(SLOTS)]
        head_split = sem("head_split")
        rest_split = sem("rest_split")
        unit_multiplied = sem("unit_multiplied")
        set_a_emptied = sem("set_a_emptied")
        set_b_emptied = sem("set_b_emptied")
        consts_loaded = sem("consts_loaded")
        params_loaded = sem("params_loaded")
        setup_step = sem("setup_step")
        powers_ready = sem("powers_ready")
        pool_setup = sem("pool_setup")
        window_ready = sem("window_ready")
        m1_full = sem("m1_full")
        m2_full = sem("m2_full")
        m1_copied = sem("m1_copied")
        m2_copied = sem("m2_copied")
        m3_written = sem("m3_written")
        m1_stored, m2_stored, m3_stored = sem("m1_stored"), sem("m2_stored"), sem("m3_stored")
        xt_loaded = [sem(f"xt_loaded{s}") for s in range(4)]
        squared = sem("squared")
        sum_added = sem("sum_added")
        sum_full = sem("sum_full")
        std_ready = sem("std_ready")
        rstd_ready = sem("rstd_ready")
        h_scaled = sem("h_scaled")
        h_head = sem("h_head")
        h_ready = sem("h_ready")
        step_rows_full = sem("step_rows_full")
        step_rows_act, step_rows_dve = sem("step_rows_act"), sem("step_rows_dve")
        m2_loaded = [sem(f"m2_loaded{s}") for s in range(4)]
        step_in_full = sem("step_in_full")
        state_in_act, state_in_dve = sem("state_in_act"), sem("state_in_dve")
        scan_done = sem("scan_done")
        mat_loaded = [sem(f"mat_loaded{s}") for s in range(2)]
        shifted_act, shifted_dve = sem("shifted_act"), sem("shifted_dve")
        y_full = sem("y_full")
        y_row_act, y_row_dve = sem("y_row_act"), sem("y_row_dve")
        y_turned = sem("y_turned")
        gelu_done = sem("gelu_done")
        g_head = sem("g_head")
        g_ready = sem("g_ready")
        glu_step = sem("glu_step")
        ys_head, ys_ready = sem("ys_head"), sem("ys_ready")
        rope_loaded = sem("rope_loaded")
        rope_step = sem("rope_step")
        rope_done = sem("rope_done")
        tables_loaded = sem("tables_loaded")
        k_turned = sem("k_turned")
        k_zeta_ready = sem("k_zeta_ready")
        scores_full = sem("scores_full")
        scores_decayed = sem("scores_decayed")
        q_xi_ready = sem("q_xi_ready")
        o_full = sem("o_full")
        kv_full = sem("kv_full")
        state_ready = sem("state_ready")
        o_copied = sem("o_copied")
        o_squared = sem("o_squared")
        osum_full = sem("osum_full")
        ostd_ready = sem("ostd_ready")
        o_step = sem("o_step")
        yr_head, yr_ready = sem("yr_head"), sem("yr_ready")
        m_added = sem("m_added")
        m_head, m_ready = sem("m_head"), sem("m_ready")
        out_squared = sem("out_squared")
        out_stat = sem("out_stat")
        out_std = sem("out_std")
        out_scaled = sem("out_scaled")
        out_ready = sem("out_ready")
        x_loaded = [sem(f"x_loaded{s}") for s in range(2)]
        gain_row_loaded = sem("gain_row_loaded")
        out_stored = sem("out_stored")
        rows_free = sem("rows_free")

        pool_waited, pe_waited = sem("pool_waited"), sem("pe_waited")

        block = ctx.enter_context(nc.Block())

        @block.sync
        def _(sp):
            sp.sem_inc(rest_split, SLOTS)
            for counted in (m_added, out_ready, rows_free, scan_done, state_ready, set_a_emptied, set_b_emptied):
                sp.sem_inc(counted, START)
            with sp.Fori(0, PASSES) as half:
                with sp.Fori(0, QUADS) as q:
                    for s in range(SLOTS):
                        sp.wait_ge(rest_split, (half * QUADS + q) * SLOTS + s + 1)
                        sp.dma_start(raw[:, s, :], wstream[q * SLOTS + s]).then_inc(raw_loaded[s], 16)

        window = area(0, 7680).rearrange("p (g i h) -> p g i h", g=32, i=15)
        bb_p = area(R2, 1024).rearrange("p (g h) -> p g h", g=GROUPS)
        bb_q = area(R2 + 1024, 1024).rearrange("p (g h) -> p g h", g=GROUPS)
        cc_p = area(R2 + 2048, 1024).rearrange("p (g h) -> p g h", g=GROUPS)
        cc_q = area(R2 + 3072, 1024).rearrange("p (g h) -> p g h", g=GROUPS)
        m1_stage = area(R3, 1024).rearrange("p (g n) -> p g n", g=8)
        m2_stage = area(R3 + 1024, 1024).rearrange("p (g n) -> p g n", g=8)
        m3_stage = area(R3 + 2048, 1024).rearrange("p (g t h) -> p g t h", g=8, t=STEP)
        m3_tmp = area(R3 + 3072, 1024).rearrange("p (g t h) -> p g t h", g=8, t=STEP)
        pow_re = area(R4, 576).rearrange("p (j g) -> p j g", j=9)
        pow_im = area(R4 + 576, 576).rearrange("p (j g) -> p j g", j=9)
        d_sb = area(R4 + 1152, 64)
        sign_sb = area(R4 + 1216, 2)
        lam_r, lam_i, step_sb, par_re, par_im, s0, s1, s2, s3, s4 = [
            area(R4 + 1408 + 64 * n, 64) for n in range(10)]
        s5, s6, s7, s8, s9 = [tmp[:, 0, 64 * n:64 * n + 64] for n in range(5)]
        b_tmp = tmp[:, :, :].rearrange("p a n -> p (a n)").rearrange("p (g h) -> p g h", g=GROUPS)
        b_tmp2 = area(R3, 1024).rearrange("p (g h) -> p g h", g=GROUPS)
        win_tmp = tmp[:, :, :].rearrange("p a n -> p (a n)").rearrange("p (g i h) -> p g i h", g=32, i=2)

        def copy(eng, dst, src):
            if eng is nc.scalar:
                return eng.activation(dst, src, ACT.Copy)
            return eng.tensor_copy(dst, src)

        def step_rows(seq, eng, half, odd):
            done = step_rows_dve if odd else step_rows_act
            for r in range(odd, 16, 2):
                seq.wait_ge(step_rows_full, half * 16 + r + 1)
                for s in range(2):
                    src = psum[0:64, r % 8, :].rearrange("p (a c s) -> p a c s", a=4, s=2)[:, :, :, s]
                    copy(eng, u_step[64 * s:64 * s + 64, 4 * r:4 * r + 4, :], src).then_inc(done, 1)

        def state_inputs(seq, eng, half, odd):
            done = state_in_dve if odd else state_in_act
            for j in range(odd, 8, 2):
                seq.wait_ge(step_in_full, half * 8 + j + 1)
                for par in range(2):
                    for r in range(2):
                        src = psum[64 * r:64 * r + 64, j, :].rearrange("p (k g c) -> p k g c", k=4, g=2)[:, :, par, :]
                        dst = state[64 * par:64 * par + 64, 1:STEPS + 1, r, 4 * j:4 * j + 4].rearrange("p c k -> p k c")
                        copy(eng, dst, src).then_inc(done, 1)

        def shift_states(seq, eng, half, j, r):
            done = shifted_act if eng is nc.scalar else shifted_dve
            if j >= 2:
                seq.wait_ge(y_full, half * 8 + j - 1)
            for par in range(2):
                src = state[64 * par:64 * par + 64, 0:STEPS, r, 4 * j:4 * j + 4].rearrange("p c k -> p k c")
                copy(eng, sc_ring[64 * r:64 * r + 64, j % 2, par::2, :], src).then_inc(done, 1)

        def y_rows(eng, j, n):
            src = psum[0:STEPS, 2 * (j % 2) + n, :].rearrange("p (q t g) -> p q t g", q=4, t=STEP)
            return copy(eng, y_row[:, :, 64 * n:64 * n + 64].rearrange("p t (q g) -> p q t g", q=4), src)

        @block.gpsimd
        def _(pool):
            for dst, src in ((lam_r, lam_re), (lam_i, lam_im), (step_sb, log_step),
                             (sign_sb, signs), (bb_p, b_ri), (bb_q, b_ir), (cc_p, c_ri),
                             (cc_q, c_ir), (d_sb, d_rep)):
                pool.dma_start(dst.rearrange("p g h -> p (g h)") if dst.ndim == 3 else dst, src
                               ).then_inc(params_loaded, 16)
            for dst, src in ((ident[:, :], eye), (ones_sb[:, :], ones), (gain_sb[:, :], gain_in),
                             (bglu_sb[:, :], b_glu), (gdec_sb[:, :], gdec)):
                pool.dma_start(dst, src).then_inc(consts_loaded, 16)
            pool.wait_ge(powers_ready, 1)
            for j in range(8):
                gs = slice(8 * j, 8 * j + 8)

                def powers(a):
                    return a[:, 1:9, gs].rearrange("p t g -> p g t").unsqueeze(3).broadcast_to([P, 8, STEP, GROUP])

                def coefs(a):
                    return a[:, gs, :].unsqueeze(2).broadcast_to([P, 8, STEP, GROUP])

                if j:
                    pool.wait_ge(m3_stored, 16 * j)
                pool.tensor_tensor(m3_stage, coefs(cc_p), powers(pow_re), ALU.mult).then_inc(pool_setup, 1)
                pool.tensor_tensor(m3_tmp, coefs(cc_q), powers(pow_im), ALU.mult).then_inc(pool_setup, 1)
                pool.wait_ge(pool_setup, 3 * j + 2)
                pool.tensor_tensor(m3_stage, m3_stage, m3_tmp, ALU.subtract).then_inc(pool_setup, 1)
                pool.wait_ge(pool_setup, 3 * j + 3)
                pool.dma_start(mats[2, j], m3_stage.rearrange("p g t h -> p (g t h)")).then_inc(m3_stored, 16)

            with pool.Fori(0, PASSES) as half:
                pool.wait_ge(m1_stored, 8 * 16)
                pool.wait_ge(m3_stored, 8 * 16)
                pool.wait_ge(m2_stored, 8 * 16)
                pool.wait_ge(m_added, half * 16 + START)
                pool.sem_inc(pool_waited, 1)
                for n in range(2 * KT_IN):
                    k = n % KT_IN
                    if 4 <= n < KT_IN + 4:
                        pool.wait_ge(squared, half * KT_IN + n - 3)
                        pool.sem_inc(pool_waited, 1)
                    elif n >= KT_IN + 4:
                        pool.wait_ge(h_scaled, half * KT_IN + k - 3)
                        pool.sem_inc(pool_waited, 1)
                    pool.dma_start(xt_ring[:, n % 4, :], xT[half * KT_IN + k]).then_inc(xt_loaded[n % 4], 16)
                pool.wait_ge(out_ready, half * 4 + START)
                pool.sem_inc(pool_waited, 1)
                for j in range(8):
                    if j >= 4:
                        pool.wait_ge(step_in_full, half * 8 + j - 3)
                        pool.sem_inc(pool_waited, 1)
                    pool.dma_start(m2_ring[:, j % 4, :], mats[1, j]).then_inc(m2_loaded[j % 4], 16)

                def load_mats(j):
                    pool.dma_start(mat_ring[:, j % 2, 0, :], mats[0, j]).then_inc(mat_loaded[j % 2], 16)
                    pool.dma_start(mat_ring[:, j % 2, 1, :], mats[2, j]).then_inc(mat_loaded[j % 2], 16)

                pool.wait_ge(step_rows_full, (half + 1) * 16)
                pool.sem_inc(pool_waited, 1)
                load_mats(0)
                load_mats(1)
                pool.wait_ge(state_in_act, (half + 1) * 16)
                pool.wait_ge(state_in_dve, (half + 1) * 16)
                pool.sem_inc(pool_waited, 1)
                per = 5 * STEPS + 2
                pool.wait_ge(scan_done, half * per + START)
                pool.sem_inc(pool_waited, 1)
                pool.tensor_copy(state[:, 0], carry[:, :, :]).then_inc(scan_done, 1)
                with pool.Fori(0, STEPS) as c:
                    now = half * per + c * 5 + 1
                    pool.wait_ge(scan_done, now + START)
                    pool.sem_inc(pool_waited, 1)
                    pool.tensor_tensor(scan_t[:, 0], state[:, c], scan_re[:, :, :], ALU.mult).then_inc(scan_done, 1)
                    for r in range(2):
                        pool.tensor_tensor(scan_t[:, 1, r, :], state[:, c, 1 - r, :], scan_im[:, r, :],
                                           ALU.mult).then_inc(scan_done, 1)
                    pool.wait_ge(scan_done, now + 3 + START)
                    pool.sem_inc(pool_waited, 1)
                    pool.tensor_tensor(scan_t[:, 0], scan_t[:, 0], scan_t[:, 1], ALU.add).then_inc(scan_done, 1)
                    pool.wait_ge(scan_done, now + 4 + START)
                    pool.sem_inc(pool_waited, 1)
                    pool.tensor_tensor(state[:, c + 1], state[:, c + 1], scan_t[:, 0], ALU.add).then_inc(scan_done, 1)
                pool.wait_ge(scan_done, half * per + 5 * STEPS + 1 + START)
                pool.sem_inc(pool_waited, 1)
                pool.tensor_copy(carry[:, :, :], state[:, STEPS]).then_inc(scan_done, 1)
                for j in range(2, 8):
                    pool.wait_ge(y_full, half * 8 + j - 1)
                    pool.sem_inc(pool_waited, 1)
                    load_mats(j)
                pool.wait_ge(g_ready, (half + 1) * 8)
                pool.sem_inc(pool_waited, 1)
                pool.dma_start(rope_sb, rope[half]).then_inc(rope_loaded, 16)
                pool.wait_ge(ys_ready, (half + 1) * 2)
                pool.sem_inc(pool_waited, 1)
                pool.dma_start(area(R3 + 2048, 1024), dmat).then_inc(tables_loaded, 16)
                pool.dma_start(zeta_sb, zeta).then_inc(tables_loaded, 16)
                pool.dma_start(xi_sb, xi).then_inc(tables_loaded, 16)
                pool.wait_ge(o_step, (half + 1) * BLOCKS * 6)
                pool.sem_inc(pool_waited, 1)
                for i in range(2):
                    pool.dma_start(x_ring[:, i, :], x[half * 4 + i]).then_inc(x_loaded[i], 16)
                pool.wait_ge(yr_ready, (half + 1) * 2)
                pool.sem_inc(pool_waited, 1)
                pool.dma_start(gain_row, gain_out).then_inc(gain_row_loaded, 16)
                for i in range(4):
                    pool.wait_ge(out_ready, half * 4 + i + 1 + START)
                    pool.sem_inc(pool_waited, 1)
                    pool.dma_start(out[half * 4 + i], o_row[:, i, :]).then_inc(out_stored, 16)
                    if i < 2:
                        pool.dma_start(x_ring[:, i, :], x[half * 4 + i + 2]).then_inc(x_loaded[i], 16)
                pool.wait_ge(out_stored, (half + 1) * 4 * 16)
                pool.sem_inc(rows_free, 1)
            pool.wait_ge(out_stored, PASSES * 4 * 16)

        @block.scalar
        def _(act):
            for j in range(8):
                act.wait_ge(m2_full, j + 1)
                if j:
                    act.wait_ge(m2_stored, 16 * j)
                for n in range(2):
                    nc.scalar.activation(m2_stage[:, 4 * n:4 * n + 4, :].rearrange("p g n -> p (g n)"),
                                         psum[:, 4 + n, :], ACT.Copy).then_inc(m2_copied, 1)
                act.wait_ge(m2_copied, 2 * j + 2)
                act.dma_start(mats[1, j], area(R3 + 1024, 1024)).then_inc(m2_stored, 16)
                act.wait_ge(m1_copied, 8 * j + 8)
                act.dma_start(mats[0, j], area(R3, 1024)).then_inc(m1_stored, 16)
            act.wait_ge(consts_loaded, CONSTS * 16)

            with act.Fori(0, PASSES) as half:
                def heads(q):
                    for s in range(SLOTS):
                        head(q, s)

                def head(q, s):
                    act.wait_ge(raw_loaded[s], (half * QUADS + q + 1) * 16)
                    act.wait_ge(unit_multiplied, (half * QUADS + q) * SLOTS + s + 1)
                    nc.scalar.activation(w_hi[:, s, :], raw[:, s, :], ACT.Copy).then_inc(head_split, 1)

                def multiplied(q):
                    act.wait_ge(unit_multiplied, (half * QUADS + q) * SLOTS + SLOTS)

                act.wait_ge(m1_stored, 8 * 16)
                for k in range(KT_IN):
                    act.wait_ge(xt_loaded[k % 4], (half * 8 + k // 4 + 1) * 16)
                    if k >= 2:
                        act.wait_ge(sum_added, half * KT_IN + k - 1)
                    nc.scalar.activation(tmp[:, k % 2, :], xt_ring[:, k % 4, :], ACT.Square).then_inc(squared, 1)
                act.wait_ge(sum_full, half + 1)
                nc.scalar.activation(rstd_in, psum[:, 0, :], ACT.Sqrt, scale=1.0 / D_MODEL,
                                     bias=eps_sb[:, 0:1]).then_inc(std_ready, 1)
                for k in range(KT_IN):
                    act.wait_ge(h_scaled, half * KT_IN + k + 1)
                    if k == 0:
                        multiplied(0)
                    nc.scalar.activation(h_hi[:, k, :], tmp[:, k % 2, :], ACT.Copy).then_inc(h_head, 1)
                    head(Q_U + k // 4, k % 4)
                heads(Q_U + 4)
                multiplied(Q_U + 4)
                act.wait_ge(rows_free, half + START)
                for n in range(4):
                    nc.scalar.activation(u_tok[:, 0:32, n, :], psum[:, n, :].rearrange("p (g h) -> p g h", h=GROUP),
                                         ACT.Copy).then_inc(set_a_emptied, 1)
                for q in range(5, 8):
                    heads(Q_U + q)
                heads(Q_ZS)
                multiplied(Q_ZS)
                for n in range(4):
                    nc.scalar.activation(u_tok[:, 32:64, n, :], psum[:, 4 + n, :].rearrange("p (g h) -> p g h", h=GROUP),
                                         ACT.Copy).then_inc(set_b_emptied, 1)
                step_rows(act, nc.scalar, half, 0)
                state_inputs(act, nc.scalar, half, 0)
                for q in range(1, 4):
                    heads(Q_ZS + q)
                heads(Q_ZS + 4)
                multiplied(Q_ZS + 4)
                for n in range(4):
                    nc.scalar.activation(z_s[:, n, :], psum[:, n, :], ACT.Silu).then_inc(set_a_emptied, 1)
                for q in range(5, 8):
                    heads(Q_ZS + q)
                heads(Q_GLU)
                multiplied(Q_GLU)
                for n in range(4):
                    nc.scalar.activation(z_s[:, 4 + n, :], psum[:, 4 + n, :], ACT.Silu).then_inc(set_b_emptied, 1)
                act.wait_ge(scan_done, (half + 1) * (5 * STEPS + 2) + START)
                shift_states(act, nc.scalar, half, 0, 1)
                for j in range(8):
                    if j + 1 < 8 and j == 0:
                        shift_states(act, nc.scalar, half, 1, 1)
                    if j:
                        act.wait_ge(y_turned, half * 8 + j)
                    act.wait_ge(y_full, half * 8 + j + 1)
                    y_rows(nc.scalar, j, 0).then_inc(y_row_act, 1)
                    if j + 2 < 8:
                        shift_states(act, nc.scalar, half, j + 2, 1)
                    act.wait_ge(y_turned, half * 8 + j + 1)
                    if j >= 2:
                        act.wait_ge(g_ready, half * 8 + j - 1)
                    nc.scalar.activation(tmp[:, j % 2, :].rearrange("p (c t) -> p t c", t=STEP),
                                         psum[:, 4 + j % 2, :].rearrange("p (t c) -> p t c", t=STEP),
                                         ACT.Gelu_apprx_tanh).then_inc(gelu_done, 1)
                    act.wait_ge(gelu_done, half * 8 + j + 1)
                    nc.scalar.activation(y_hi[:, j, :], tmp[:, j % 2, :], ACT.Copy).then_inc(g_head, 1)
                heads(Q_GLU + 1)
                heads(Q_GLU + 2)
                multiplied(Q_GLU + 2)
                for n in range(4):
                    nc.scalar.activation(gate[:, n, :], psum[:, n, :], ACT.Sigmoid,
                                         bias=bglu_sb[:, n:n + 1]).then_inc(set_a_emptied, 1)
                heads(Q_GLU + 3)
                heads(Q_Q)
                multiplied(Q_Q)
                act.wait_ge(glu_step, half * 24 + 12)
                for n in range(4):
                    nc.scalar.activation(gate[:, n, :], psum[:, 4 + n, :], ACT.Sigmoid,
                                         bias=bglu_sb[:, 4 + n:5 + n]).then_inc(set_b_emptied, 1)
                act.wait_ge(glu_step, (half + 1) * 24)
                for n in range(2):
                    nc.scalar.activation(y_hi[:, 4 * n:4 * n + 4, :], z_s[:, 4 * n:4 * n + 4, :],
                                         ACT.Copy).then_inc(ys_head, 1)
                for q in range(1, 4):
                    heads(Q_Q + q)
                for q in range(4):
                    heads(Q_K + q)
                for q in range(8):
                    heads(Q_V + q)
                for q in range(4):
                    heads(Q_ZR + q)
                heads(Q_ZR + 4)
                multiplied(Q_ZR + 4)
                act.wait_ge(rope_done, (half + 1) * 32)
                for n in range(4):
                    nc.scalar.activation(z_r[:, n, :], psum[:, n, :], ACT.Silu).then_inc(set_a_emptied, 1)
                for q in range(5, 8):
                    heads(Q_ZR + q)
                heads(Q_S)
                multiplied(Q_S)
                for n in range(4):
                    nc.scalar.activation(z_r[:, 4 + n, :], psum[:, 4 + n, :], ACT.Silu).then_inc(set_b_emptied, 1)
                for t in range(BLOCKS):
                    for par in range(2):
                        act.wait_ge(o_full, half * 2 * BLOCKS + 2 * t + par + 1)
                        if t and par == 0:
                            act.wait_ge(o_step, (half * BLOCKS + t) * 6)
                        nc.scalar.activation(o_t[:, par], psum[:, 3 + par, :].rearrange("p (a n) -> p a n", a=4),
                                             ACT.Copy).then_inc(o_copied, 1)
                        act.wait_ge(o_copied, half * 2 * BLOCKS + 2 * t + par + 1)
                        nc.scalar.activation(o_sq[:, par], o_t[:, par], ACT.Square).then_inc(o_squared, 1)
                    for par in range(2):
                        act.wait_ge(osum_full, half * 2 * BLOCKS + 2 * t + par + 1)
                        nc.scalar.activation(o_sq[:, par], psum[:, 6 + par, :].rearrange("p (a n) -> p a n", a=4),
                                             ACT.Sqrt, scale=1.0 / V_HEAD, bias=eps_sb[:, 0:1]).then_inc(ostd_ready, 1)
                act.wait_ge(o_step, (half + 1) * BLOCKS * 6)
                with act.Fori(0, MERGES) as b:
                    q0 = Q_S + b * Q_MERGE
                    for q in range(1, 5):
                        heads(q0 + q)
                    multiplied(q0 + 4)
                    act.wait_ge(set_b_emptied, (half * BLOCKS_SET + B_S + b) * 4 + START)
                    for n in range(4):
                        nc.scalar.activation(gate[:, n, :], psum[:, n, :], ACT.Sigmoid).then_inc(set_a_emptied, 1)
                    heads(q0 + 5)
                    heads(q0 + 6)
                multiplied(Q_R)
                for n in range(2):
                    nc.scalar.activation(y_hi[:, 4 * n:4 * n + 4, :], z_r[:, 4 * n:4 * n + 4, :],
                                         ACT.Copy).then_inc(yr_head, 1)
                with act.Fori(0, MERGES) as b:
                    q0 = Q_R + b * Q_MERGE
                    for q in range(1, 5):
                        heads(q0 + q)
                    multiplied(q0 + 4)
                    act.wait_ge(m_added, half * 16 + b * 4 + START)
                    for n in range(4):
                        nc.scalar.activation(gate[:, n, :], psum[:, n, :], ACT.Sigmoid).then_inc(set_a_emptied, 1)
                    heads(q0 + 5)
                    heads(q0 + 6)
                multiplied(Q_OUT - 2)
                for n in range(4):
                    act.wait_ge(m_added, half * 16 + 4 * n + 4 + START)
                    nc.scalar.activation(h_hi[:, 4 * n:4 * n + 4, :], m_t[:, 4 * n:4 * n + 4, :],
                                         ACT.Copy).then_inc(m_head, 1)
                for c in range(4):
                    for q in range(1, 5 if c < 3 else 4):
                        heads(Q_OUT + 4 * c + q)
                    emptied, first = (set_a_emptied, 0) if c % 2 == 0 else (set_b_emptied, 4)
                    for i in range(4):
                        act.wait_ge(emptied, (half * BLOCKS_SET + B_OUT + c // 2) * 4 + i + 1 + START)
                        if c or i:
                            act.wait_ge(out_squared, half * 16 + 4 * c + i)
                        nc.scalar.activation(tmp[:, 0, :], o_row[:, i, COLS * c:COLS * c + COLS], ACT.Square,
                                             accum_out=ssq[:, i, c:c + 1]).then_inc(out_squared, 1)
                act.wait_ge(out_stat, half * 2 + 1)
                nc.scalar.activation(rstd_out[:, :], rstd_out[:, :], ACT.Sqrt, scale=1.0 / D_MODEL,
                                     bias=eps_sb[:, 0:1]).then_inc(out_std, 1)

        @block.vector
        def _(dve):
            V = nc.vector
            steps = [0]

            def then(ins):
                steps[0] += 1
                ins.then_inc(setup_step, 1)
                dve.wait_ge(setup_step, steps[0])

            def ts(dst, src, a, op, b=None, op2=ALU.bypass):
                if b is None:
                    then(V.tensor_scalar(dst, src, a, None, op))
                else:
                    then(V.tensor_scalar(dst, src, a, b, op, op2))

            def tt(dst, a, b, op):
                then(V.tensor_tensor(dst, a, b, op))

            MAGIC = 12582912.0

            def rint(dst, src):
                ts(dst, src, MAGIC, ALU.add)
                ts(dst, dst, -MAGIC, ALU.add)

            def poly(dst, z, coefs):
                ts(dst, z, coefs[0], ALU.mult, coefs[1], ALU.add)
                for c in coefs[2:]:
                    tt(dst, dst, z, ALU.mult)
                    ts(dst, dst, c, ALU.add)

            def exp(dst, arg, n, r, bits):
                ts(r, arg, 89.0, ALU.min, -110.0, ALU.max)
                ts(n, r, 1.0 / math.log(2.0), ALU.mult)
                rint(n, n)
                then(V.scalar_tensor_tensor(r, n, -0.693359375, r, ALU.mult, ALU.add))
                then(V.scalar_tensor_tensor(r, n, 2.12194440e-4, r, ALU.mult, ALU.add))
                poly(dst, r, [1 / 5040, 1 / 720, 1 / 120, 1 / 24, 1 / 6, 0.5, 1.0, 1.0])
                ts(n, n, 127.0, ALU.add, 0.0, ALU.max)
                ts(n, n, 255.0, ALU.min, 8388608.0, ALU.mult)
                then(V.tensor_copy(bits.bitcast(I32), n))
                tt(dst, dst, bits, ALU.mult)

            then(V.memset(window[:, :, 8:15, :], 0.0))
            then(V.memset(eps_sb[:, :], EPS))
            then(V.memset(carry[:, :, :], 0.0))
            then(V.memset(ret_state[:, :, :], 0.0))
            dve.wait_ge(params_loaded, 9 * 16)
            dve.wait_ge(consts_loaded, CONSTS * 16)
            exp(s0, step_sb, s1, s2, s3)
            tt(s4, lam_r, s0, ALU.mult)
            exp(par_re, s4, s1, s2, s3)
            tt(s4, lam_i, s0, ALU.mult)
            ts(s1, s4, 2.0 / math.pi, ALU.mult)
            rint(s1, s1)
            half_pi = [1.5703125, 4.8351287841796875e-4, -3.1385570764541626e-7, 6.077100506506192e-11]
            then(V.scalar_tensor_tensor(s2, s1, -half_pi[0], s4, ALU.mult, ALU.add))
            for c in half_pi[1:]:
                then(V.scalar_tensor_tensor(s2, s1, -c, s2, ALU.mult, ALU.add))
            ts(s3, s1, 0.25, ALU.mult, -0.375, ALU.add)
            rint(s3, s3)
            then(V.scalar_tensor_tensor(s1, s3, -4.0, s1, ALU.mult, ALU.add))
            tt(s5, s2, s2, ALU.mult)
            poly(s6, s5, [2.7557319e-6, -1.98412698e-4, 8.33333333e-3, -1.66666667e-1, 1.0])
            tt(s6, s6, s2, ALU.mult)
            poly(s7, s5, [2.48015873e-5, -1.38888889e-3, 4.16666667e-2, -0.5, 1.0])
            ts(s3, s1, 1.0, ALU.is_equal)
            ts(s4, s1, 3.0, ALU.is_equal)
            tt(s3, s3, s4, ALU.add)
            ts(s4, s3, -1.0, ALU.mult, 1.0, ALU.add)
            tt(s8, s6, s4, ALU.mult)
            tt(s9, s7, s3, ALU.mult)
            tt(s8, s8, s9, ALU.add)
            tt(s7, s7, s4, ALU.mult)
            tt(s6, s6, s3, ALU.mult)
            tt(s7, s7, s6, ALU.add)
            ts(s3, s1, 2.0, ALU.is_ge, -2.0, ALU.mult)
            ts(s3, s3, 1.0, ALU.add)
            tt(s8, s8, s3, ALU.mult)
            ts(s3, s1, 1.0, ALU.is_equal)
            ts(s4, s1, 2.0, ALU.is_equal)
            tt(s3, s3, s4, ALU.add)
            ts(s3, s3, -2.0, ALU.mult, 1.0, ALU.add)
            tt(s7, s7, s3, ALU.mult)
            then(V.memset(pow_re[:, 0, :], 1.0))
            then(V.memset(pow_im[:, 0, :], 0.0))
            tt(pow_im[:, 1, :], par_re, s8, ALU.mult)
            tt(pow_re[:, 1, :], par_re, s7, ALU.mult)
            for j in range(2, 9):
                a, b = j // 2, j - j // 2
                tt(s1, pow_re[:, a, :], pow_re[:, b, :], ALU.mult)
                tt(s2, pow_im[:, a, :], pow_im[:, b, :], ALU.mult)
                tt(pow_re[:, j, :], s1, s2, ALU.subtract)
                tt(s1, pow_re[:, a, :], pow_im[:, b, :], ALU.mult)
                tt(s2, pow_im[:, a, :], pow_re[:, b, :], ALU.mult)
                tt(pow_im[:, j, :], s1, s2, ALU.add)
            V.tensor_scalar(cc_p, cc_p, sign_sb[:, 0:1], None, ALU.mult).then_inc(powers_ready, 1)
            tt(s1, lam_r, lam_r, ALU.mult)
            tt(s2, lam_i, lam_i, ALU.mult)
            tt(s1, s1, s2, ALU.add)
            then(V.reciprocal(s1, s1))
            ts(s0, pow_re[:, 1, :], -1.0, ALU.add)
            tt(s2, s0, lam_r, ALU.mult)
            tt(s3, pow_im[:, 1, :], lam_i, ALU.mult)
            tt(s2, s2, s3, ALU.add)
            tt(par_re, s2, s1, ALU.mult)
            tt(s2, pow_im[:, 1, :], lam_r, ALU.mult)
            tt(s3, s0, lam_i, ALU.mult)
            tt(s2, s2, s3, ALU.subtract)
            tt(par_im, s2, s1, ALU.mult)

            def by_group(a):
                return a.unsqueeze(2).broadcast_to([P, GROUPS, GROUP])

            then(V.tensor_scalar(bb_q, bb_q, sign_sb[:, 1:2], None, ALU.mult))
            tt(b_tmp, bb_p, by_group(par_im), ALU.mult)
            tt(bb_p, bb_p, by_group(par_re), ALU.mult)
            tt(b_tmp2, bb_q, by_group(par_im), ALU.mult)
            tt(bb_p, bb_p, b_tmp2, ALU.add)
            tt(bb_q, bb_q, by_group(par_re), ALU.mult)
            tt(bb_q, bb_q, b_tmp, ALU.subtract)
            for par in range(2):
                half_rows = slice(64 * par, 64 * par + 64)
                for r in range(2):
                    then(V.tensor_copy(scan_re[half_rows, r, :], pow_re[half_rows, 8, par::2]))
                    ts(scan_im[half_rows, r, :], pow_im[half_rows, 8, par::2], 1.0 if r else -1.0, ALU.mult)
            for gh in range(2):
                gs = slice(32 * gh, 32 * gh + 32)
                if gh:
                    dve.wait_ge(m1_full, 8)
                    dve.wait_ge(m2_full, 4)
                    dve.wait_ge(window_ready, 1)
                for i0 in range(0, 8, 2):
                    def powers(a):
                        two = a[:, 6 - i0:8 - i0, gs][:, ::-1, :]
                        return two.rearrange("p i g -> p g i").unsqueeze(3).broadcast_to([P, 32, 2, GROUP])

                    def coefs(a):
                        return a[:, gs, :].unsqueeze(2).broadcast_to([P, 32, 2, GROUP])

                    part = window[:, :, i0:i0 + 2, :]
                    tt(part, coefs(bb_p), powers(pow_re), ALU.mult)
                    tt(win_tmp, coefs(bb_q), powers(pow_im), ALU.mult)
                    last = V.tensor_tensor(part, part, win_tmp, ALU.add)
                    if i0 < 6:
                        then(last)
                last.then_inc(window_ready, 1)
                for j in range(4 * gh, 4 * gh + 4):
                    if j:
                        dve.wait_ge(m1_stored, 16 * j)
                    for g in range(8):
                        if g % 4 == 0:
                            dve.wait_ge(m1_full, 2 * j + g // 4 + 1)
                        V.scalar_tensor_tensor(m1_stage[:, g, :], ident[:, :], d_sb[:, 8 * j + g:8 * j + g + 1],
                                               psum[:, 2 * (j % 2) + g // 4, 128 * (g % 4):128 * (g % 4) + 128],
                                               ALU.mult, ALU.add).then_inc(m1_copied, 1)
            dve.wait_ge(m1_stored, 8 * 16)

            with dve.Fori(0, PASSES) as half:
                def rests(q):
                    for s in range(SLOTS):
                        rest(q, s)

                def rest(q, s):
                    dve.wait_ge(head_split, (half * QUADS + q) * SLOTS + s + 1)
                    V.tensor_tensor(w_lo[:, s, :], raw[:, s, :], w_hi[:, s, :].bitcast(F32),
                                    ALU.subtract).then_inc(rest_split, 1)

                def multiplied(q):
                    dve.wait_ge(unit_multiplied, (half * QUADS + q) * SLOTS + SLOTS)

                for k in range(KT_IN):
                    dve.wait_ge(squared, half * KT_IN + k + 1)
                    if k == 0:
                        V.tensor_copy(sq_sum, tmp[:, 0, :]).then_inc(sum_added, 1)
                    else:
                        dve.wait_ge(sum_added, half * KT_IN + k)
                        V.tensor_tensor(sq_sum, sq_sum, tmp[:, k % 2, :], ALU.add).then_inc(sum_added, 1)
                dve.wait_ge(std_ready, half + 1)
                V.reciprocal(rstd_in, rstd_in).then_inc(rstd_ready, 1)
                dve.wait_ge(rstd_ready, half + 1)

                def scale_h(k):
                    dve.wait_ge(xt_loaded[k % 4], (half * 8 + 4 + k // 4 + 1) * 16)
                    if k >= 2:
                        dve.wait_ge(h_ready, half * KT_IN + k - 1)
                    V.scalar_tensor_tensor(tmp[:, k % 2, :], xt_ring[:, k % 4, :], gain_sb[:, k:k + 1],
                                           rstd_in, ALU.mult, ALU.mult).then_inc(h_scaled, 1)

                scale_h(0)
                for k in range(KT_IN):
                    if k + 1 < KT_IN:
                        scale_h(k + 1)
                    dve.wait_ge(h_head, half * KT_IN + k + 1)
                    V.tensor_tensor(h_lo[:, k, :], tmp[:, k % 2, :], h_hi[:, k, :].bitcast(F32),
                                    ALU.subtract).then_inc(h_ready, 1)
                    rest(Q_U + k // 4, k % 4)
                for q in range(4, 8):
                    rests(Q_U + q)
                rests(Q_ZS)
                step_rows(dve, V, half, 1)
                state_inputs(dve, V, half, 1)
                for q in range(1, 8):
                    rests(Q_ZS + q)
                rests(Q_GLU)
                dve.wait_ge(scan_done, (half + 1) * (5 * STEPS + 2) + START)
                shift_states(dve, V, half, 0, 0)
                shift_states(dve, V, half, 1, 0)
                for j in range(8):
                    if j:
                        dve.wait_ge(y_turned, half * 8 + j)
                    dve.wait_ge(y_full, half * 8 + j + 1)
                    y_rows(V, j, 1).then_inc(y_row_dve, 1)
                    if j + 2 < 8:
                        shift_states(dve, V, half, j + 2, 0)
                    dve.wait_ge(g_head, half * 8 + j + 1)
                    V.tensor_tensor(y_lo[:, j, :], tmp[:, j % 2, :], y_hi[:, j, :].bitcast(F32),
                                    ALU.subtract).then_inc(g_ready, 1)
                rests(Q_GLU + 1)

                def glu(b):
                    emptied = set_b_emptied if b else set_a_emptied
                    base = half * 24 + 12 * b
                    for n in range(4):
                        k = 4 * b + n
                        dve.wait_ge(emptied, (half * BLOCKS_SET + B_GLU) * 4 + n + 1 + START)
                        if n or b:
                            dve.wait_ge(glu_step, base + 3 * n)
                        V.tensor_tensor(tmp[:, 0, :], y_hi[:, k, :].bitcast(F32), y_lo[:, k, :].bitcast(F32),
                                        ALU.add).then_inc(glu_step, 1)
                        dve.wait_ge(glu_step, base + 3 * n + 1)
                        V.tensor_tensor(tmp[:, 0, :], tmp[:, 0, :], gate[:, n, :], ALU.mult).then_inc(glu_step, 1)
                        dve.wait_ge(glu_step, base + 3 * n + 2)
                        V.tensor_tensor(z_s[:, k, :], z_s[:, k, :], tmp[:, 0, :], ALU.mult).then_inc(glu_step, 1)

                rests(Q_GLU + 2)
                glu(0)
                rests(Q_GLU + 3)
                rests(Q_Q)
                glu(1)
                for n in range(2):
                    dve.wait_ge(ys_head, half * 2 + n + 1)
                    V.tensor_tensor(y_lo[:, 4 * n:4 * n + 4, :], z_s[:, 4 * n:4 * n + 4, :],
                                    y_hi[:, 4 * n:4 * n + 4, :].bitcast(F32), ALU.subtract).then_inc(ys_ready, 1)
                for q in range(1, 4):
                    rests(Q_Q + q)

                def rotate(dst, b, emptied, first):
                    dve.wait_ge(rope_loaded, (half + 1) * 16)
                    for j in range(2):
                        base = half * 32 + 16 * b + 8 * j
                        if j or b:
                            dve.wait_ge(rope_done, base)
                        cos, sin = rope_sb[:, 0, :], rope_sb[:, 1, :]
                        one, two = psum[:, first + j, :], psum[:, first + 2 + j, :]
                        V.tensor_tensor(gate[:, 0, :], one, cos, ALU.mult).then_inc(rope_step, 1)
                        V.tensor_tensor(gate[:, 1, :], two, sin, ALU.mult).then_inc(rope_step, 1)
                        V.tensor_tensor(gate[:, 2, :], one, sin, ALU.mult).then_inc(emptied, 1)
                        V.tensor_tensor(gate[:, 3, :], two, cos, ALU.mult).then_inc(emptied, 1)
                        dve.wait_ge(rope_step, half * 8 + 4 * b + 2 * j + 2)
                        dve.wait_ge(emptied, (half * BLOCKS_SET + B_QK) * 4 + 2 * j + 2 + START)
                        for hh in range(4):
                            pair, par = (4 * j + hh) // 2, hh % 2
                            rows = slice(32 * hh, 32 * hh + 32)
                            V.tensor_tensor(dst[64 * par:64 * par + 32, pair, :], gate[rows, 0, :], gate[rows, 1, :],
                                            ALU.subtract).then_inc(rope_done, 1)
                            V.tensor_tensor(dst[64 * par + 32:64 * par + 64, pair, :], gate[rows, 2, :], gate[rows, 3, :],
                                            ALU.add).then_inc(rope_done, 1)

                rests(Q_K)
                multiplied(Q_K)
                rotate(q_t, 0, set_a_emptied, 0)
                for q in range(1, 4):
                    rests(Q_K + q)
                rests(Q_V)
                multiplied(Q_V)
                rotate(k_t, 1, set_b_emptied, 4)
                for q in range(1, 4):
                    rests(Q_V + q)
                rests(Q_V + 4)
                multiplied(Q_V + 4)
                for i in range(4):
                    V.tensor_copy(v_row[:, i, 0:512], psum[:, i, :]).then_inc(set_a_emptied, 1)
                for q in range(5, 8):
                    rests(Q_V + q)
                rests(Q_ZR)
                multiplied(Q_ZR)
                for i in range(4):
                    V.tensor_copy(v_row[:, i, 512:1024], psum[:, 4 + i, :]).then_inc(set_b_emptied, 1)
                for q in range(1, 8):
                    rests(Q_ZR + q)
                rests(Q_S)
                dve.wait_ge(tables_loaded, (half + 1) * 3 * 16)
                dve.wait_ge(rope_done, (half + 1) * 32)
                dve.wait_ge(set_a_emptied, (half * BLOCKS_SET + B_ZR + 1) * 4 + START)
                dve.wait_ge(set_b_emptied, (half * BLOCKS_SET + B_ZR + 1) * 4 + START)

                def normalise(t):
                    tok = slice(BLOCK * t, BLOCK * t + BLOCK)
                    base = (half * BLOCKS + t) * 6
                    for par in range(2):
                        dve.wait_ge(ostd_ready, half * 2 * BLOCKS + 2 * t + par + 1)
                        V.reciprocal(o_sq[:, par], o_sq[:, par]).then_inc(o_step, 1)
                        dve.wait_ge(o_step, base + 3 * par + 1)
                        V.tensor_tensor(o_t[:, par], o_t[:, par], o_sq[:, par], ALU.mult).then_inc(o_step, 1)
                        dve.wait_ge(o_step, base + 3 * par + 2)
                        dst = z_r[:, par::2, tok]
                        V.tensor_tensor(dst, dst, o_t[:, par], ALU.mult).then_inc(o_step, 1)

                for t in range(BLOCKS):
                    n = half * BLOCKS + t
                    tok = slice(BLOCK * t, BLOCK * t + BLOCK)
                    if t:
                        dve.wait_ge(kv_full, n)
                    V.tensor_tensor(q_xi, q_t[:, :, tok], xi_sb.rearrange("p (a n) -> p a n", a=4),
                                    ALU.mult).then_inc(q_xi_ready, 1)
                    for par in range(2):
                        dve.wait_ge(scores_full, 2 * n + par + 1)
                        V.tensor_tensor(s_dec[:, par, :], psum[:, 1 + par, :], dmat_sb[:, par, :],
                                        ALU.mult).then_inc(scores_decayed, 1)
                    dve.wait_ge(k_turned, n + 1)
                    V.tensor_tensor(k_zeta, psum[:, 0, :], zeta_sb, ALU.mult).then_inc(k_zeta_ready, 1)
                    dve.wait_ge(kv_full, n + 1)
                    for a in range(4):
                        V.scalar_tensor_tensor(ret_state[:, a, :], ret_state[:, a, :], gdec_sb[:, a:a + 1],
                                               psum[:, 5, 128 * a:128 * a + 128], ALU.mult, ALU.add
                                               ).then_inc(state_ready, 1)
                    normalise(t)
                with dve.Fori(0, MERGES) as b:
                    q0 = Q_S + b * Q_MERGE
                    for q in range(1, 7):
                        rests(q0 + q)
                    multiplied(q0 + 6)
                    dve.wait_ge(set_a_emptied, (half * BLOCKS_SET + B_S + 1 + b) * 4 + START)
                    for n in range(4):
                        V.tensor_tensor(m_t[:, b * 4 + n, :], gate[:, n, :], psum[:, 4 + n, :],
                                        ALU.mult).then_inc(set_b_emptied, 1)
                for n in range(2):
                    dve.wait_ge(yr_head, half * 2 + n + 1)
                    V.tensor_tensor(y_lo[:, 4 * n:4 * n + 4, :], z_r[:, 4 * n:4 * n + 4, :],
                                    y_hi[:, 4 * n:4 * n + 4, :].bitcast(F32), ALU.subtract).then_inc(yr_ready, 1)
                with dve.Fori(0, MERGES) as b:
                    q0 = Q_R + b * Q_MERGE
                    for q in range(1, 7):
                        rests(q0 + q)
                    multiplied(q0 + 6)
                    dve.wait_ge(set_a_emptied, (half * BLOCKS_SET + B_R + 1 + b) * 4 + START)
                    for n in range(4):
                        V.tensor_tensor(gate[:, n, :], gate[:, n, :], psum[:, 4 + n, :],
                                        ALU.mult).then_inc(set_b_emptied, 1)
                    for n in range(4):
                        dve.wait_ge(set_b_emptied, (half * BLOCKS_SET + B_R + b) * 4 + n + 1 + START)
                        V.tensor_tensor(m_t[:, b * 4 + n, :], m_t[:, b * 4 + n, :], gate[:, n, :],
                                        ALU.add).then_inc(m_added, 1)
                for n in range(4):
                    dve.wait_ge(m_head, half * 4 + n + 1)
                    V.tensor_tensor(h_lo[:, 4 * n:4 * n + 4, :], m_t[:, 4 * n:4 * n + 4, :],
                                    h_hi[:, 4 * n:4 * n + 4, :].bitcast(F32), ALU.subtract).then_inc(m_ready, 1)
                dve.wait_ge(m_ready, (half + 1) * 4)
                for c in range(4):
                    for q in range(1, 5 if c < 3 else 4):
                        rests(Q_OUT + 4 * c + q)
                    multiplied(Q_OUT + 4 * c + 4)
                    emptied, first = (set_a_emptied, 0) if c % 2 == 0 else (set_b_emptied, 4)
                    for i in range(4):
                        V.tensor_copy(o_row[:, i, COLS * c:COLS * c + COLS], psum[:, first + i, :]).then_inc(emptied, 1)
                dve.wait_ge(out_squared, (half + 1) * 16)
                V.tensor_reduce(rstd_out[:, :], ssq[:, :, :], AX_X, ALU.add).then_inc(out_stat, 1)
                dve.wait_ge(out_std, half + 1)
                V.reciprocal(rstd_out[:, :], rstd_out[:, :]).then_inc(out_stat, 1)
                dve.wait_ge(out_stat, half * 2 + 2)
                dve.wait_ge(gain_row_loaded, (half + 1) * 16)
                for i in range(4):
                    V.scalar_tensor_tensor(o_row[:, i, :], o_row[:, i, :], rstd_out[:, i:i + 1], gain_row,
                                           ALU.mult, ALU.mult).then_inc(out_scaled, 1)
                    dve.wait_ge(out_scaled, half * 4 + i + 1)
                    dve.wait_ge(x_loaded[i % 2], (half * 2 + i // 2 + 1) * 16)
                    V.tensor_tensor(o_row[:, i, :], o_row[:, i, :], x_ring[:, i % 2, :], ALU.add).then_inc(out_ready, 1)

        @block.tensor
        def _(pe):
            T = nc.tensor
            pe.sem_inc(unit_multiplied, SLOTS)
            pe.wait_ge(consts_loaded, CONSTS * 16)
            for j in range(8):
                if j % 4 == 0:
                    pe.wait_ge(window_ready, j // 4 + 1)
                if j >= 2:
                    pe.wait_ge(m1_copied, 8 * j - 8)
                if j >= 1:
                    pe.wait_ge(m2_copied, 2 * j)
                for n in range(2):
                    for a in range(4):
                        g = 8 * j + 4 * n + a

                        for t in range(STEP):
                            col = 128 * a + GROUP * t
                            m1 = T.matmul(psum[:, 2 * (j % 2) + n, col:col + GROUP],
                                          window[:, g % 32, 7 - t:15 - t, :].rearrange("p i h -> p (i h)"), cc_p[:, g, :],
                                          start=True, stop=True)
                    m1.then_inc(m1_full, 1)
                for n in range(2):
                    for a in range(4):
                        g = 8 * j + 4 * n + a
                        w = window[:, g % 32, 0:8, :].rearrange("p i h -> p (i h)")
                        m2 = T.transpose(psum[:, 4 + n, 128 * a:128 * a + 128], w, ident[:, :])
                m2.then_inc(m2_full, 1)
            pe.wait_ge(m1_copied, 64)
            pe.wait_ge(m2_copied, 16)

            with pe.Fori(0, PASSES) as half:
                def unit_ready(q, s):
                    pe.wait_ge(rest_split, (half * QUADS + q) * SLOTS + s + 1 + SLOTS)

                def columns_out(q, first, x_hi, x_lo, tiles, ready=None):
                    for k in range(tiles):
                        if ready is not None:
                            ready(k)
                        s = k % SLOTS
                        unit_ready(q + k // SLOTS, s)
                        for n in range(4):
                            cols = slice(P * n, P * n + P)
                            bank = psum[:, first + n, :]
                            T.matmul(bank, w_hi[:, s, cols], x_hi[:, k, :], start=(k == 0), stop=False)
                            T.matmul(bank, w_lo[:, s, cols], x_hi[:, k, :], start=False, stop=False)
                            last = T.matmul(bank, w_hi[:, s, cols], x_lo[:, k, :], start=False, stop=(k == tiles - 1))
                        last.then_inc(unit_multiplied, 1)

                def rows_out(q, first, x_hi, x_lo, pick, ready=None):
                    for k in range(KT_IN):
                        if ready is not None:
                            ready(k)
                        s = k % SLOTS
                        unit_ready(q + k // SLOTS, s)
                        for n in range(4):
                            bank = psum[:, first + n, :]
                            T.matmul(bank, pick(x_hi, k, n), w_hi[:, s, :], start=(k == 0), stop=False)
                            T.matmul(bank, pick(x_hi, k, n), w_lo[:, s, :], start=False, stop=False)
                            last = T.matmul(bank, pick(x_lo, k, n), w_hi[:, s, :], start=False, stop=(k == KT_IN - 1))
                        last.then_inc(unit_multiplied, 1)

                def empty(which, b):
                    pe.wait_ge(which, (half * BLOCKS_SET + b) * 4 + START)

                def step_tokens(a, k, n):
                    return a[:, k, n::4]

                def block_tokens(a, k, n):
                    return a[:, k, P * n:P * n + P]

                pe.wait_ge(sum_added, (half + 1) * KT_IN)
                empty(set_a_emptied, 0)
                empty(set_b_emptied, 0)
                T.matmul(psum[:, 0, :], ones_sb[:, :], sq_sum, start=True, stop=True).then_inc(sum_full, 1)
                rows_out(Q_U, 0, h_hi, h_lo, step_tokens, lambda k: pe.wait_ge(h_ready, half * KT_IN + k + 1))
                rows_out(Q_U + 4, 4, h_hi, h_lo, step_tokens)
                empty(set_a_emptied, B_U + 1)
                empty(set_b_emptied, B_U + 1)
                for r in range(16):
                    if r >= 8:
                        done = step_rows_dve if r % 2 else step_rows_act
                        pe.wait_ge(done, half * 16 + 2 * ((r - 8) // 2 + 1))
                    pe.sem_inc(pe_waited, 1)
                    for a in range(4):
                        g = 4 * r + a
                        last = T.transpose(psum[0:64, r % 8, 128 * a:128 * a + 128],
                                           u_tok[:, g, :, :].rearrange("p q h -> p (q h)"), ident[:, :])
                    last.then_inc(step_rows_full, 1)
                pe.wait_ge(step_rows_act, (half + 1) * 16)
                pe.wait_ge(step_rows_dve, (half + 1) * 16)
                for j in range(8):
                    pe.wait_ge(m2_loaded[j % 4], (half * 2 + j // 4 + 1) * 16)
                    for a in range(8):
                        last = T.matmul(psum[:, j, 64 * a:64 * a + 64], m2_ring[:, j % 4, 128 * a:128 * a + 128],
                                        u_step[:, 8 * j + a, :], start=True, stop=True)
                    last.then_inc(step_in_full, 1)
                pe.wait_ge(state_in_act, (half + 1) * 16)
                pe.wait_ge(state_in_dve, (half + 1) * 16)
                columns_out(Q_ZS, 0, h_hi, h_lo, KT_IN)
                columns_out(Q_ZS + 4, 4, h_hi, h_lo, KT_IN)
                empty(set_a_emptied, B_ZS + 1)
                empty(set_b_emptied, B_ZS + 1)

                def y_products(j):
                    if j >= 2:
                        pe.wait_ge(y_row_act, half * 8 + j - 1)
                        pe.wait_ge(y_row_dve, half * 8 + j - 1)
                    pe.wait_ge(shifted_act, half * 16 + 2 * j + 2)
                    pe.wait_ge(shifted_dve, half * 16 + 2 * j + 2)
                    pe.wait_ge(mat_loaded[j % 2], (half * 4 + j // 2 + 1) * 32)
                    for a in range(8):
                        bank = psum[0:STEPS, 2 * (j % 2) + a // 4, 128 * (a % 4):128 * (a % 4) + 128]
                        cols = slice(128 * a, 128 * a + 128)
                        T.matmul(bank, u_step[:, 8 * j + a, :], mat_ring[:, j % 2, 0, cols], start=True, stop=False)
                        last = T.matmul(bank, sc_ring[:, j % 2, a, :], mat_ring[:, j % 2, 1, cols], start=False, stop=True)
                    last.then_inc(y_full, 1)

                def y_turn(j):
                    pe.wait_ge(y_row_act, half * 8 + j + 1)
                    pe.wait_ge(y_row_dve, half * 8 + j + 1)
                    if j >= 2:
                        pe.wait_ge(gelu_done, half * 8 + j - 1)
                    pe.sem_inc(pe_waited, 1)
                    for t in range(STEP):
                        last = T.transpose(psum[:, 4 + j % 2, STEPS * t:STEPS * t + STEPS], y_row[:, t, :],
                                           ident[0:STEPS, 0:STEPS])
                    last.then_inc(y_turned, 1)

                y_products(0)
                for j in range(8):
                    if j + 1 < 8:
                        y_products(j + 1)
                    y_turn(j)
                columns_out(Q_GLU, 0, y_hi, y_lo, KT_MID, lambda k: pe.wait_ge(g_ready, half * 8 + k + 1))
                columns_out(Q_GLU + 2, 4, y_hi, y_lo, KT_MID)
                empty(set_a_emptied, B_QK)
                columns_out(Q_Q, 0, h_hi, h_lo, KT_IN)
                empty(set_b_emptied, B_QK)
                columns_out(Q_K, 4, h_hi, h_lo, KT_IN)
                empty(set_a_emptied, B_V)
                rows_out(Q_V, 0, h_hi, h_lo, block_tokens)
                empty(set_b_emptied, B_V)
                rows_out(Q_V + 4, 4, h_hi, h_lo, block_tokens)
                empty(set_a_emptied, B_ZR)
                columns_out(Q_ZR, 0, h_hi, h_lo, KT_IN)
                empty(set_b_emptied, B_ZR)
                columns_out(Q_ZR + 4, 4, h_hi, h_lo, KT_IN)
                empty(set_a_emptied, B_ZR + 1)
                empty(set_b_emptied, B_ZR + 1)
                pe.wait_ge(rope_done, (half + 1) * 32)
                def square_sums(t):
                    n = half * BLOCKS + t
                    for par in range(2):
                        pe.wait_ge(o_squared, 2 * n + par + 1)
                        if t:
                            pe.wait_ge(ostd_ready, 2 * n + par - 1)
                        T.matmul(psum[:, 6 + par, :], ones_sb[:, :],
                                 o_sq[:, par].rearrange("p a n -> p (a n)"), start=True, stop=True).then_inc(osum_full, 1)

                for t in range(BLOCKS):
                    n = half * BLOCKS + t
                    tok = slice(BLOCK * t, BLOCK * t + BLOCK)
                    if t:
                        pe.wait_ge(scores_decayed, 2 * n)
                        pe.wait_ge(k_zeta_ready, n)
                    for a in range(4):
                        for par in range(2):
                            rows = slice(64 * par, 64 * par + 64)
                            last = T.matmul(psum[:, 1 + par, 128 * a:128 * a + 128], k_t[rows, a, tok], q_t[rows, a, tok],
                                            start=True, stop=True)
                            if a == 3:
                                last.then_inc(scores_full, 1)
                    for a in range(4):
                        last = T.transpose(psum[:, 0, 128 * a:128 * a + 128], k_t[:, a, tok], ident[:, :])
                    last.then_inc(k_turned, 1)
                    pe.wait_ge(q_xi_ready, n + 1)
                    pe.wait_ge(state_ready, 4 * n + START)
                    for par in range(2):
                        rows = slice(64 * par, 64 * par + 64)
                        pe.wait_ge(scores_decayed, 2 * n + par + 1)
                        if t:
                            pe.wait_ge(o_copied, 2 * n + par - 1)
                        for a in range(4):
                            head = 2 * a + par
                            bank = psum[:, 3 + par, 128 * a:128 * a + 128]
                            T.matmul(bank, v_row[:, t, V_HEAD * head:V_HEAD * head + V_HEAD],
                                     s_dec[:, par, 128 * a:128 * a + 128], start=True, stop=False)
                            last = T.matmul(bank, ret_state[rows, a, :], q_xi[rows, a, :], start=False, stop=True)
                        last.then_inc(o_full, 1)
                    pe.wait_ge(k_zeta_ready, n + 1)
                    for a in range(4):
                        for par in range(2):
                            head = 2 * a + par
                            last = T.matmul(psum[64 * par:64 * par + 64, 5, 128 * a:128 * a + 128],
                                            k_zeta[:, 64 * head:64 * head + 64],
                                            v_row[:, t, V_HEAD * head:V_HEAD * head + V_HEAD], start=True, stop=True)
                    last.then_inc(kv_full, 1)
                    square_sums(t)
                pe.wait_ge(ostd_ready, (half + 1) * BLOCKS * 2)
                pe.wait_ge(state_ready, (half + 1) * BLOCKS * 4 + START)
                pe.wait_ge(o_copied, (half + 1) * BLOCKS * 2)
                pe.wait_ge(ys_ready, (half + 1) * 2)
                pe.sem_inc(pe_waited, 1)
                with pe.Fori(0, MERGES) as b:
                    q0 = Q_S + b * Q_MERGE
                    columns_out(q0, 0, h_hi, h_lo, KT_IN)
                    empty(set_b_emptied, B_S + b)
                    columns_out(q0 + 4, 4, y_hi, y_lo, KT_MID)
                    empty(set_a_emptied, B_S + 1 + b)
                    pe.sem_inc(pe_waited, 1)
                with pe.Fori(0, MERGES) as b:
                    q0 = Q_R + b * Q_MERGE
                    columns_out(q0, 0, h_hi, h_lo, KT_IN)
                    empty(set_b_emptied, B_R + b)
                    pe.wait_ge(yr_ready, (half + 1) * 2)
                    columns_out(q0 + 4, 4, y_hi, y_lo, KT_MID)
                    empty(set_a_emptied, B_R + 1 + b)
                    pe.sem_inc(pe_waited, 1)
                for c in range(4):
                    which, first = (set_a_emptied, 0) if c % 2 == 0 else (set_b_emptied, 4)
                    empty(which, B_OUT + c // 2)
                    ready = (lambda k: pe.wait_ge(m_ready, half * 4 + k // 4 + 1)) if c == 0 else None
                    rows_out(Q_OUT + 4 * c, first, h_hi, h_lo, block_tokens, ready)


def retention_tables():
    log_g = np.log1p(-np.exp2(-5.0 - np.arange(HEADS)))
    idx = np.arange(BLOCK)
    scale = QK_HEAD ** -0.5
    ahead = (idx[:, None] // CHUNK) > (idx[None, :] // CHUNK)
    dist = np.abs(idx[None, :] - idx[:, None])
    dmat = np.where(ahead, 0.0, np.exp(dist[None] * log_g[:, None, None])) * scale
    dmat = dmat.reshape(4, 2, BLOCK, BLOCK).transpose(2, 1, 0, 3).reshape(BLOCK, -1)
    zeta = np.exp((BLOCK - 1 - idx)[:, None] * log_g[None, :]) * scale
    zeta = np.repeat(zeta, QK_HEAD, axis=1)
    xi = np.exp((idx + 1.0)[None, :] * log_g[:, None])
    xi = np.repeat(xi.reshape(4, 2, 1, BLOCK), QK_HEAD, axis=2).transpose(1, 2, 0, 3).reshape(P, -1)
    gdec = np.repeat(np.exp(BLOCK * log_g).reshape(4, 2).T, QK_HEAD, axis=0)
    return [np.ascontiguousarray(a, dtype=np.float32) for a in (dmat, zeta, xi, gdec)]


def rope_table():
    half = QK_HEAD // 2
    inv = np.float32(ROPE_BASE) ** (-np.arange(0, QK_HEAD, 2, dtype=np.float32) / np.float32(QK_HEAD))
    angle = (np.arange(SEQ, dtype=np.float32)[None, :] * inv.astype(np.float32)[:, None]).astype(np.float32)
    both = np.stack([np.cos(angle.astype(np.float64)), np.sin(angle.astype(np.float64))], 1)
    both = np.tile(both, (P // half, 1, 1)).reshape(P, 2, PASSES, TOK).transpose(2, 0, 1, 3)
    return np.ascontiguousarray(both, dtype=np.float32)


def layouts(x, norm_pre, w_in, lam_re, lam_im, log_step, s5_b_re, s5_b_im, s5_c_re, s5_c_im,
            s5_d, w_glu, b_glu, w_proj_s5, w_proj_ret, w_out, norm_post):
    def units(w):
        r, c = w.shape
        return w.reshape(r // P, P, c // COLS, COLS).transpose(2, 0, 1, 3)

    w = w_in[0]
    at = np.cumsum([0, S5_WIDTH, S5_WIDTH, 512, 512, S5_WIDTH, S5_WIDTH, D_MODEL, D_MODEL])
    part = [w[:, a:b] for a, b in zip(at[:-1], at[1:])]
    rot = np.arange(512).reshape(HEADS, 2, QK_HEAD // 2).transpose(1, 0, 2).reshape(-1)
    runs = [units(part[0]), units(part[1]), units(w_glu[0]), units(part[2][:, rot]), units(part[3][:, rot]),
            units(part[4]), units(part[5])]
    for gate, proj in ((part[6], w_proj_s5[0]), (part[7], w_proj_ret[0])):
        g, p = units(gate), units(proj)
        for b in range(MERGES):
            runs += [g[b:b + 1], p[b:b + 1]]
    runs.append(units(w_out[0]))
    stream = np.concatenate([r.reshape(-1, P, COLS) for r in runs], axis=0)

    def states(a):
        return np.ascontiguousarray(np.concatenate([a.T, a.T], axis=0))

    def stack(a, b):
        both = np.concatenate([a.transpose(1, 0, 2), b.transpose(1, 0, 2)], axis=0)
        return np.ascontiguousarray(both.reshape(P, -1))

    br, bi = s5_b_re[0], s5_b_im[0]
    cr, ci = s5_c_re[0].transpose(0, 2, 1), s5_c_im[0].transpose(0, 2, 1)
    d = np.tile(s5_d[0].reshape(GROUPS, GROUP).T, (STEP, 1))
    signs = np.ones((P, 2), np.float32)
    signs[64:, 0] = -1.0
    signs[:64, 1] = -1.0
    dmat, zeta, xi, gdec = retention_tables()
    xs = x[0]
    arrays = {
        "x": xs.reshape(SEQ // P, P, D_MODEL),
        "xT": xs.reshape(PASSES, TOK, KT_IN, P).transpose(0, 2, 3, 1).reshape(PASSES * KT_IN, P, TOK),
        "wstream": stream,
        "gain_in": norm_pre[0].reshape(KT_IN, P).T,
        "gain_out": np.broadcast_to(norm_post[0], (P, D_MODEL)),
        "b_glu": b_glu[0].reshape(KT_MID, P).T,
        "lam_re": states(lam_re[0]),
        "lam_im": states(lam_im[0]),
        "log_step": np.broadcast_to(log_step[0], (P, GROUPS)),
        "b_ri": stack(br, bi), "b_ir": stack(bi, br),
        "c_ri": stack(cr, ci), "c_ir": stack(ci, cr),
        "d_rep": d, "signs": signs, "eye": np.eye(P, dtype=np.float32),
        "ones": np.ones((P, P), np.float32),
        "dmat": dmat, "zeta": zeta, "xi": xi, "gdec": gdec, "rope": rope_table(),
    }
    return {n: np.ascontiguousarray(a) for n, a in arrays.items()}


def kernel(**inputs):
    import concourse.bacc as bacc
    from concourse.bass_utils import run_bass_kernel_spmd

    arrays = layouts(**{n: np.asarray(a) for n, a in inputs.items()})
    nc = bacc.Bacc("TRN2", target_bir_lowering=False, num_devices=1)
    args = {n: nc.dram_tensor(f"in_{n}", a.shape, F32, kind="ExternalInput").ap() for n, a in arrays.items()}
    args["mats"] = nc.dram_tensor("mats", (3, 8, P, 1024), F32, kind="Internal").ap()
    args["out"] = nc.dram_tensor("out_rows", (SEQ // P, P, D_MODEL), F32, kind="ExternalOutput").ap()
    build_program(nc, **args)
    r = run_bass_kernel_spmd(nc, [{f"in_{n}": a for n, a in arrays.items()}], core_ids=[0])
    return r.results[0]["out_rows"].reshape(1, SEQ, D_MODEL)
```

```python
import math
from contextlib import ExitStack

import numpy as np

import concourse.bass as bass
from concourse import mybir

F32 = mybir.dt.float32
F32R = mybir.dt.float32r
I32 = mybir.dt.int32
ALU = mybir.AluOpType
ACT = mybir.ActivationFunctionType
AX_X = mybir.AxisListType.X

P = 128
D_MODEL = 2048
SEQ = 1024
CHUNK = 64
EPS = 1e-6
S5_WIDTH = D_MODEL // 2
GROUP = 16
GROUPS = S5_WIDTH // GROUP
STATE = 64
HEADS = 8
V_HEAD = S5_WIDTH // HEADS
QK_HEAD = V_HEAD // 2
ROPE_BASE = 10000.0

PASSES = 2
TOK = SEQ // PASSES
KT_IN = D_MODEL // P
KT_MID = S5_WIDTH // P
COLS = 512
STEP = 8
STEPS = TOK // STEP
BLOCK = 128
BLOCKS = TOK // BLOCK

SLOTS = 4
Q_U, Q_ZS, Q_GLU, Q_Q, Q_K, Q_V, Q_ZR, Q_S, Q_R, Q_OUT = 0, 8, 16, 20, 24, 28, 36, 44, 68, 92
QUADS = 108
Q_MERGE = 6
MERGES = D_MODEL // COLS
B_U, B_ZS, B_GLU, B_QK, B_V, B_ZR, B_S, B_R, B_OUT = 0, 1, 2, 3, 4, 5, 6, 10, 14
BLOCKS_SET = 16
START = 1
CONSTS = 5
SCAN = 5 * STEPS + 2


def build_program(nc, x, xT, wstream, gain_in, gain_out, b_glu, lam_re, lam_im, log_step,
                  b_ri, b_ir, c_ri, c_ir, d_rep, signs, eye, ones, dmat, zeta, xi,
                  gdec, rope, mats, rstd, out):
    with ExitStack() as ctx:
        def sb(name, shape, dt=F32):
            return ctx.enter_context(nc.sbuf_tensor(name, shape, dt))

        def sem(name):
            return ctx.enter_context(nc.semaphore(name))

        raw = sb("raw", [P, SLOTS, COLS])
        w_hi = sb("w_hi", [P, SLOTS, COLS], F32R)
        with nc.sbuf_tensor("plain", [P, SLOTS * COLS + 2 * KT_IN * TOK + 2 * KT_MID * TOK], F32) as plain_mem:
            pass
        w_lo = sb("w_lo", [P, SLOTS, COLS], F32R)
        h_hi = sb("h_hi", [P, KT_IN, TOK], F32R)
        h_lo = sb("h_lo", [P, KT_IN, TOK], F32R)
        y_hi = sb("y_hi", [P, KT_MID, TOK], F32R)
        y_lo = sb("y_lo", [P, KT_MID, TOK], F32R)
        R2, R3, R4 = 8192, 8192 + 4160, 8192 + 4160 + 4096
        work = sb("work", [P, R4 + 2048])
        tmp = sb("tmp", [P, 2, TOK])
        eye_sb = sb("eye_sb", [P, 2 * P - GROUP])
        ones_sb = sb("ones_sb", [P, P])
        gain_sb = sb("gain_sb", [P, KT_IN])
        bglu_sb = sb("bglu_sb", [P, KT_MID])
        gdec_sb = sb("gdec_sb", [P, 4])
        eps_sb = sb("eps_sb", [P, 1])
        scan_re = sb("scan_re", [P, 2, 32])
        scan_im = sb("scan_im", [P, 2, 32])
        carry = sb("carry", [P, 2, 32])
        scan_t = sb("scan_t", [P, 2, 2, 32])
        ret_state = sb("ret_state", [P, 4, V_HEAD])
        ssq = sb("ssq", [P, 4, 4])
        rstd_out = sb("rstd_out", [P, 4])
        sign_sb = sb("sign_sb", [P, 2])
        psum = ctx.enter_context(nc.psum_tensor("psum", [P, 8, COLS], F32))
        ident = eye_sb[:, 0:P]

        def area(a, n):
            return work[:, a:a + n]

        PLAIN = {"w_lo": 0, "h_hi": 2048, "h_lo": 2048 + 8192, "y_hi": 2048 + 2 * 8192, "y_lo": 2048 + 2 * 8192 + 4096}

        def plain(name, a, n):
            return plain_mem[:, PLAIN[name] + a:PLAIN[name] + a + n]

        u_tok = area(0, 4096).rearrange("p (g q h) -> p g q h", g=GROUPS, q=4)
        mat_ring = area(0, 4096).rearrange("p (s m n) -> p s m n", s=2, m=2)
        q_t = area(0, 2048).rearrange("p (a n) -> p a n", a=4)
        k_t = area(2048, 2048).rearrange("p (a n) -> p a n", a=4)
        m_t = area(0, 8192).rearrange("p (k n) -> p k n", k=KT_IN)
        o_row = area(0, 8192).rearrange("p (i n) -> p i n", i=4)
        u_step = area(4096, 4096).rearrange("p (g c) -> p g c", g=GROUPS)
        v_row = area(4096, 4096).rearrange("p (i n) -> p i n", i=4)
        state = area(R2, 4160).rearrange("p (c r k) -> p c r k", c=STEPS + 1, r=2)
        rope_sb = area(R2, 1024).rearrange("p (s n) -> p s n", s=2)
        z_r = area(R2, 4096).rearrange("p (k n) -> p k n", k=KT_MID)
        gain_row = area(R2, 2048)
        m2_ring = area(R3, 4096).rearrange("p (s n) -> p s n", s=4)
        z_s = area(R3, 4096).rearrange("p (k n) -> p k n", k=KT_MID)
        o_t = [a.rearrange("p (h a n) -> p h a n", h=2, a=4)
               for a in (area(R3, 1024), tmp[:, :, :].rearrange("p a n -> p (a n)"))]
        o_sq = area(R3 + 1024, 1024).rearrange("p (h a n) -> p h a n", h=2, a=4)
        dmat_sb = area(R3 + 2048, 1024).rearrange("p (h n) -> p h n", h=2)
        zeta_sb = area(R3 + 3072, 512)
        xi_sb = area(R3 + 3584, 512)
        x_rows = area(R3, 4096).rearrange("p (s n) -> p s n", s=2)
        xt_ring = area(R4, 2048).rearrange("p (s n) -> p s n", s=4)
        sc_ring = area(R4, 1024).rearrange("p (s g c) -> p s g c", s=2, g=8)
        y_row = work[0:STEPS, R4 + 1024:R4 + 2048].rearrange("p (t n) -> p t n", t=STEP)
        gate = area(R4, 2048).rearrange("p (s n) -> p s n", s=4)
        s_dec = area(R4, 1024).rearrange("p (h n) -> p h n", h=2)
        q_xi = area(R4 + 1024, 512).rearrange("p (a n) -> p a n", a=4)
        k_zeta = area(R4 + 1536, 512)

        rstd_in = plain("y_lo", 7 * TOK, TOK)
        x_rows_2 = plain("y_hi", 0, 4096).rearrange("p (s n) -> p s n", s=2)

        raw_loaded = [sem(f"raw_loaded{s}") for s in range(SLOTS)]
        head_split = sem("head_split")
        rest_split = sem("rest_split")
        unit_multiplied = sem("unit_multiplied")
        set_a_emptied = sem("set_a_emptied")
        set_b_emptied = sem("set_b_emptied")
        consts_loaded = sem("consts_loaded")
        rates_loaded = sem("rates_loaded")
        params_loaded = sem("params_loaded")
        sq_loaded = [sem(f"sq_loaded{s}") for s in range(SLOTS)]
        squared = sem("squared")
        square_added = sem("square_added")
        eps_ready = sem("eps_ready")
        std_ready = sem("std_ready")
        rstd_ready = sem("rstd_ready")
        rstd_stored = sem("rstd_stored")
        rstd_loaded = sem("rstd_loaded")
        setup_step = sem("setup_step")
        powers_ready = sem("powers_ready")
        pool_setup = sem("pool_setup")
        window_ready = sem("window_ready")
        m2_full = sem("m2_full")
        m2_copied = sem("m2_copied")
        lags_full = sem("lags_full")
        lags_ready = sem("lags_ready")
        m1_full = sem("m1_full")
        m1_act, m1_dve = sem("m1_act"), sem("m1_dve")
        m1_stored, m2_stored = sem("m1_stored"), sem("m2_stored")
        m3_stored = [sem(f"m3_stored{s}") for s in range(2)]
        xt_loaded = [sem(f"xt_loaded{s}") for s in range(4)]
        h_scaled = sem("h_scaled")
        h_head = sem("h_head")
        h_ready = sem("h_ready")
        step_rows_full = sem("step_rows_full")
        step_rows_act, step_rows_dve = sem("step_rows_act"), sem("step_rows_dve")
        m2_loaded = [sem(f"m2_loaded{s}") for s in range(4)]
        step_in_full = sem("step_in_full")
        state_in_act, state_in_dve = sem("state_in_act"), sem("state_in_dve")
        scan_done = sem("scan_done")
        mat_loaded = [sem(f"mat_loaded{s}") for s in range(2)]
        shifted_act, shifted_dve = sem("shifted_act"), sem("shifted_dve")
        y_full = sem("y_full")
        y_row_act, y_row_dve = sem("y_row_act"), sem("y_row_dve")
        y_turned = sem("y_turned")
        gelu_done = sem("gelu_done")
        g_head = sem("g_head")
        g_ready = sem("g_ready")
        glu_step = sem("glu_step")
        ys_head, ys_ready = sem("ys_head"), sem("ys_ready")
        rope_loaded = sem("rope_loaded")
        rope_step = sem("rope_step")
        rope_done = sem("rope_done")
        tables_loaded = sem("tables_loaded")
        k_turned = sem("k_turned")
        k_zeta_ready = sem("k_zeta_ready")
        scores_full = sem("scores_full")
        scores_decayed = sem("scores_decayed")
        q_xi_ready = sem("q_xi_ready")
        o_full = sem("o_full")
        kv_full = sem("kv_full")
        state_ready = sem("state_ready")
        o_copied = sem("o_copied")
        o_squared = sem("o_squared")
        osum_full = sem("osum_full")
        ostd_ready = sem("ostd_ready")
        o_inverse = sem("o_inverse")
        o_scaled = sem("o_scaled")
        z_scaled = sem("z_scaled")
        yr_head, yr_ready = sem("yr_head"), sem("yr_ready")
        m_added = sem("m_added")
        m_head, m_ready = sem("m_head"), sem("m_ready")
        out_squared = sem("out_squared")
        out_stat = sem("out_stat")
        out_std = sem("out_std")
        out_ready = sem("out_ready")
        row_block_full = sem("row_block_full")
        x_loaded = sem("x_loaded")
        gain_row_loaded = sem("gain_row_loaded")
        out_stored = sem("out_stored")
        rows_free = sem("rows_free")

        pool_waited, pe_waited = sem("pool_waited"), sem("pe_waited")

        block = ctx.enter_context(nc.Block())

        @block.sync
        def _(sp):
            sp.sem_inc(rest_split, SLOTS)
            sp.sem_inc(h_scaled, SLOTS)
            for counted in (m_added, out_squared, out_ready, rows_free, scan_done, state_ready,
                            set_a_emptied, set_b_emptied):
                sp.sem_inc(counted, START)
            sp.sem_inc(squared, SLOTS)
            with sp.Fori(0, PASSES * KT_IN // SLOTS) as i:
                for s in range(SLOTS):
                    sp.wait_ge(squared, i * SLOTS + s + 1)
                    sp.dma_start(raw[:, s, :], xT[i * SLOTS + s]).then_inc(sq_loaded[s], 16)
            sp.wait_ge(squared, PASSES * KT_IN + SLOTS)
            with sp.Fori(0, PASSES) as half:
                def load_unit(q, s):
                    sp.wait_ge(rest_split, (half * QUADS + q) * SLOTS + s + 1)
                    sp.dma_start(raw[:, s, :], wstream[q * SLOTS + s]).then_inc(raw_loaded[s], 16)

                sp.wait_ge(rstd_stored, 16)
                sp.wait_ge(m_added, half * 16 + START)
                sp.dma_start(rstd_in, rstd[half]).then_inc(rstd_loaded, 16)
                with sp.Fori(0, KT_IN // SLOTS) as q:
                    for s in range(SLOTS):
                        load_unit(q, s)
                        sp.wait_ge(h_scaled, half * KT_IN + q * SLOTS + s + 1)
                        sp.dma_start(xt_ring[:, s, :], xT[half * KT_IN + q * SLOTS + s]).then_inc(xt_loaded[s], 16)
                with sp.Fori(KT_IN // SLOTS, QUADS) as q:
                    for s in range(SLOTS):
                        load_unit(q, s)

        window = plain("h_hi", 0, 8192).rearrange("p (g i h) -> p g i h", g=GROUPS, i=STEP)
        m1_stage = area(0, 8192).rearrange("p (g t h) -> p g t h", g=GROUPS, t=STEP)
        m2_stage = area(R2, 8192)
        bb_p = plain("h_lo", 0, 1024).rearrange("p (g h) -> p g h", g=GROUPS)
        bb_q = plain("h_lo", 1024, 1024).rearrange("p (g h) -> p g h", g=GROUPS)
        b_tmp = plain("h_lo", 2048, 1024).rearrange("p (g h) -> p g h", g=GROUPS)
        b_tmp2 = plain("h_lo", 3072, 1024).rearrange("p (g h) -> p g h", g=GROUPS)
        win_tmp = plain("h_lo", 4096, 2048).rearrange("p (g i h) -> p g i h", g=16, i=STEP)
        lags = plain("h_lo", 6144, 1024)
        rstd_stage = plain("h_lo", 7168, 1024)
        cc_p = plain("y_hi", 0, 1024).rearrange("p (g h) -> p g h", g=GROUPS)
        cc_q = plain("y_hi", 1024, 1024).rearrange("p (g h) -> p g h", g=GROUPS)
        m3_stage = [plain("y_hi", 2048 + 1024 * n, 1024).rearrange("p (g t h) -> p g t h", g=8, t=STEP) for n in range(2)]
        m3_tmp = plain("y_lo", 0, 1024).rearrange("p (g t h) -> p g t h", g=8, t=STEP)
        pow_re = plain("y_lo", 1024, 576).rearrange("p (j g) -> p j g", j=9)
        pow_im = plain("y_lo", 1600, 576).rearrange("p (j g) -> p j g", j=9)
        small = tmp[:, :, :].rearrange("p a n -> p (a n)")
        (lam_r, lam_i, step_sb, par_re, par_im, d_sb, s0, s1, s2, s3, s4, s5, s6, s7, s8, s9) = [
            small[:, 64 * n:64 * n + 64] for n in range(16)]

        def copy(eng, dst, src):
            if eng is nc.scalar:
                return eng.activation(dst, src, ACT.Copy)
            return eng.tensor_copy(dst, src)

        def m1_banks(seq, eng, odd):
            done = m1_dve if odd else m1_act
            for n in range(odd, 16, 2):
                seq.wait_ge(m1_full, n + 1)
                gs = slice(32 * (n % 2), 32 * (n % 2) + 32)
                copy(eng, m1_stage[:, gs, n // 2, :], psum[:, n % 8, :].rearrange("p (g h) -> p g h", h=GROUP)).then_inc(done, 1)

        def step_rows(seq, eng, half, odd):
            done = step_rows_dve if odd else step_rows_act
            for r in range(odd, 16, 2):
                seq.wait_ge(step_rows_full, half * 16 + r + 1)
                for s in range(2):
                    src = psum[0:64, r % 8, :].rearrange("p (a c s) -> p a c s", a=4, s=2)[:, :, :, s]
                    copy(eng, u_step[64 * s:64 * s + 64, 4 * r:4 * r + 4, :], src).then_inc(done, 1)

        def state_inputs(seq, eng, half, odd):
            done = state_in_dve if odd else state_in_act
            for j in range(odd, 8, 2):
                seq.wait_ge(step_in_full, half * 8 + j + 1)
                for par in range(2):
                    for r in range(2):
                        src = psum[64 * r:64 * r + 64, j, :].rearrange("p (k g c) -> p k g c", k=4, g=2)[:, :, par, :]
                        dst = state[64 * par:64 * par + 64, 1:STEPS + 1, r, 4 * j:4 * j + 4].rearrange("p c k -> p k c")
                        copy(eng, dst, src).then_inc(done, 1)

        def shift_states(seq, eng, half, j, r):
            done = shifted_act if eng is nc.scalar else shifted_dve
            if j >= 2:
                seq.wait_ge(y_full, half * 8 + j - 1)
            for par in range(2):
                src = state[64 * par:64 * par + 64, 0:STEPS, r, 4 * j:4 * j + 4].rearrange("p c k -> p k c")
                copy(eng, sc_ring[64 * r:64 * r + 64, j % 2, par::2, :], src).then_inc(done, 1)

        def y_rows(eng, j, n):
            src = psum[0:STEPS, 2 * (j % 2) + n, :].rearrange("p (q t g) -> p q t g", q=4, t=STEP)
            return copy(eng, y_row[:, :, 64 * n:64 * n + 64].rearrange("p t (q g) -> p q t g", q=4), src)

        @block.gpsimd
        def _(pool):
            for dst, src in ((ones_sb[:, :], ones), (eye_sb[:, :], eye), (gain_sb[:, :], gain_in),
                             (bglu_sb[:, :], b_glu), (gdec_sb[:, :], gdec)):
                pool.dma_start(dst, src).then_inc(consts_loaded, 16)
            pool.wait_ge(powers_ready, 1)
            for j in range(8):
                gs = slice(8 * j, 8 * j + 8)

                def powers(a):
                    return a[:, 1:9, gs].rearrange("p t g -> p g t").unsqueeze(3).broadcast_to([P, 8, STEP, GROUP])

                def coefs(a):
                    return a[:, gs, :].unsqueeze(2).broadcast_to([P, 8, STEP, GROUP])

                if j >= 2:
                    pool.wait_ge(m3_stored[j % 2], 16 * (j // 2))
                stage = m3_stage[j % 2]
                pool.tensor_tensor(stage, coefs(cc_p), powers(pow_re), ALU.mult).then_inc(pool_setup, 1)
                if j:
                    pool.wait_ge(pool_setup, 3 * j)
                pool.tensor_tensor(m3_tmp, coefs(cc_q), powers(pow_im), ALU.mult).then_inc(pool_setup, 1)
                pool.wait_ge(pool_setup, 3 * j + 2)
                pool.tensor_tensor(stage, stage, m3_tmp, ALU.subtract).then_inc(pool_setup, 1)
                pool.wait_ge(pool_setup, 3 * j + 3)
                pool.dma_start(mats[2, j], stage.rearrange("p g t h -> p (g t h)")).then_inc(m3_stored[j % 2], 16)

            with pool.Fori(0, PASSES) as half:
                pool.wait_ge(m1_stored, 8 * 16)
                pool.wait_ge(m2_stored, 8 * 16)
                pool.wait_ge(m3_stored[0], 4 * 16)
                pool.wait_ge(m3_stored[1], 4 * 16)
                pool.wait_ge(out_ready, half * 4 + START)
                pool.sem_inc(pool_waited, 1)
                for j in range(8):
                    if j >= 4:
                        pool.wait_ge(step_in_full, half * 8 + j - 3)
                        pool.sem_inc(pool_waited, 1)
                    pool.dma_start(m2_ring[:, j % 4, :], mats[1, j]).then_inc(m2_loaded[j % 4], 16)

                def load_mats(j):
                    pool.dma_start(mat_ring[:, j % 2, 0, :], mats[0, j]).then_inc(mat_loaded[j % 2], 16)
                    pool.dma_start(mat_ring[:, j % 2, 1, :], mats[2, j]).then_inc(mat_loaded[j % 2], 16)

                pool.wait_ge(step_rows_full, (half + 1) * 16)
                pool.sem_inc(pool_waited, 1)
                load_mats(0)
                load_mats(1)
                for j in range(2, 8):
                    pool.wait_ge(y_full, half * 8 + j - 1)
                    pool.sem_inc(pool_waited, 1)
                    load_mats(j)
                pool.wait_ge(g_ready, (half + 1) * 8)
                pool.sem_inc(pool_waited, 1)
                pool.dma_start(rope_sb, rope[half]).then_inc(rope_loaded, 16)
                pool.wait_ge(ys_ready, (half + 1) * 2)
                pool.sem_inc(pool_waited, 1)
                pool.dma_start(area(R3 + 2048, 1024), dmat).then_inc(tables_loaded, 16)
                pool.dma_start(zeta_sb, zeta).then_inc(tables_loaded, 16)
                pool.dma_start(xi_sb, xi).then_inc(tables_loaded, 16)
                for t in range(BLOCKS):
                    for par in range(2):
                        n = half * 2 * BLOCKS + 2 * t + par
                        pool.wait_ge(o_inverse, n + 1)
                        pool.sem_inc(pool_waited, 1)
                        pool.tensor_tensor(o_t[t % 2][:, par], o_t[t % 2][:, par], o_sq[:, par], ALU.mult).then_inc(o_scaled, 1)
                        pool.wait_ge(o_scaled, n + 1)
                        pool.sem_inc(pool_waited, 1)
                        dst = z_r[:, par::2, BLOCK * t:BLOCK * t + BLOCK]
                        pool.tensor_tensor(dst, dst, o_t[t % 2][:, par], ALU.mult).then_inc(z_scaled, 1)
                pool.wait_ge(z_scaled, (half + 1) * BLOCKS * 2)
                pool.sem_inc(pool_waited, 1)
                for i in range(2):
                    pool.dma_start(x_rows[:, i, :], x[half * 4 + i]).then_inc(x_loaded, 16)
                pool.wait_ge(yr_ready, (half + 1) * 2)
                pool.sem_inc(pool_waited, 1)
                pool.dma_start(gain_row, gain_out).then_inc(gain_row_loaded, 16)
                pool.wait_ge(m_added, (half + 1) * 16)
                pool.sem_inc(pool_waited, 1)
                for i in range(2):
                    pool.dma_start(x_rows_2[:, i, :], x[half * 4 + 2 + i]).then_inc(x_loaded, 16)
                for i in range(4):
                    pool.wait_ge(out_ready, half * 4 + i + 1 + START)
                    pool.sem_inc(pool_waited, 1)
                    pool.dma_start(out[half * 4 + i], o_row[:, i, :]).then_inc(out_stored, 16)
                pool.wait_ge(out_stored, (half + 1) * 4 * 16)
                pool.sem_inc(rows_free, 1)
            pool.wait_ge(out_stored, PASSES * 4 * 16)

        @block.scalar
        def _(act):
            for dst, src in ((lam_r, lam_re), (lam_i, lam_im), (step_sb, log_step)):
                act.dma_start(dst, src).then_inc(rates_loaded, 16)
            for dst, src in ((sign_sb[:, :], signs), (bb_p, b_ri), (bb_q, b_ir), (cc_p, c_ri), (cc_q, c_ir), (d_sb, d_rep)):
                act.dma_start(dst.rearrange("p g h -> p (g h)") if dst.ndim == 3 else dst, src
                              ).then_inc(params_loaded, 16)
            act.sem_inc(square_added, SLOTS)
            with act.Fori(0, PASSES * KT_IN // SLOTS) as i:
                for s in range(SLOTS):
                    act.wait_ge(sq_loaded[s], i * 16 + 16)
                    act.wait_ge(square_added, i * SLOTS + s + 1)
                    nc.scalar.activation(plain("w_lo", COLS * s, COLS), raw[:, s, :], ACT.Square).then_inc(squared, 1)
            act.wait_ge(consts_loaded, CONSTS * 16)
            act.wait_ge(square_added, PASSES * KT_IN + SLOTS)
            act.wait_ge(eps_ready, 1)
            for p in range(PASSES):
                nc.scalar.activation(rstd_stage[:, TOK * p:TOK * p + TOK], psum[:, 6 + p, :], ACT.Sqrt,
                                     scale=1.0 / D_MODEL, bias=eps_sb[:, 0:1]).then_inc(std_ready, 1)
            for n in range(16):
                act.wait_ge(m2_full, n + 1)
                nc.scalar.activation(m2_stage[:, COLS * n:COLS * n + COLS], psum[:, 2 + n % 4, :],
                                     ACT.Copy).then_inc(m2_copied, 1)
                if n % 2:
                    act.wait_ge(m2_copied, n + 1)
                    act.dma_start(mats[1, n // 2], m2_stage[:, 512 * n - 512:512 * n + 512]).then_inc(m2_stored, 16)
            act.wait_ge(rstd_ready, 1)
            act.dma_start(rstd.rearrange("a p n -> p a n"), rstd_stage.rearrange("p (a n) -> p a n", a=PASSES)
                          ).then_inc(rstd_stored, 16)
            m1_banks(act, nc.scalar, 0)
            act.wait_ge(m1_act, 8)
            act.wait_ge(m1_dve, 8)
            for j in range(8):
                act.dma_start(mats[0, j], area(1024 * j, 1024)).then_inc(m1_stored, 16)

            with act.Fori(0, PASSES) as half:
                def heads(q):
                    for s in range(SLOTS):
                        head(q, s)

                def head(q, s):
                    act.wait_ge(raw_loaded[s], (half * QUADS + q + 1) * 16)
                    act.wait_ge(unit_multiplied, (half * QUADS + q) * SLOTS + s + 1)
                    nc.scalar.activation(w_hi[:, s, :], raw[:, s, :], ACT.Copy).then_inc(head_split, 1)

                def multiplied(q):
                    act.wait_ge(unit_multiplied, (half * QUADS + q) * SLOTS + SLOTS)

                for k in range(KT_IN):
                    act.wait_ge(h_scaled, half * KT_IN + k + 1 + SLOTS)
                    if k == 0:
                        multiplied(0)
                    nc.scalar.activation(h_hi[:, k, :], tmp[:, k % 2, :], ACT.Copy).then_inc(h_head, 1)
                    head(Q_U + k // 4, k % 4)
                heads(Q_U + 4)
                multiplied(Q_U + 4)
                act.wait_ge(m1_stored, 8 * 16)
                act.wait_ge(m2_stored, 8 * 16)
                act.wait_ge(rows_free, half + START)
                for n in range(4):
                    nc.scalar.activation(u_tok[:, 0:32, n, :], psum[:, n, :].rearrange("p (g h) -> p g h", h=GROUP),
                                         ACT.Copy).then_inc(set_a_emptied, 1)
                for q in range(5, 8):
                    heads(Q_U + q)
                heads(Q_ZS)
                multiplied(Q_ZS)
                for n in range(4):
                    nc.scalar.activation(u_tok[:, 32:64, n, :], psum[:, 4 + n, :].rearrange("p (g h) -> p g h", h=GROUP),
                                         ACT.Copy).then_inc(set_b_emptied, 1)
                step_rows(act, nc.scalar, half, 0)
                state_inputs(act, nc.scalar, half, 0)
                for q in range(1, 4):
                    heads(Q_ZS + q)
                heads(Q_ZS + 4)
                multiplied(Q_ZS + 4)
                for n in range(4):
                    nc.scalar.activation(z_s[:, n, :], psum[:, n, :], ACT.Silu).then_inc(set_a_emptied, 1)
                for q in range(5, 8):
                    heads(Q_ZS + q)
                heads(Q_GLU)
                multiplied(Q_GLU)
                for n in range(4):
                    nc.scalar.activation(z_s[:, 4 + n, :], psum[:, 4 + n, :], ACT.Silu).then_inc(set_b_emptied, 1)
                act.wait_ge(scan_done, (half + 1) * SCAN + START)
                shift_states(act, nc.scalar, half, 0, 1)
                for j in range(8):
                    if j + 1 < 8 and j == 0:
                        shift_states(act, nc.scalar, half, 1, 1)
                    if j:
                        act.wait_ge(y_turned, half * 8 + j)
                    act.wait_ge(y_full, half * 8 + j + 1)
                    y_rows(nc.scalar, j, 0).then_inc(y_row_act, 1)
                    if j + 2 < 8:
                        shift_states(act, nc.scalar, half, j + 2, 1)
                    act.wait_ge(y_turned, half * 8 + j + 1)
                    if j >= 2:
                        act.wait_ge(g_ready, half * 8 + j - 1)
                    nc.scalar.activation(tmp[:, j % 2, :].rearrange("p (c t) -> p t c", t=STEP),
                                         psum[:, 4 + j % 2, :].rearrange("p (t c) -> p t c", t=STEP),
                                         ACT.Gelu_apprx_tanh).then_inc(gelu_done, 1)
                    act.wait_ge(gelu_done, half * 8 + j + 1)
                    nc.scalar.activation(y_hi[:, j, :], tmp[:, j % 2, :], ACT.Copy).then_inc(g_head, 1)
                heads(Q_GLU + 1)
                heads(Q_GLU + 2)
                multiplied(Q_GLU + 2)
                for n in range(4):
                    nc.scalar.activation(gate[:, n, :], psum[:, n, :], ACT.Sigmoid,
                                         bias=bglu_sb[:, n:n + 1]).then_inc(set_a_emptied, 1)
                heads(Q_GLU + 3)
                heads(Q_Q)
                multiplied(Q_Q)
                act.wait_ge(glu_step, half * 24 + 12)
                for n in range(4):
                    nc.scalar.activation(gate[:, n, :], psum[:, 4 + n, :], ACT.Sigmoid,
                                         bias=bglu_sb[:, 4 + n:5 + n]).then_inc(set_b_emptied, 1)
                heads(Q_Q + 1)
                act.wait_ge(glu_step, (half + 1) * 24)
                for n in range(2):
                    nc.scalar.activation(y_hi[:, 4 * n:4 * n + 4, :], z_s[:, 4 * n:4 * n + 4, :],
                                         ACT.Copy).then_inc(ys_head, 1)
                for q in range(2, 4):
                    heads(Q_Q + q)
                for q in range(4):
                    heads(Q_K + q)
                for q in range(8):
                    heads(Q_V + q)
                for q in range(4):
                    heads(Q_ZR + q)
                heads(Q_ZR + 4)
                multiplied(Q_ZR + 4)
                act.wait_ge(rope_done, (half + 1) * 32)
                for n in range(4):
                    nc.scalar.activation(z_r[:, n, :], psum[:, n, :], ACT.Silu).then_inc(set_a_emptied, 1)
                for q in range(5, 8):
                    heads(Q_ZR + q)
                heads(Q_S)
                multiplied(Q_S)
                for n in range(4):
                    nc.scalar.activation(z_r[:, 4 + n, :], psum[:, 4 + n, :], ACT.Silu).then_inc(set_b_emptied, 1)
                for t in range(BLOCKS):
                    before = half * 2 * BLOCKS + 2 * t
                    for par in range(2):
                        act.wait_ge(o_full, before + par + 1)
                        if t >= 2 and par == 0:
                            act.wait_ge(z_scaled, before - 2)
                        nc.scalar.activation(o_t[t % 2][:, par], psum[:, 3 + par, :].rearrange("p (a n) -> p a n", a=4),
                                             ACT.Copy).then_inc(o_copied, 1)
                    for par in range(2):
                        act.wait_ge(o_copied, before + par + 1)
                        if t:
                            act.wait_ge(o_scaled, before - 1 + par)
                        nc.scalar.activation(o_sq[:, par], o_t[t % 2][:, par], ACT.Square).then_inc(o_squared, 1)
                    for par in range(2):
                        act.wait_ge(osum_full, before + par + 1)
                        nc.scalar.activation(o_sq[:, par], psum[:, 6 + par, :].rearrange("p (a n) -> p a n", a=4),
                                             ACT.Sqrt, scale=1.0 / V_HEAD, bias=eps_sb[:, 0:1]).then_inc(ostd_ready, 1)
                act.wait_ge(kv_full, (half + 1) * BLOCKS)
                with act.Fori(0, MERGES) as b:
                    q0 = Q_S + b * Q_MERGE
                    for q in range(1, 5):
                        heads(q0 + q)
                    multiplied(q0 + 4)
                    act.wait_ge(set_b_emptied, (half * BLOCKS_SET + B_S + b) * 4 + START)
                    for n in range(4):
                        nc.scalar.activation(gate[:, n, :], psum[:, n, :], ACT.Sigmoid).then_inc(set_a_emptied, 1)
                    heads(q0 + 5)
                    heads(q0 + 6)
                multiplied(Q_R)
                act.wait_ge(z_scaled, (half + 1) * BLOCKS * 2)
                for n in range(2):
                    nc.scalar.activation(y_hi[:, 4 * n:4 * n + 4, :], z_r[:, 4 * n:4 * n + 4, :],
                                         ACT.Copy).then_inc(yr_head, 1)
                def merge_gates(b):
                    q0 = Q_R + b * Q_MERGE
                    for q in range(1, 5):
                        heads(q0 + q)
                    multiplied(q0 + 4)
                    act.wait_ge(m_added, half * 16 + b * 4 + START)
                    for n in range(4):
                        nc.scalar.activation(gate[:, n, :], psum[:, n, :], ACT.Sigmoid).then_inc(set_a_emptied, 1)
                    heads(q0 + 5)

                def m_heads(n):
                    act.wait_ge(m_added, half * 16 + 4 * n + 4 + START)
                    nc.scalar.activation(h_hi[:, 4 * n:4 * n + 4, :], m_t[:, 4 * n:4 * n + 4, :],
                                         ACT.Copy).then_inc(m_head, 1)

                with act.Fori(0, MERGES - 1) as b:
                    merge_gates(b)
                    heads(Q_R + b * Q_MERGE + 6)
                merge_gates(MERGES - 1)
                for n in range(MERGES - 1):
                    m_heads(n)
                heads(Q_OUT)
                m_heads(MERGES - 1)
                for c in range(3):
                    for q in range(1, 5):
                        heads(Q_OUT + 4 * c + q)
                    multiplied(Q_OUT + 4 * c + 4)
                    first = 4 * (c % 2)
                    for i in range(4):
                        if c or i:
                            act.wait_ge(out_squared, half * 16 + 4 * c + i + START)
                        nc.scalar.activation(tmp[:, 0, :], psum[:, first + i, :], ACT.Square,
                                             accum_out=ssq[:, i, c:c + 1]).then_inc(out_squared, 1)
                for q in range(1, 4):
                    heads(Q_OUT + 12 + q)
                for i in range(4):
                    if i < 3:
                        act.wait_ge(row_block_full, half * 3 + i + 1)
                    else:
                        multiplied(QUADS)
                    act.wait_ge(out_squared, half * 16 + 12 + i + START)
                    nc.scalar.activation(tmp[:, 0, :], psum[:, 4 + i, :], ACT.Square,
                                         accum_out=ssq[:, i, 3:4]).then_inc(out_squared, 1)
                    act.wait_ge(out_stat, half * 8 + 2 * i + 1)
                    nc.scalar.activation(rstd_out[:, i:i + 1], rstd_out[:, i:i + 1], ACT.Sqrt, scale=1.0 / D_MODEL,
                                         bias=eps_sb[:, 0:1]).then_inc(out_std, 1)

        @block.vector
        def _(dve):
            V = nc.vector
            steps = [0]

            def then(ins):
                steps[0] += 1
                ins.then_inc(setup_step, 1)
                dve.wait_ge(setup_step, steps[0])

            def ts(dst, src, a, op, b=None, op2=ALU.bypass):
                if b is None:
                    then(V.tensor_scalar(dst, src, a, None, op))
                else:
                    then(V.tensor_scalar(dst, src, a, b, op, op2))

            def tt(dst, a, b, op):
                then(V.tensor_tensor(dst, a, b, op))

            MAGIC = 12582912.0

            def rint(dst, src):
                ts(dst, src, MAGIC, ALU.add)
                ts(dst, dst, -MAGIC, ALU.add)

            def poly(dst, z, coefs):
                ts(dst, z, coefs[0], ALU.mult, coefs[1], ALU.add)
                for c in coefs[2:]:
                    tt(dst, dst, z, ALU.mult)
                    ts(dst, dst, c, ALU.add)

            def exp(dst, arg, n, r, bits):
                ts(r, arg, 89.0, ALU.min, -110.0, ALU.max)
                ts(n, r, 1.0 / math.log(2.0), ALU.mult)
                rint(n, n)
                then(V.scalar_tensor_tensor(r, n, -0.693359375, r, ALU.mult, ALU.add))
                then(V.scalar_tensor_tensor(r, n, 2.12194440e-4, r, ALU.mult, ALU.add))
                poly(dst, r, [1 / 5040, 1 / 720, 1 / 120, 1 / 24, 1 / 6, 0.5, 1.0, 1.0])
                ts(n, n, 127.0, ALU.add, 0.0, ALU.max)
                ts(n, n, 255.0, ALU.min, 8388608.0, ALU.mult)
                then(V.tensor_copy(bits.bitcast(I32), n))
                tt(dst, dst, bits, ALU.mult)

            V.memset(eps_sb[:, :], EPS).then_inc(eps_ready, 1)
            then(V.memset(carry[:, :, :], 0.0))
            then(V.memset(ret_state[:, :, :], 0.0))
            dve.wait_ge(rates_loaded, 3 * 16)
            exp(s0, step_sb, s1, s2, s3)
            tt(s4, lam_r, s0, ALU.mult)
            exp(par_re, s4, s1, s2, s3)
            tt(s4, lam_i, s0, ALU.mult)
            ts(s1, s4, 2.0 / math.pi, ALU.mult)
            rint(s1, s1)
            half_pi = [1.5703125, 4.8351287841796875e-4, -3.1385570764541626e-7, 6.077100506506192e-11]
            then(V.scalar_tensor_tensor(s2, s1, -half_pi[0], s4, ALU.mult, ALU.add))
            for c in half_pi[1:]:
                then(V.scalar_tensor_tensor(s2, s1, -c, s2, ALU.mult, ALU.add))
            ts(s3, s1, 0.25, ALU.mult, -0.375, ALU.add)
            rint(s3, s3)
            then(V.scalar_tensor_tensor(s1, s3, -4.0, s1, ALU.mult, ALU.add))
            tt(s5, s2, s2, ALU.mult)
            poly(s6, s5, [2.7557319e-6, -1.98412698e-4, 8.33333333e-3, -1.66666667e-1, 1.0])
            tt(s6, s6, s2, ALU.mult)
            poly(s7, s5, [2.48015873e-5, -1.38888889e-3, 4.16666667e-2, -0.5, 1.0])
            ts(s3, s1, 1.0, ALU.is_equal)
            ts(s4, s1, 3.0, ALU.is_equal)
            tt(s3, s3, s4, ALU.add)
            ts(s4, s3, -1.0, ALU.mult, 1.0, ALU.add)
            tt(s8, s6, s4, ALU.mult)
            tt(s9, s7, s3, ALU.mult)
            tt(s8, s8, s9, ALU.add)
            tt(s7, s7, s4, ALU.mult)
            tt(s6, s6, s3, ALU.mult)
            tt(s7, s7, s6, ALU.add)
            ts(s3, s1, 2.0, ALU.is_ge, -2.0, ALU.mult)
            ts(s3, s3, 1.0, ALU.add)
            tt(s8, s8, s3, ALU.mult)
            ts(s3, s1, 1.0, ALU.is_equal)
            ts(s4, s1, 2.0, ALU.is_equal)
            tt(s3, s3, s4, ALU.add)
            ts(s3, s3, -2.0, ALU.mult, 1.0, ALU.add)
            tt(s7, s7, s3, ALU.mult)
            then(V.memset(pow_re[:, 0, :], 1.0))
            then(V.memset(pow_im[:, 0, :], 0.0))
            tt(pow_im[:, 1, :], par_re, s8, ALU.mult)
            tt(pow_re[:, 1, :], par_re, s7, ALU.mult)
            for j in range(2, 9):
                a, b = j // 2, j - j // 2
                tt(s1, pow_re[:, a, :], pow_re[:, b, :], ALU.mult)
                tt(s2, pow_im[:, a, :], pow_im[:, b, :], ALU.mult)
                tt(pow_re[:, j, :], s1, s2, ALU.subtract)
                tt(s1, pow_re[:, a, :], pow_im[:, b, :], ALU.mult)
                tt(s2, pow_im[:, a, :], pow_re[:, b, :], ALU.mult)
                tt(pow_im[:, j, :], s1, s2, ALU.add)
            dve.wait_ge(params_loaded, 6 * 16)
            V.tensor_scalar(cc_p, cc_p, sign_sb[:, 0:1], None, ALU.mult).then_inc(powers_ready, 1)
            tt(s1, lam_r, lam_r, ALU.mult)
            tt(s2, lam_i, lam_i, ALU.mult)
            tt(s1, s1, s2, ALU.add)
            then(V.reciprocal(s1, s1))
            ts(s0, pow_re[:, 1, :], -1.0, ALU.add)
            tt(s2, s0, lam_r, ALU.mult)
            tt(s3, pow_im[:, 1, :], lam_i, ALU.mult)
            tt(s2, s2, s3, ALU.add)
            tt(par_re, s2, s1, ALU.mult)
            tt(s2, pow_im[:, 1, :], lam_r, ALU.mult)
            tt(s3, s0, lam_i, ALU.mult)
            tt(s2, s2, s3, ALU.subtract)
            tt(par_im, s2, s1, ALU.mult)

            def by_group(a):
                return a.unsqueeze(2).broadcast_to([P, GROUPS, GROUP])

            then(V.tensor_scalar(bb_q, bb_q, sign_sb[:, 1:2], None, ALU.mult))
            tt(b_tmp, bb_p, by_group(par_im), ALU.mult)
            tt(bb_p, bb_p, by_group(par_re), ALU.mult)
            tt(b_tmp2, bb_q, by_group(par_im), ALU.mult)
            tt(bb_p, bb_p, b_tmp2, ALU.add)
            tt(bb_q, bb_q, by_group(par_re), ALU.mult)
            tt(bb_q, bb_q, b_tmp, ALU.subtract)
            for par in range(2):
                half_rows = slice(64 * par, 64 * par + 64)
                for r in range(2):
                    then(V.tensor_copy(scan_re[half_rows, r, :], pow_re[half_rows, 8, par::2]))
                    ts(scan_im[half_rows, r, :], pow_im[half_rows, 8, par::2], 1.0 if r else -1.0, ALU.mult)
            for part in range(4):
                gs = slice(16 * part, 16 * part + 16)

                def powers(a):
                    return a[:, 0:8, gs][:, ::-1, :].rearrange("p i g -> p g i").unsqueeze(3).broadcast_to([P, 16, STEP, GROUP])

                def coefs(a):
                    return a[:, gs, :].unsqueeze(2).broadcast_to([P, 16, STEP, GROUP])

                tt(window[:, gs], coefs(bb_p), powers(pow_re), ALU.mult)
                tt(win_tmp, coefs(bb_q), powers(pow_im), ALU.mult)
                V.tensor_tensor(window[:, gs], window[:, gs], win_tmp, ALU.add).then_inc(window_ready, 1)
                dve.wait_ge(window_ready, part + 1)
            dve.wait_ge(std_ready, 2)
            V.reciprocal(rstd_stage, rstd_stage).then_inc(rstd_ready, 1)
            dve.wait_ge(consts_loaded, CONSTS * 16)
            lags_3d = lags.rearrange("p (g h) -> p g h", h=GROUP)
            tt(lags_3d, ident[:, P - GROUP:P].unsqueeze(1).broadcast_to([P, GROUPS, GROUP]),
               d_sb.unsqueeze(2).broadcast_to([P, GROUPS, GROUP]), ALU.mult)
            dve.wait_ge(lags_full, 1)
            V.tensor_tensor(lags, lags, psum[:, 0:2, :].rearrange("p b n -> p (b n)"), ALU.add).then_inc(lags_ready, 1)
            m1_banks(dve, V, 1)

            with dve.Fori(0, PASSES) as half:
                def rests(q):
                    for s in range(SLOTS):
                        rest(q, s)

                def rest(q, s):
                    dve.wait_ge(head_split, (half * QUADS + q) * SLOTS + s + 1)
                    V.tensor_tensor(w_lo[:, s, :], raw[:, s, :], w_hi[:, s, :].bitcast(F32),
                                    ALU.subtract).then_inc(rest_split, 1)

                def multiplied(q):
                    dve.wait_ge(unit_multiplied, (half * QUADS + q) * SLOTS + SLOTS)

                def scan_step(c):
                    now = half * SCAN + c * 5 + 1 + START
                    dve.wait_ge(scan_done, now)
                    V.tensor_tensor(scan_t[:, 0], state[:, c], scan_re[:, :, :], ALU.mult).then_inc(scan_done, 1)
                    for r in range(2):
                        V.tensor_tensor(scan_t[:, 1, r, :], state[:, c, 1 - r, :], scan_im[:, r, :],
                                        ALU.mult).then_inc(scan_done, 1)
                    dve.wait_ge(scan_done, now + 1)
                    V.tensor_tensor(state[:, c + 1], state[:, c + 1], scan_t[:, 0], ALU.add).then_inc(scan_done, 1)
                    dve.wait_ge(scan_done, now + 4)
                    V.tensor_tensor(state[:, c + 1], state[:, c + 1], scan_t[:, 1], ALU.add).then_inc(scan_done, 1)

                def scale_h(k):
                    dve.wait_ge(xt_loaded[k % 4], (half * 4 + k // 4 + 1) * 16)
                    if k >= 2:
                        dve.wait_ge(h_ready, half * KT_IN + k - 1)
                    else:
                        dve.wait_ge(rstd_loaded, (half + 1) * 16)
                    V.scalar_tensor_tensor(tmp[:, k % 2, :], xt_ring[:, k % 4, :], gain_sb[:, k:k + 1],
                                           rstd_in, ALU.mult, ALU.mult).then_inc(h_scaled, 1)

                scale_h(0)
                for k in range(KT_IN):
                    if k + 1 < KT_IN:
                        scale_h(k + 1)
                    dve.wait_ge(h_head, half * KT_IN + k + 1)
                    V.tensor_tensor(h_lo[:, k, :], tmp[:, k % 2, :], h_hi[:, k, :].bitcast(F32),
                                    ALU.subtract).then_inc(h_ready, 1)
                    rest(Q_U + k // 4, k % 4)
                for q in range(4, 8):
                    rests(Q_U + q)
                rests(Q_ZS)
                step_rows(dve, V, half, 1)
                state_inputs(dve, V, half, 1)
                dve.wait_ge(state_in_act, (half + 1) * 16)
                dve.wait_ge(state_in_dve, (half + 1) * 16)
                V.tensor_copy(state[:, 0], carry[:, :, :]).then_inc(scan_done, 1)
                with dve.Fori(0, 8) as i:
                    for s in range(SLOTS):
                        rest(Q_ZS + 1 + i, s)
                        scan_step(i * 8 + 2 * s)
                        scan_step(i * 8 + 2 * s + 1)
                dve.wait_ge(scan_done, half * SCAN + 5 * STEPS + 1 + START)
                V.tensor_copy(carry[:, :, :], state[:, STEPS]).then_inc(scan_done, 1)
                shift_states(dve, V, half, 0, 0)
                shift_states(dve, V, half, 1, 0)
                for j in range(8):
                    if j:
                        dve.wait_ge(y_turned, half * 8 + j)
                    dve.wait_ge(y_full, half * 8 + j + 1)
                    y_rows(V, j, 1).then_inc(y_row_dve, 1)
                    if j + 2 < 8:
                        shift_states(dve, V, half, j + 2, 0)
                    dve.wait_ge(g_head, half * 8 + j + 1)
                    V.tensor_tensor(y_lo[:, j, :], tmp[:, j % 2, :], y_hi[:, j, :].bitcast(F32),
                                    ALU.subtract).then_inc(g_ready, 1)
                rests(Q_GLU + 1)

                def glu(b):
                    emptied = set_b_emptied if b else set_a_emptied
                    base = half * 24 + 12 * b
                    for n in range(4):
                        k = 4 * b + n
                        dve.wait_ge(emptied, (half * BLOCKS_SET + B_GLU) * 4 + n + 1 + START)
                        if n or b:
                            dve.wait_ge(glu_step, base + 3 * n)
                        V.tensor_tensor(tmp[:, 0, :], y_hi[:, k, :].bitcast(F32), y_lo[:, k, :].bitcast(F32),
                                        ALU.add).then_inc(glu_step, 1)
                        dve.wait_ge(glu_step, base + 3 * n + 1)
                        V.tensor_tensor(tmp[:, 0, :], tmp[:, 0, :], gate[:, n, :], ALU.mult).then_inc(glu_step, 1)
                        dve.wait_ge(glu_step, base + 3 * n + 2)
                        V.tensor_tensor(z_s[:, k, :], z_s[:, k, :], tmp[:, 0, :], ALU.mult).then_inc(glu_step, 1)

                rests(Q_GLU + 2)
                glu(0)
                rests(Q_GLU + 3)
                rests(Q_Q)
                multiplied(Q_Q)
                glu(1)
                rests(Q_Q + 1)
                for n in range(2):
                    dve.wait_ge(ys_head, half * 2 + n + 1)
                    V.tensor_tensor(y_lo[:, 4 * n:4 * n + 4, :], z_s[:, 4 * n:4 * n + 4, :],
                                    y_hi[:, 4 * n:4 * n + 4, :].bitcast(F32), ALU.subtract).then_inc(ys_ready, 1)
                for q in range(2, 4):
                    rests(Q_Q + q)

                def rotate(dst, b, emptied, first, j):
                    dve.wait_ge(rope_loaded, (half + 1) * 16)
                    base = half * 32 + 16 * b + 8 * j
                    if j or b:
                        dve.wait_ge(rope_done, base)
                    cos, sin = rope_sb[:, 0, :], rope_sb[:, 1, :]
                    one, two = psum[:, first + j, :], psum[:, first + 2 + j, :]
                    V.tensor_tensor(gate[:, 0, :], one, cos, ALU.mult).then_inc(rope_step, 1)
                    V.tensor_tensor(gate[:, 1, :], two, sin, ALU.mult).then_inc(rope_step, 1)
                    V.tensor_tensor(gate[:, 2, :], one, sin, ALU.mult).then_inc(emptied, 1)
                    V.tensor_tensor(gate[:, 3, :], two, cos, ALU.mult).then_inc(emptied, 1)
                    dve.wait_ge(rope_step, half * 8 + 4 * b + 2 * j + 2)
                    dve.wait_ge(emptied, (half * BLOCKS_SET + B_QK) * 4 + 2 * j + 2 + START)
                    for hh in range(4):
                        pair, par = (4 * j + hh) // 2, hh % 2
                        rows = slice(32 * hh, 32 * hh + 32)
                        V.tensor_tensor(dst[64 * par:64 * par + 32, pair, :], gate[rows, 0, :], gate[rows, 1, :],
                                        ALU.subtract).then_inc(rope_done, 1)
                        V.tensor_tensor(dst[64 * par + 32:64 * par + 64, pair, :], gate[rows, 2, :], gate[rows, 3, :],
                                        ALU.add).then_inc(rope_done, 1)

                rests(Q_K)
                multiplied(Q_K)
                for j in range(2):
                    rotate(q_t, 0, set_a_emptied, 0, j)
                    rests(Q_K + 1 + j)
                rests(Q_K + 3)
                rests(Q_V)
                multiplied(Q_V)
                for j in range(2):
                    rotate(k_t, 1, set_b_emptied, 4, j)
                    rests(Q_V + 1 + j)
                rests(Q_V + 3)
                rests(Q_V + 4)
                multiplied(Q_V + 4)
                for i in range(4):
                    V.tensor_copy(v_row[:, i, 0:512], psum[:, i, :]).then_inc(set_a_emptied, 1)
                for q in range(5, 8):
                    rests(Q_V + q)
                rests(Q_ZR)
                multiplied(Q_ZR)
                for i in range(4):
                    V.tensor_copy(v_row[:, i, 512:1024], psum[:, 4 + i, :]).then_inc(set_b_emptied, 1)
                for q in range(1, 8):
                    rests(Q_ZR + q)
                rests(Q_S)
                dve.wait_ge(tables_loaded, (half + 1) * 3 * 16)
                dve.wait_ge(rope_done, (half + 1) * 32)
                dve.wait_ge(set_a_emptied, (half * BLOCKS_SET + B_ZR + 1) * 4 + START)
                dve.wait_ge(set_b_emptied, (half * BLOCKS_SET + B_ZR + 1) * 4 + START)

                def inverse(t):
                    for par in range(2):
                        dve.wait_ge(ostd_ready, half * 2 * BLOCKS + 2 * t + par + 1)
                        V.reciprocal(o_sq[:, par], o_sq[:, par]).then_inc(o_inverse, 1)

                for t in range(BLOCKS):
                    n = half * BLOCKS + t
                    tok = slice(BLOCK * t, BLOCK * t + BLOCK)
                    if t:
                        dve.wait_ge(o_full, 2 * n)
                    V.tensor_tensor(q_xi, q_t[:, :, tok], xi_sb.rearrange("p (a n) -> p a n", a=4),
                                    ALU.mult).then_inc(q_xi_ready, 1)
                    for par in range(2):
                        dve.wait_ge(scores_full, 2 * n + par + 1)
                        V.tensor_tensor(s_dec[:, par, :], psum[:, 1 + par, :], dmat_sb[:, par, :],
                                        ALU.mult).then_inc(scores_decayed, 1)
                    dve.wait_ge(k_turned, n + 1)
                    if t:
                        dve.wait_ge(kv_full, n)
                    V.tensor_tensor(k_zeta, psum[:, 0, :], zeta_sb, ALU.mult).then_inc(k_zeta_ready, 1)
                    if t:
                        inverse(t - 1)
                    dve.wait_ge(kv_full, n + 1)
                    for a in range(4):
                        V.scalar_tensor_tensor(ret_state[:, a, :], ret_state[:, a, :], gdec_sb[:, a:a + 1],
                                               psum[:, 5, 128 * a:128 * a + 128], ALU.mult, ALU.add
                                               ).then_inc(state_ready, 1)
                inverse(BLOCKS - 1)
                with dve.Fori(0, MERGES) as b:
                    q0 = Q_S + b * Q_MERGE
                    for q in range(1, 7):
                        rests(q0 + q)
                    multiplied(q0 + 6)
                    dve.wait_ge(set_a_emptied, (half * BLOCKS_SET + B_S + 1 + b) * 4 + START)
                    for n in range(4):
                        V.tensor_tensor(m_t[:, b * 4 + n, :], gate[:, n, :], psum[:, 4 + n, :],
                                        ALU.mult).then_inc(set_b_emptied, 1)
                for n in range(2):
                    dve.wait_ge(yr_head, half * 2 + n + 1)
                    V.tensor_tensor(y_lo[:, 4 * n:4 * n + 4, :], z_r[:, 4 * n:4 * n + 4, :],
                                    y_hi[:, 4 * n:4 * n + 4, :].bitcast(F32), ALU.subtract).then_inc(yr_ready, 1)
                def m_rests(n):
                    dve.wait_ge(m_head, half * 4 + n + 1)
                    V.tensor_tensor(h_lo[:, 4 * n:4 * n + 4, :], m_t[:, 4 * n:4 * n + 4, :],
                                    h_hi[:, 4 * n:4 * n + 4, :].bitcast(F32), ALU.subtract).then_inc(m_ready, 1)

                def merge_sums(b):
                    multiplied(Q_R + b * Q_MERGE + 6)
                    dve.wait_ge(set_a_emptied, (half * BLOCKS_SET + B_R + 1 + b) * 4 + START)
                    for n in range(4):
                        V.tensor_tensor(gate[:, n, :], gate[:, n, :], psum[:, 4 + n, :],
                                        ALU.mult).then_inc(set_b_emptied, 1)
                    for n in range(4):
                        dve.wait_ge(set_b_emptied, (half * BLOCKS_SET + B_R + b) * 4 + n + 1 + START)
                        V.tensor_tensor(m_t[:, b * 4 + n, :], m_t[:, b * 4 + n, :], gate[:, n, :],
                                        ALU.add).then_inc(m_added, 1)

                with dve.Fori(0, MERGES - 1) as b:
                    for q in range(1, 7):
                        rests(Q_R + b * Q_MERGE + q)
                    merge_sums(b)
                for q in range(1, 6):
                    rests(Q_R + (MERGES - 1) * Q_MERGE + q)
                for n in range(MERGES - 1):
                    m_rests(n)
                rests(Q_OUT)
                merge_sums(MERGES - 1)
                rests(Q_OUT + 1)
                m_rests(MERGES - 1)
                dve.wait_ge(m_ready, (half + 1) * 4)
                dve.wait_ge(gain_row_loaded, (half + 1) * 16)

                def gained(c, i, emptied):
                    dve.wait_ge(out_squared, half * 16 + 4 * c + i + 1 + START)
                    cols = slice(COLS * c, COLS * c + COLS)
                    V.tensor_tensor(o_row[:, i, cols], psum[:, 4 * (c % 2) + i, :], gain_row[:, cols],
                                    ALU.mult).then_inc(emptied, 1)

                for c in range(3):
                    for q in range(2 if c == 0 else 1, 5):
                        rests(Q_OUT + 4 * c + q)
                    multiplied(Q_OUT + 4 * c + 4)
                    for i in range(4):
                        gained(c, i, set_b_emptied if c % 2 else set_a_emptied)
                for q in range(1, 4):
                    rests(Q_OUT + 12 + q)
                dve.wait_ge(x_loaded, (half + 1) * 4 * 16)

                def finish(i):
                    dve.wait_ge(out_std, half * 4 + i + 1)
                    V.reciprocal(rstd_out[:, i:i + 1], rstd_out[:, i:i + 1]).then_inc(out_stat, 1)
                    dve.wait_ge(out_stat, half * 8 + 2 * i + 2)
                    dve.wait_ge(set_b_emptied, (half * BLOCKS_SET + B_OUT + 1) * 4 + i + 1 + START)
                    V.scalar_tensor_tensor(o_row[:, i, :], o_row[:, i, :], rstd_out[:, i:i + 1],
                                           x_rows[:, i, :] if i < 2 else x_rows_2[:, i - 2, :],
                                           ALU.mult, ALU.add).then_inc(out_ready, 1)

                for i in range(4):
                    dve.wait_ge(out_squared, half * 16 + 12 + i + 1 + START)
                    V.tensor_reduce(rstd_out[:, i:i + 1], ssq[:, i, :], AX_X, ALU.add).then_inc(out_stat, 1)
                    gained(3, i, set_b_emptied)
                    finish(i)

        @block.tensor
        def _(pe):
            T = nc.tensor
            pe.sem_inc(unit_multiplied, SLOTS)
            pe.wait_ge(consts_loaded, CONSTS * 16)
            for n in range(PASSES * KT_IN):
                pe.wait_ge(squared, n + 1 + SLOTS)
                T.matmul(psum[:, 6 + n // KT_IN, :], ones_sb[:, :], plain("w_lo", COLS * (n % SLOTS), COLS),
                         start=(n % KT_IN == 0), stop=(n % KT_IN == KT_IN - 1)).then_inc(square_added, 1)
            for b in range(16):
                if b % 4 == 0:
                    pe.wait_ge(window_ready, b // 4 + 1)
                if b >= 4:
                    pe.wait_ge(m2_copied, b - 3)
                for a in range(4):
                    g = 4 * b + a
                    w = window[:, g].rearrange("p i h -> p (i h)")
                    m2 = T.transpose(psum[:, 2 + b % 4, 128 * a:128 * a + 128], w, ident)
                    lag = T.matmul(psum[:, g // 32, GROUP * (g % 32):GROUP * (g % 32) + GROUP], w, cc_p[:, g, :],
                                   start=True, stop=True)
                    if a == 3:
                        m2.then_inc(m2_full, 1)
            lag.then_inc(lags_full, 1)
            pe.wait_ge(lags_ready, 1)
            for n in range(16):
                t = n // 2
                if n >= 8:
                    pe.wait_ge(m1_dve if n % 2 else m1_act, (n - 8) // 2 + 1)
                elif 2 <= n < 6:
                    pe.wait_ge(m2_copied, 16)
                elif n >= 6:
                    pe.wait_ge(std_ready, 2)
                move = GROUP * (STEP - 1 - t)
                T.matmul(psum[:, n % 8, :], eye_sb[:, move:move + P], lags[:, COLS * (n % 2):COLS * (n % 2) + COLS],
                         start=True, stop=True).then_inc(m1_full, 1)
            pe.wait_ge(m1_act, 8)
            pe.wait_ge(m1_dve, 8)

            with pe.Fori(0, PASSES) as half:
                def unit_ready(q, s):
                    pe.wait_ge(rest_split, (half * QUADS + q) * SLOTS + s + 1 + SLOTS)

                def columns_out(q, first, x_hi, x_lo, tiles, ready=None):
                    for k in range(tiles):
                        if ready is not None:
                            ready(k)
                        s = k % SLOTS
                        unit_ready(q + k // SLOTS, s)
                        for n in range(4):
                            cols = slice(P * n, P * n + P)
                            bank = psum[:, first + n, :]
                            T.matmul(bank, w_hi[:, s, cols], x_hi[:, k, :], start=(k == 0), stop=False)
                            T.matmul(bank, w_lo[:, s, cols], x_hi[:, k, :], start=False, stop=False)
                            last = T.matmul(bank, w_hi[:, s, cols], x_lo[:, k, :], start=False, stop=(k == tiles - 1))
                        last.then_inc(unit_multiplied, 1)

                def rows_out(q, first, x_hi, x_lo, pick, ready=None, tiles=KT_IN):
                    for k in range(tiles):
                        if ready is not None:
                            ready(k)
                        s = k % SLOTS
                        unit_ready(q + k // SLOTS, s)
                        for n in range(4):
                            bank = psum[:, first + n, :]
                            T.matmul(bank, pick(x_hi, k, n), w_hi[:, s, :], start=(k == 0), stop=False)
                            T.matmul(bank, pick(x_hi, k, n), w_lo[:, s, :], start=False, stop=False)
                            last = T.matmul(bank, pick(x_lo, k, n), w_hi[:, s, :], start=False, stop=(k == KT_IN - 1))
                        last.then_inc(unit_multiplied, 1)

                def empty(which, b):
                    pe.wait_ge(which, (half * BLOCKS_SET + b) * 4 + START)

                def step_tokens(a, k, n):
                    return a[:, k, n::4]

                def block_tokens(a, k, n):
                    return a[:, k, P * n:P * n + P]

                empty(set_a_emptied, 0)
                rows_out(Q_U, 0, h_hi, h_lo, step_tokens, lambda k: pe.wait_ge(h_ready, half * KT_IN + k + 1))
                rows_out(Q_U + 4, 4, h_hi, h_lo, step_tokens)
                empty(set_a_emptied, B_U + 1)
                empty(set_b_emptied, B_U + 1)
                for r in range(16):
                    if r >= 8:
                        done = step_rows_dve if r % 2 else step_rows_act
                        pe.wait_ge(done, half * 16 + 2 * ((r - 8) // 2 + 1))
                    pe.sem_inc(pe_waited, 1)
                    for a in range(4):
                        g = 4 * r + a
                        last = T.transpose(psum[0:64, r % 8, 128 * a:128 * a + 128],
                                           u_tok[:, g, :, :].rearrange("p q h -> p (q h)"), ident)
                    last.then_inc(step_rows_full, 1)
                pe.wait_ge(step_rows_act, (half + 1) * 16)
                pe.wait_ge(step_rows_dve, (half + 1) * 16)
                for j in range(8):
                    pe.wait_ge(m2_loaded[j % 4], (half * 2 + j // 4 + 1) * 16)
                    for a in range(8):
                        last = T.matmul(psum[:, j, 64 * a:64 * a + 64], m2_ring[:, j % 4, 128 * a:128 * a + 128],
                                        u_step[:, 8 * j + a, :], start=True, stop=True)
                    last.then_inc(step_in_full, 1)
                pe.wait_ge(state_in_act, (half + 1) * 16)
                pe.wait_ge(state_in_dve, (half + 1) * 16)
                columns_out(Q_ZS, 0, h_hi, h_lo, KT_IN)
                columns_out(Q_ZS + 4, 4, h_hi, h_lo, KT_IN)
                empty(set_a_emptied, B_ZS + 1)
                empty(set_b_emptied, B_ZS + 1)

                def y_products(j):
                    if j >= 2:
                        pe.wait_ge(y_row_act, half * 8 + j - 1)
                        pe.wait_ge(y_row_dve, half * 8 + j - 1)
                    pe.wait_ge(shifted_act, half * 16 + 2 * j + 2)
                    pe.wait_ge(shifted_dve, half * 16 + 2 * j + 2)
                    pe.wait_ge(mat_loaded[j % 2], (half * 4 + j // 2 + 1) * 32)
                    for a in range(8):
                        bank = psum[0:STEPS, 2 * (j % 2) + a // 4, 128 * (a % 4):128 * (a % 4) + 128]
                        cols = slice(128 * a, 128 * a + 128)
                        T.matmul(bank, u_step[:, 8 * j + a, :], mat_ring[:, j % 2, 0, cols], start=True, stop=False)
                        last = T.matmul(bank, sc_ring[:, j % 2, a, :], mat_ring[:, j % 2, 1, cols], start=False, stop=True)
                    last.then_inc(y_full, 1)

                def y_turn(j):
                    pe.wait_ge(y_row_act, half * 8 + j + 1)
                    pe.wait_ge(y_row_dve, half * 8 + j + 1)
                    if j >= 2:
                        pe.wait_ge(gelu_done, half * 8 + j - 1)
                    pe.sem_inc(pe_waited, 1)
                    for t in range(STEP):
                        last = T.transpose(psum[:, 4 + j % 2, STEPS * t:STEPS * t + STEPS], y_row[:, t, :],
                                           ident[0:STEPS, 0:STEPS])
                    last.then_inc(y_turned, 1)

                y_products(0)
                for j in range(8):
                    if j + 1 < 8:
                        y_products(j + 1)
                    y_turn(j)
                columns_out(Q_GLU, 0, y_hi, y_lo, KT_MID, lambda k: pe.wait_ge(g_ready, half * 8 + k + 1))
                columns_out(Q_GLU + 2, 4, y_hi, y_lo, KT_MID)
                empty(set_a_emptied, B_QK)
                columns_out(Q_Q, 0, h_hi, h_lo, KT_IN)
                empty(set_b_emptied, B_QK)
                columns_out(Q_K, 4, h_hi, h_lo, KT_IN)
                empty(set_a_emptied, B_V)
                rows_out(Q_V, 0, h_hi, h_lo, block_tokens)
                empty(set_b_emptied, B_V)
                rows_out(Q_V + 4, 4, h_hi, h_lo, block_tokens)
                empty(set_a_emptied, B_ZR)
                columns_out(Q_ZR, 0, h_hi, h_lo, KT_IN)
                empty(set_b_emptied, B_ZR)
                columns_out(Q_ZR + 4, 4, h_hi, h_lo, KT_IN)
                empty(set_a_emptied, B_ZR + 1)
                empty(set_b_emptied, B_ZR + 1)
                pe.wait_ge(rope_done, (half + 1) * 32)
                def square_sums(t):
                    n = half * BLOCKS + t
                    for par in range(2):
                        pe.wait_ge(o_squared, 2 * n + par + 1)
                        if t:
                            pe.wait_ge(ostd_ready, 2 * n + par - 1)
                        T.matmul(psum[:, 6 + par, :], ones_sb[:, :],
                                 o_sq[:, par].rearrange("p a n -> p (a n)"), start=True, stop=True).then_inc(osum_full, 1)

                def scores(t):
                    n = half * BLOCKS + t
                    tok = slice(BLOCK * t, BLOCK * t + BLOCK)
                    if t:
                        pe.wait_ge(scores_decayed, 2 * n)
                    for a in range(4):
                        for par in range(2):
                            rows = slice(64 * par, 64 * par + 64)
                            last = T.matmul(psum[:, 1 + par, 128 * a:128 * a + 128], k_t[rows, a, tok], q_t[rows, a, tok],
                                            start=True, stop=True)
                            if a == 3:
                                last.then_inc(scores_full, 1)
                    if t:
                        pe.wait_ge(k_zeta_ready, n)
                    for a in range(4):
                        last = T.transpose(psum[:, 0, 128 * a:128 * a + 128], k_t[:, a, tok], ident)
                    last.then_inc(k_turned, 1)

                scores(0)
                for t in range(BLOCKS):
                    n = half * BLOCKS + t
                    pe.wait_ge(q_xi_ready, n + 1)
                    pe.wait_ge(state_ready, 4 * n + START)
                    for par in range(2):
                        rows = slice(64 * par, 64 * par + 64)
                        pe.wait_ge(scores_decayed, 2 * n + par + 1)
                        if t:
                            pe.wait_ge(o_copied, 2 * n + par - 1)
                        for a in range(4):
                            head = 2 * a + par
                            bank = psum[:, 3 + par, 128 * a:128 * a + 128]
                            T.matmul(bank, v_row[:, t, V_HEAD * head:V_HEAD * head + V_HEAD],
                                     s_dec[:, par, 128 * a:128 * a + 128], start=True, stop=False)
                            last = T.matmul(bank, ret_state[rows, a, :], q_xi[rows, a, :], start=False, stop=True)
                        last.then_inc(o_full, 1)
                    pe.wait_ge(k_zeta_ready, n + 1)
                    for a in range(4):
                        for par in range(2):
                            head = 2 * a + par
                            last = T.matmul(psum[64 * par:64 * par + 64, 5, 128 * a:128 * a + 128],
                                            k_zeta[:, 64 * head:64 * head + 64],
                                            v_row[:, t, V_HEAD * head:V_HEAD * head + V_HEAD], start=True, stop=True)
                    last.then_inc(kv_full, 1)
                    if t + 1 < BLOCKS:
                        scores(t + 1)
                    square_sums(t)
                pe.wait_ge(ostd_ready, (half + 1) * BLOCKS * 2)
                pe.wait_ge(state_ready, (half + 1) * BLOCKS * 4 + START)
                pe.wait_ge(o_copied, (half + 1) * BLOCKS * 2)
                pe.wait_ge(ys_ready, (half + 1) * 2)
                pe.sem_inc(pe_waited, 1)
                with pe.Fori(0, MERGES) as b:
                    q0 = Q_S + b * Q_MERGE
                    columns_out(q0, 0, h_hi, h_lo, KT_IN)
                    empty(set_b_emptied, B_S + b)
                    columns_out(q0 + 4, 4, y_hi, y_lo, KT_MID)
                    empty(set_a_emptied, B_S + 1 + b)
                    pe.sem_inc(pe_waited, 1)
                with pe.Fori(0, MERGES) as b:
                    q0 = Q_R + b * Q_MERGE
                    columns_out(q0, 0, h_hi, h_lo, KT_IN)
                    empty(set_b_emptied, B_R + b)
                    pe.wait_ge(yr_ready, (half + 1) * 2)
                    columns_out(q0 + 4, 4, y_hi, y_lo, KT_MID)
                    empty(set_a_emptied, B_R + 1 + b)
                    pe.sem_inc(pe_waited, 1)
                for c in range(4):
                    which, first = (set_a_emptied, 0) if c % 2 == 0 else (set_b_emptied, 4)
                    empty(which, B_OUT + c // 2)
                    ready = (lambda k: pe.wait_ge(m_ready, half * 4 + k // 4 + 1)) if c == 0 else None
                    rows_out(Q_OUT + 4 * c, first, h_hi, h_lo, block_tokens, ready, KT_IN if c < 3 else KT_IN - SLOTS)
                for s in range(SLOTS):
                    unit_ready(QUADS - 1, s)
                for n in range(4):
                    for s in range(SLOTS):
                        k = KT_IN - SLOTS + s
                        bank = psum[:, 4 + n, :]
                        T.matmul(bank, block_tokens(h_hi, k, n), w_hi[:, s, :], start=False, stop=False)
                        T.matmul(bank, block_tokens(h_hi, k, n), w_lo[:, s, :], start=False, stop=False)
                        last = T.matmul(bank, block_tokens(h_lo, k, n), w_hi[:, s, :], start=False, stop=(s == SLOTS - 1))
                        if n == 3:
                            last.then_inc(unit_multiplied, 1)
                        elif s == SLOTS - 1:
                            last.then_inc(row_block_full, 1)


def retention_tables():
    log_g = np.log1p(-np.exp2(-5.0 - np.arange(HEADS)))
    idx = np.arange(BLOCK)
    scale = QK_HEAD ** -0.5
    ahead = (idx[:, None] // CHUNK) > (idx[None, :] // CHUNK)
    dist = np.abs(idx[None, :] - idx[:, None])
    dmat = np.where(ahead, 0.0, np.exp(dist[None] * log_g[:, None, None])) * scale
    dmat = dmat.reshape(4, 2, BLOCK, BLOCK).transpose(2, 1, 0, 3).reshape(BLOCK, -1)
    zeta = np.exp((BLOCK - 1 - idx)[:, None] * log_g[None, :]) * scale
    zeta = np.repeat(zeta, QK_HEAD, axis=1)
    xi = np.exp((idx + 1.0)[None, :] * log_g[:, None])
    xi = np.repeat(xi.reshape(4, 2, 1, BLOCK), QK_HEAD, axis=2).transpose(1, 2, 0, 3).reshape(P, -1)
    gdec = np.repeat(np.exp(BLOCK * log_g).reshape(4, 2).T, QK_HEAD, axis=0)
    return [np.ascontiguousarray(a, dtype=np.float32) for a in (dmat, zeta, xi, gdec)]


def rope_table():
    half = QK_HEAD // 2
    inv = np.float32(ROPE_BASE) ** (-np.arange(0, QK_HEAD, 2, dtype=np.float32) / np.float32(QK_HEAD))
    angle = (np.arange(SEQ, dtype=np.float32)[None, :] * inv.astype(np.float32)[:, None]).astype(np.float32)
    both = np.stack([np.cos(angle.astype(np.float64)), np.sin(angle.astype(np.float64))], 1)
    both = np.tile(both, (P // half, 1, 1)).reshape(P, 2, PASSES, TOK).transpose(2, 0, 1, 3)
    return np.ascontiguousarray(both, dtype=np.float32)


def layouts(x, norm_pre, w_in, lam_re, lam_im, log_step, s5_b_re, s5_b_im, s5_c_re, s5_c_im,
            s5_d, w_glu, b_glu, w_proj_s5, w_proj_ret, w_out, norm_post):
    def units(w):
        r, c = w.shape
        return w.reshape(r // P, P, c // COLS, COLS).transpose(2, 0, 1, 3)

    w = w_in[0]
    at = np.cumsum([0, S5_WIDTH, S5_WIDTH, 512, 512, S5_WIDTH, S5_WIDTH, D_MODEL, D_MODEL])
    part = [w[:, a:b] for a, b in zip(at[:-1], at[1:])]
    rot = np.arange(512).reshape(HEADS, 2, QK_HEAD // 2).transpose(1, 0, 2).reshape(-1)
    runs = [units(part[0]), units(part[1]), units(w_glu[0]), units(part[2][:, rot]), units(part[3][:, rot]),
            units(part[4]), units(part[5])]
    for gate, proj in ((part[6], w_proj_s5[0]), (part[7], w_proj_ret[0])):
        g, p = units(gate), units(proj)
        for b in range(MERGES):
            runs += [g[b:b + 1], p[b:b + 1]]
    runs.append(units(w_out[0]))
    stream = np.concatenate([r.reshape(-1, P, COLS) for r in runs], axis=0)

    def states(a):
        return np.ascontiguousarray(np.concatenate([a.T, a.T], axis=0))

    def stack(a, b):
        both = np.concatenate([a.transpose(1, 0, 2), b.transpose(1, 0, 2)], axis=0)
        return np.ascontiguousarray(both.reshape(P, -1))

    br, bi = s5_b_re[0], s5_b_im[0]
    cr, ci = s5_c_re[0].transpose(0, 2, 1), s5_c_im[0].transpose(0, 2, 1)
    d = np.tile(s5_d[0].reshape(GROUPS, GROUP).T, (STEP, 1))
    signs = np.ones((P, 2), np.float32)
    signs[64:, 0] = -1.0
    signs[:64, 1] = -1.0
    dmat, zeta, xi, gdec = retention_tables()
    xs = x[0]
    arrays = {
        "x": xs.reshape(SEQ // P, P, D_MODEL),
        "xT": xs.reshape(PASSES, TOK, KT_IN, P).transpose(0, 2, 3, 1).reshape(PASSES * KT_IN, P, TOK),
        "wstream": stream,
        "gain_in": norm_pre[0].reshape(KT_IN, P).T,
        "gain_out": np.broadcast_to(norm_post[0], (P, D_MODEL)),
        "b_glu": b_glu[0].reshape(KT_MID, P).T,
        "lam_re": states(lam_re[0]),
        "lam_im": states(lam_im[0]),
        "log_step": np.broadcast_to(log_step[0], (P, GROUPS)),
        "b_ri": stack(br, bi), "b_ir": stack(bi, br),
        "c_ri": stack(cr, ci), "c_ir": stack(ci, cr),
        "d_rep": d, "signs": signs, "eye": np.eye(P, 2 * P - GROUP, dtype=np.float32),
        "ones": np.ones((P, P), np.float32),
        "dmat": dmat, "zeta": zeta, "xi": xi, "gdec": gdec, "rope": rope_table(),
    }
    return {n: np.ascontiguousarray(a) for n, a in arrays.items()}


def kernel(**inputs):
    import concourse.bacc as bacc
    from concourse.bass_utils import run_bass_kernel_spmd

    arrays = layouts(**{n: np.asarray(a) for n, a in inputs.items()})
    nc = bacc.Bacc("TRN2", target_bir_lowering=False, num_devices=1)
    args = {n: nc.dram_tensor(f"in_{n}", a.shape, F32, kind="ExternalInput").ap() for n, a in arrays.items()}
    args["mats"] = nc.dram_tensor("mats", (3, 8, P, 1024), F32, kind="Internal").ap()
    args["rstd"] = nc.dram_tensor("rstd", (PASSES, P, TOK), F32, kind="Internal").ap()
    args["out"] = nc.dram_tensor("out_rows", (SEQ // P, P, D_MODEL), F32, kind="ExternalOutput").ap()
    build_program(nc, **args)
    r = run_bass_kernel_spmd(nc, [{f"in_{n}": a for n, a in arrays.items()}], core_ids=[0])
    return r.results[0]["out_rows"].reshape(1, SEQ, D_MODEL)
```

```python
import math
from contextlib import ExitStack

import numpy as np

import concourse.bass as bass
from concourse import mybir

F32 = mybir.dt.float32
F32R = mybir.dt.float32r
I32 = mybir.dt.int32
ALU = mybir.AluOpType
ACT = mybir.ActivationFunctionType
AX_X = mybir.AxisListType.X

P = 128
D_MODEL = 2048
SEQ = 1024
CHUNK = 64
EPS = 1e-6
S5_WIDTH = D_MODEL // 2
GROUP = 16
GROUPS = S5_WIDTH // GROUP
STATE = 64
HEADS = 8
V_HEAD = S5_WIDTH // HEADS
QK_HEAD = V_HEAD // 2
ROPE_BASE = 10000.0

PASSES = 2
TOK = SEQ // PASSES
KT_IN = D_MODEL // P
KT_MID = S5_WIDTH // P
COLS = 512
STEP = 8
STEPS = TOK // STEP
BLOCK = 128
BLOCKS = TOK // BLOCK

SLOTS = 4
Q_U, Q_ZS, Q_GLU, Q_Q, Q_K, Q_V, Q_ZR, Q_S, Q_R, Q_OUT = 0, 8, 16, 20, 24, 28, 36, 44, 68, 92
QUADS = 108
Q_MERGE = 6
MERGES = D_MODEL // COLS
B_U, B_ZS, B_GLU, B_QK, B_V, B_ZR, B_S, B_R, B_OUT = 0, 1, 2, 3, 4, 5, 6, 10, 14
BLOCKS_SET = 16
XT_SLOTS = 6
START = 1
CONSTS = 5
SCAN = 4 * STEPS + 2


def build_program(nc, x, xT, wstream, gain_in, gain_out, b_glu, lam_re, lam_im, log_step,
                  b_ri, b_ir, c_ri, c_ir, d_rep, signs, eye, ones, dmat, zeta, xi,
                  gdec, rope, mats, rstd, turned, out):
    with ExitStack() as ctx:
        def sb(name, shape, dt=F32):
            return ctx.enter_context(nc.sbuf_tensor(name, shape, dt))

        def sem(name):
            return ctx.enter_context(nc.semaphore(name))

        raw = sb("raw", [P, SLOTS, COLS])
        w_hi = sb("w_hi", [P, SLOTS, COLS], F32R)
        with nc.sbuf_tensor("plain", [P, SLOTS * COLS + 2 * KT_IN * TOK + 2 * KT_MID * TOK], F32) as plain_mem:
            pass
        w_lo = sb("w_lo", [P, SLOTS, COLS], F32R)
        h_hi = sb("h_hi", [P, KT_IN, TOK], F32R)
        h_lo = sb("h_lo", [P, KT_IN, TOK], F32R)
        y_hi = sb("y_hi", [P, KT_MID, TOK], F32R)
        y_lo = sb("y_lo", [P, KT_MID, TOK], F32R)
        R2, R3, R4 = 8192, 8192 + 4160, 8192 + 4160 + 4096
        work = sb("work", [P, R4 + 2048])
        tmp = sb("tmp", [P, 2, TOK])
        g_in = sb("g_in", [P, 2, TOK])
        eye_sb = sb("eye_sb", [P, 2 * P - GROUP])
        ones_sb = sb("ones_sb", [P, P])
        gain_sb = sb("gain_sb", [P, KT_IN])
        bglu_sb = sb("bglu_sb", [P, KT_MID])
        gdec_sb = sb("gdec_sb", [P, 4])
        eps_sb = sb("eps_sb", [P, 1])
        scan_re = sb("scan_re", [P, 2, 32])
        scan_im = sb("scan_im", [P, 2, 32])
        carry = sb("carry", [P, 2, 32])
        scan_t = sb("scan_t", [P, 2, 2, 32])
        ret_state = sb("ret_state", [P, 4, V_HEAD])
        ssq = sb("ssq", [P, 4, 4])
        rstd_out = sb("rstd_out", [P, 4])
        sign_sb = sb("sign_sb", [P, 2])
        psum = ctx.enter_context(nc.psum_tensor("psum", [P, 8, COLS], F32))
        ident = eye_sb[:, 0:P]

        def area(a, n):
            return work[:, a:a + n]

        at_h, at_y = SLOTS * COLS, SLOTS * COLS + 2 * KT_IN * TOK
        PLAIN = {"w_lo": 0, "h_hi": at_h, "h_lo": at_h + KT_IN * TOK, "y_hi": at_y, "y_lo": at_y + KT_MID * TOK}

        def plain(name, a, n):
            return plain_mem[:, PLAIN[name] + a:PLAIN[name] + a + n]

        u_chan = area(0, 4096).rearrange("p (j t c) -> p j t c", j=KT_MID, t=STEP)
        q_t = area(0, 2048).rearrange("p (a n) -> p a n", a=4)
        k_t = area(2048, 2048).rearrange("p (a n) -> p a n", a=4)
        m_t = area(0, 8192).rearrange("p (k n) -> p k n", k=KT_IN)
        o_row = area(0, 8192).rearrange("p (i n) -> p i n", i=4)
        u_step = area(4096, 4096).rearrange("p (g c) -> p g c", g=GROUPS)
        v_row = area(4096, 4096).rearrange("p (i n) -> p i n", i=4)
        state = area(R2, 4160).rearrange("p (c r k) -> p c r k", c=STEPS + 1, r=2)
        rope_sb = area(R2, 1024).rearrange("p (s n) -> p s n", s=2)
        z_r = area(R2, 4096).rearrange("p (k n) -> p k n", k=KT_MID)
        gain_row = area(R2, 2048)
        z_s = area(R3, 4096).rearrange("p (k n) -> p k n", k=KT_MID)
        o_t = [a.rearrange("p (h a n) -> p h a n", h=2, a=4)
               for a in (area(R3, 1024), tmp[:, :, :].rearrange("p a n -> p (a n)"))]
        o_sq = area(R3 + 1024, 1024).rearrange("p (h a n) -> p h a n", h=2, a=4)
        dmat_sb = area(R3 + 2048, 1024).rearrange("p (h n) -> p h n", h=2)
        zeta_sb = area(R3 + 3072, 512)
        xi_sb = area(R3 + 3584, 512)
        x_rows = area(R3, 4096).rearrange("p (s n) -> p s n", s=2)
        xt_ring = area(R4, 2048).rearrange("p (s n) -> p s n", s=4)
        sc_ring = area(R4, 1024).rearrange("p (s g c) -> p s g c", s=2, g=8)
        g_step = area(R4 + 1024, 1024).rearrange("p (s n) -> p s n", s=2)
        gate = area(R4, 2048).rearrange("p (s n) -> p s n", s=4)
        s_dec = area(R4, 1024).rearrange("p (h n) -> p h n", h=2)
        q_xi = area(R4 + 1024, 512).rearrange("p (a n) -> p a n", a=4)
        k_zeta = area(R4 + 1536, 512)

        rstd_in = plain("y_lo", 7 * TOK, TOK)
        x_rows_2 = plain("y_hi", 0, 4096).rearrange("p (s n) -> p s n", s=2)

        def m2_tile(j):
            return area(R3 + 1024 * j, 1024) if j < 4 else plain("y_lo", 1024 * (j - 4), 1024)

        def mat_tile(j, m):
            at = 2048 * (j % 2) + 1024 * m
            if j in (2, 3):
                return plain("y_hi", at, 1024)
            return plain("y_lo", at, 1024) if j in (4, 5) else area(at, 1024)

        def xt_slot(k):
            return xt_ring[:, k % XT_SLOTS, :] if k % XT_SLOTS < 4 else g_in[:, k % XT_SLOTS - 4, :]

        raw_loaded = [sem(f"raw_loaded{s}") for s in range(SLOTS)]
        head_split = sem("head_split")
        rest_split = sem("rest_split")
        unit_multiplied = sem("unit_multiplied")
        set_a_emptied = sem("set_a_emptied")
        set_b_emptied = sem("set_b_emptied")
        consts_loaded = sem("consts_loaded")
        rates_loaded = sem("rates_loaded")
        params_loaded = sem("params_loaded")
        sq_loaded = [sem(f"sq_loaded{s}") for s in range(SLOTS)]
        squared = sem("squared")
        square_added = sem("square_added")
        eps_ready = sem("eps_ready")
        std_ready = sem("std_ready")
        rstd_ready = sem("rstd_ready")
        rstd_stored = sem("rstd_stored")
        rstd_loaded = sem("rstd_loaded")
        setup_step = sem("setup_step")
        powers_ready = sem("powers_ready")
        pool_setup = sem("pool_setup")
        window_ready = sem("window_ready")
        m2_full = sem("m2_full")
        m2_copied = sem("m2_copied")
        lags_full = sem("lags_full")
        lags_ready = sem("lags_ready")
        m1_full = sem("m1_full")
        m1_act, m1_dve = sem("m1_act"), sem("m1_dve")
        m1_stored, m2_stored = sem("m1_stored"), sem("m2_stored")
        m3_stored = [sem(f"m3_stored{s}") for s in range(2)]
        xt_loaded = [sem(f"xt_loaded{k}") for k in range(KT_IN)]
        h_scaled = sem("h_scaled")
        h_head = sem("h_head")
        h_ready = sem("h_ready")
        u_stored = [sem(f"u_stored{b}") for b in range(2)]
        u_loaded = [sem(f"u_loaded{b}") for b in range(2)]
        m2_loaded = [sem(f"m2_loaded{b}") for b in range(2)]
        step_in_full = sem("step_in_full")
        state_in_act, state_in_dve = sem("state_in_act"), sem("state_in_dve")
        scan_done = sem("scan_done")
        mat_loaded = [sem(f"mat_loaded{j}") for j in range(KT_MID)]
        shifted_act, shifted_dve = sem("shifted_act"), sem("shifted_dve")
        y_full = sem("y_full")
        gelu_done = sem("gelu_done")
        g_stored = [sem(f"g_stored{j}") for j in range(KT_MID)]
        g_loaded = [sem(f"g_loaded{j}") for j in range(KT_MID)]
        g_head = sem("g_head")
        g_ready = sem("g_ready")
        glu_step = sem("glu_step")
        ys_head, ys_ready = sem("ys_head"), sem("ys_ready")
        rope_loaded = sem("rope_loaded")
        rope_step = sem("rope_step")
        rope_done = sem("rope_done")
        tables_loaded = sem("tables_loaded")
        k_turned = sem("k_turned")
        k_zeta_ready = sem("k_zeta_ready")
        scores_full = sem("scores_full")
        scores_decayed = sem("scores_decayed")
        q_xi_ready = sem("q_xi_ready")
        o_full = sem("o_full")
        kv_full = sem("kv_full")
        state_ready = sem("state_ready")
        o_copied = sem("o_copied")
        o_squared = sem("o_squared")
        osum_full = sem("osum_full")
        ostd_ready = sem("ostd_ready")
        o_inverse = sem("o_inverse")
        o_scaled = sem("o_scaled")
        z_scaled = sem("z_scaled")
        yr_head, yr_ready = sem("yr_head"), sem("yr_ready")
        m_added = sem("m_added")
        m_head, m_ready = sem("m_head"), sem("m_ready")
        out_squared = sem("out_squared")
        out_stat = sem("out_stat")
        out_std = sem("out_std")
        rows_scaled = sem("rows_scaled")
        top_ready = sem("top_ready")
        out_ready = sem("out_ready")
        row_block_full = sem("row_block_full")
        x_loaded = sem("x_loaded")
        gain_row_loaded = sem("gain_row_loaded")
        out_stored = sem("out_stored")
        bottom_stored = sem("bottom_stored")
        rows_free = sem("rows_free")

        pool_waited, pe_waited = sem("pool_waited"), sem("pe_waited")

        block = ctx.enter_context(nc.Block())

        @block.sync
        def _(sp):
            sp.sem_inc(rest_split, SLOTS)
            sp.sem_inc(h_scaled, XT_SLOTS)
            for counted in (m_added, out_squared, out_ready, bottom_stored, rows_free, scan_done, state_ready,
                            set_a_emptied, set_b_emptied):
                sp.sem_inc(counted, START)
            sp.sem_inc(squared, SLOTS)
            with sp.Fori(0, PASSES * KT_IN // SLOTS) as i:
                for s in range(SLOTS):
                    sp.wait_ge(squared, i * SLOTS + s + 1)
                    sp.dma_start(raw[:, s, :], xT[i * SLOTS + s]).then_inc(sq_loaded[s], 16)
            sp.wait_ge(squared, PASSES * KT_IN + SLOTS)
            with sp.Fori(0, PASSES) as half:
                def load_unit(q, s):
                    sp.wait_ge(rest_split, (half * QUADS + q) * SLOTS + s + 1)
                    sp.dma_start(raw[:, s, :], wstream[q * SLOTS + s]).then_inc(raw_loaded[s], 16)

                sp.wait_ge(rstd_stored, 16)
                sp.wait_ge(m_added, half * 16 + START)
                sp.dma_start(rstd_in, rstd[half]).then_inc(rstd_loaded, 16)
                for k in range(KT_IN):
                    load_unit(k // SLOTS, k % SLOTS)
                    for t in ((0, 1, 2) if k == 0 else (k + 2,) if k + 2 < KT_IN else ()):
                        sp.wait_ge(h_scaled, half * KT_IN + t + 1)
                        sp.dma_start(xt_slot(t), xT[half * KT_IN + t]).then_inc(xt_loaded[t], 16)
                with sp.Fori(KT_IN // SLOTS, QUADS) as q:
                    for s in range(SLOTS):
                        load_unit(q, s)

        window = plain("h_hi", 0, 8192).rearrange("p (g i h) -> p g i h", g=GROUPS, i=STEP)
        m1_stage = area(0, 8192).rearrange("p (g t h) -> p g t h", g=GROUPS, t=STEP)
        m2_stage = area(R2, 8192)
        bb_p = plain("h_lo", 0, 1024).rearrange("p (g h) -> p g h", g=GROUPS)
        bb_q = plain("h_lo", 1024, 1024).rearrange("p (g h) -> p g h", g=GROUPS)
        b_tmp = plain("h_lo", 2048, 1024).rearrange("p (g h) -> p g h", g=GROUPS)
        b_tmp2 = plain("h_lo", 3072, 1024).rearrange("p (g h) -> p g h", g=GROUPS)
        win_tmp = plain("h_lo", 4096, 1024).rearrange("p (g i h) -> p g i h", g=8, i=STEP)
        lags = plain("h_lo", 6144, 1024)
        rstd_stage = plain("h_lo", 7168, 1024)
        cc_p = plain("y_hi", 0, 1024).rearrange("p (g h) -> p g h", g=GROUPS)
        cc_q = plain("y_hi", 1024, 1024).rearrange("p (g h) -> p g h", g=GROUPS)
        m3_stage = [plain("y_hi", 2048 + 1024 * n, 1024).rearrange("p (g t h) -> p g t h", g=8, t=STEP) for n in range(2)]
        m3_tmp = plain("y_lo", 0, 1024).rearrange("p (g t h) -> p g t h", g=8, t=STEP)
        pow_re = plain("y_lo", 1024, 576).rearrange("p (j g) -> p j g", j=9)
        pow_im = plain("y_lo", 1600, 576).rearrange("p (j g) -> p j g", j=9)
        powers_tmp = plain("h_lo", 4096, 1024).rearrange("p (n g) -> p n g", n=16)
        small = tmp[:, :, :].rearrange("p a n -> p (a n)")
        (lam_r, lam_i, step_sb, par_re, par_im, d_sb, s0, s1, s2, s3, s4, s5, s6, s7, s8, s9) = [
            small[:, 64 * n:64 * n + 64] for n in range(16)]

        def copy(eng, dst, src):
            if eng is nc.scalar:
                return eng.activation(dst, src, ACT.Copy)
            return eng.tensor_copy(dst, src)

        def m1_banks(seq, eng, odd):
            done = m1_dve if odd else m1_act
            for n in range(odd, 16, 2):
                seq.wait_ge(m1_full, n + 1)
                gs = slice(32 * (n % 2), 32 * (n % 2) + 32)
                copy(eng, m1_stage[:, gs, n // 2, :], psum[:, n % 8, :].rearrange("p (g h) -> p g h", h=GROUP)).then_inc(done, 1)

        def g_slot(j):
            return (tmp if j % 4 < 2 else g_in)[:, j % 2, :]

        def g_tile(j):
            return g_slot(j).rearrange("p (t c) -> p c t", t=STEP)

        def by_channel(n):
            return turned[n].rearrange("(t q c) -> q t c", t=STEP, q=P)

        def state_inputs(seq, eng, half, odd):
            done = state_in_dve if odd else state_in_act
            for j in range(odd, 8, 2):
                seq.wait_ge(step_in_full, half * 8 + j + 1)
                for par in range(2):
                    for r in range(2):
                        src = psum[64 * r:64 * r + 64, 4 + j % 4, :].rearrange("p (k g c) -> p k g c", k=4, g=2)[:, :, par, :]
                        dst = state[64 * par:64 * par + 64, 1:STEPS + 1, r, 4 * j:4 * j + 4].rearrange("p c k -> p k c")
                        copy(eng, dst, src).then_inc(done, 1)

        def shift_states(seq, eng, half, j, r):
            done = shifted_act if eng is nc.scalar else shifted_dve
            if j >= 2:
                seq.wait_ge(y_full, half * 8 + j - 1)
            for par in range(2):
                src = state[64 * par:64 * par + 64, 0:STEPS, r, 4 * j:4 * j + 4].rearrange("p c k -> p k c")
                copy(eng, sc_ring[64 * r:64 * r + 64, j % 2, par::2, :], src).then_inc(done, 1)

        @block.gpsimd
        def _(pool):
            for dst, src in ((ones_sb[:, :], ones), (eye_sb[:, :], eye), (gain_sb[:, :], gain_in),
                             (bglu_sb[:, :], b_glu), (gdec_sb[:, :], gdec)):
                pool.dma_start(dst, src).then_inc(consts_loaded, 16)
            pool.wait_ge(powers_ready, 1)
            for j in range(8):
                gs = slice(8 * j, 8 * j + 8)

                def powers(a):
                    return a[:, 1:9, gs].rearrange("p t g -> p g t").unsqueeze(3).broadcast_to([P, 8, STEP, GROUP])

                def coefs(a):
                    return a[:, gs, :].unsqueeze(2).broadcast_to([P, 8, STEP, GROUP])

                if j >= 2:
                    pool.wait_ge(m3_stored[j % 2], 16 * (j // 2))
                stage = m3_stage[j % 2]
                pool.tensor_tensor(stage, coefs(cc_p), powers(pow_re), ALU.mult).then_inc(pool_setup, 1)
                if j:
                    pool.wait_ge(pool_setup, 3 * j)
                pool.tensor_tensor(m3_tmp, coefs(cc_q), powers(pow_im), ALU.mult).then_inc(pool_setup, 1)
                pool.wait_ge(pool_setup, 3 * j + 2)
                pool.tensor_tensor(stage, stage, m3_tmp, ALU.subtract).then_inc(pool_setup, 1)
                pool.wait_ge(pool_setup, 3 * j + 3)
                pool.dma_start(mats[2, j], stage.rearrange("p g t h -> p (g t h)")).then_inc(m3_stored[j % 2], 16)

            with pool.Fori(0, PASSES) as half:
                pool.wait_ge(m1_stored, 16)
                pool.wait_ge(m2_stored, 8 * 16)
                pool.wait_ge(m3_stored[0], 4 * 16)
                pool.wait_ge(m3_stored[1], 4 * 16)
                pool.wait_ge(out_ready, half * 2 + START)
                pool.sem_inc(pool_waited, 1)

                def load_mats(j):
                    pool.dma_start(mat_tile(j, 0), mats[0, j]).then_inc(mat_loaded[j], 16)
                    pool.dma_start(mat_tile(j, 1), mats[2, j]).then_inc(mat_loaded[j], 16)

                pool.wait_ge(h_scaled, (half + 1) * KT_IN + XT_SLOTS)
                pool.sem_inc(pool_waited, 1)
                for j in range(8):
                    pool.dma_start(m2_tile(j), mats[1, j]).then_inc(m2_loaded[j // 4], 16)
                pool.wait_ge(bottom_stored, half * 32 + START)
                pool.sem_inc(pool_waited, 1)
                for b in range(2):
                    pool.wait_ge(u_stored[b], (half + 1) * 64)
                    pool.sem_inc(pool_waited, 1)
                    for j in range(4 * b, 4 * b + 4):
                        pool.dma_start(u_step[:, 8 * j:8 * j + 8, :],
                                       turned[j].rearrange("(p g c) -> p g c", p=P, g=8)).then_inc(u_loaded[b], 16)
                for j in range(4):
                    load_mats(j)
                pool.wait_ge(step_in_full, (half + 1) * 8)
                pool.sem_inc(pool_waited, 1)
                load_mats(4)
                load_mats(5)
                with pool.Fori(Q_ZS + 2, Q_GLU + 1) as q:
                    for s in range(SLOTS):
                        pool.wait_ge(head_split, (half * QUADS + q) * SLOTS + s + 1)
                        pool.sem_inc(pool_waited, 1)
                        pool.tensor_tensor(w_lo[:, s, :], raw[:, s, :], w_hi[:, s, :].bitcast(F32),
                                           ALU.subtract).then_inc(rest_split, 1)
                for j in range(2):
                    pool.wait_ge(y_full, half * 8 + j + 1)
                    pool.sem_inc(pool_waited, 1)
                    load_mats(6 + j)
                for j in range(8):
                    pool.wait_ge(g_stored[j], (half + 1) * 16)
                    if j >= 4:
                        pool.wait_ge(g_ready, half * 8 + j - 3)
                    pool.sem_inc(pool_waited, 1)
                    pool.dma_start(g_slot(j).rearrange("p (t c) -> p t c", t=STEP),
                                   by_channel(KT_MID + j)).then_inc(g_loaded[j], 16)
                pool.wait_ge(g_ready, (half + 1) * 8)
                pool.sem_inc(pool_waited, 1)
                pool.dma_start(rope_sb, rope[half]).then_inc(rope_loaded, 16)
                pool.wait_ge(ys_ready, (half + 1) * 2)
                pool.sem_inc(pool_waited, 1)
                pool.dma_start(area(R3 + 2048, 1024), dmat).then_inc(tables_loaded, 16)
                pool.dma_start(zeta_sb, zeta).then_inc(tables_loaded, 16)
                pool.dma_start(xi_sb, xi).then_inc(tables_loaded, 16)
                for t in range(BLOCKS):
                    for par in range(2):
                        n = half * 2 * BLOCKS + 2 * t + par
                        pool.wait_ge(o_inverse, n + 1)
                        pool.sem_inc(pool_waited, 1)
                        pool.tensor_tensor(o_t[t % 2][:, par], o_t[t % 2][:, par], o_sq[:, par], ALU.mult).then_inc(o_scaled, 1)
                        pool.wait_ge(o_scaled, n + 1)
                        pool.sem_inc(pool_waited, 1)
                        dst = z_r[:, par::2, BLOCK * t:BLOCK * t + BLOCK]
                        pool.tensor_tensor(dst, dst, o_t[t % 2][:, par], ALU.mult).then_inc(z_scaled, 1)
                pool.wait_ge(z_scaled, (half + 1) * BLOCKS * 2)
                pool.sem_inc(pool_waited, 1)
                for i in range(2):
                    pool.dma_start(x_rows[:, i, :], x[half * 4 + i]).then_inc(x_loaded, 16)
                pool.wait_ge(yr_ready, (half + 1) * 2)
                pool.sem_inc(pool_waited, 1)
                pool.dma_start(gain_row, gain_out).then_inc(gain_row_loaded, 16)
                pool.wait_ge(m_added, (half + 1) * 16)
                pool.sem_inc(pool_waited, 1)
                for i in range(2):
                    pool.dma_start(x_rows_2[:, i, :], x[half * 4 + 2 + i]).then_inc(x_loaded, 16)
                pool.wait_ge(x_loaded, (half + 1) * 4 * 16)
                for i in range(2):
                    pool.wait_ge(rows_scaled, half * 2 + i + 1)
                    pool.sem_inc(pool_waited, 1)
                    pool.tensor_tensor(o_row[:, i, :], o_row[:, i, :], x_rows[:, i, :], ALU.add).then_inc(top_ready, 1)
                    pool.wait_ge(top_ready, half * 2 + i + 1)
                    pool.sem_inc(pool_waited, 1)
                    pool.dma_start(out[half * 4 + i], o_row[:, i, :]).then_inc(out_stored, 16)
                pool.wait_ge(out_stored, (half + 1) * 2 * 16)
                pool.sem_inc(rows_free, 1)
            pool.wait_ge(out_stored, PASSES * 2 * 16)

        @block.scalar
        def _(act):
            for dst, src in ((lam_r, lam_re), (lam_i, lam_im), (step_sb, log_step)):
                act.dma_start(dst, src).then_inc(rates_loaded, 16)
            for dst, src in ((sign_sb[:, :], signs), (bb_p, b_ri), (bb_q, b_ir), (cc_p, c_ri), (cc_q, c_ir), (d_sb, d_rep)):
                act.dma_start(dst.rearrange("p g h -> p (g h)") if dst.ndim == 3 else dst, src
                              ).then_inc(params_loaded, 16)
            act.sem_inc(square_added, SLOTS)
            with act.Fori(0, PASSES * KT_IN // SLOTS) as i:
                for s in range(SLOTS):
                    act.wait_ge(sq_loaded[s], i * 16 + 16)
                    act.wait_ge(square_added, i * SLOTS + s + 1)
                    nc.scalar.activation(plain("w_lo", COLS * s, COLS), raw[:, s, :], ACT.Square).then_inc(squared, 1)
            act.wait_ge(consts_loaded, CONSTS * 16)
            act.wait_ge(square_added, PASSES * KT_IN + SLOTS)
            act.wait_ge(eps_ready, 1)
            for p in range(PASSES):
                nc.scalar.activation(rstd_stage[:, TOK * p:TOK * p + TOK], psum[:, 6 + p, :], ACT.Sqrt,
                                     scale=1.0 / D_MODEL, bias=eps_sb[:, 0:1]).then_inc(std_ready, 1)
            for n in range(16):
                act.wait_ge(m2_full, n + 1)
                nc.scalar.activation(m2_stage[:, COLS * n:COLS * n + COLS], psum[:, 2 + n % 4, :],
                                     ACT.Copy).then_inc(m2_copied, 1)
                if n % 2:
                    act.wait_ge(m2_copied, n + 1)
                    act.dma_start(mats[1, n // 2], m2_stage[:, 512 * n - 512:512 * n + 512]).then_inc(m2_stored, 16)
            act.wait_ge(rstd_ready, 1)
            act.dma_start(rstd.rearrange("a p n -> p a n"), rstd_stage.rearrange("p (a n) -> p a n", a=PASSES)
                          ).then_inc(rstd_stored, 16)
            m1_banks(act, nc.scalar, 0)
            act.wait_ge(m1_act, 8)
            act.wait_ge(m1_dve, 8)
            act.dma_start(mats[0].rearrange("j p n -> p j n"), area(0, 8192).rearrange("p (j n) -> p j n", j=8)
                          ).then_inc(m1_stored, 16)

            with act.Fori(0, PASSES) as half:
                def heads(q):
                    for s in range(SLOTS):
                        head(q, s)

                def head(q, s):
                    act.wait_ge(raw_loaded[s], (half * QUADS + q + 1) * 16)
                    act.wait_ge(unit_multiplied, (half * QUADS + q) * SLOTS + s + 1)
                    nc.scalar.activation(w_hi[:, s, :], raw[:, s, :], ACT.Copy).then_inc(head_split, 1)

                def multiplied(q):
                    act.wait_ge(unit_multiplied, (half * QUADS + q) * SLOTS + SLOTS)

                for k in range(KT_IN):
                    act.wait_ge(h_scaled, half * KT_IN + k + 1 + XT_SLOTS)
                    if k == 0:
                        multiplied(0)
                    nc.scalar.activation(h_hi[:, k, :], tmp[:, k % 2, :], ACT.Copy).then_inc(h_head, 1)
                    head(Q_U + k // 4, k % 4)
                def turn_u(b, emptied):
                    for n in range(4):
                        nc.scalar.activation(u_chan[:, 4 * b + n], psum[:, 4 * b + n, :].rearrange("p (c t) -> p t c", t=STEP),
                                             ACT.Copy).then_inc(emptied, 1)
                        act.wait_ge(emptied, (half * BLOCKS_SET + B_U) * 4 + n + 1 + START)
                        act.dma_start(by_channel(4 * b + n), u_chan[:, 4 * b + n]).then_inc(u_stored[b], 16)

                heads(Q_U + 4)
                multiplied(Q_U + 4)
                act.wait_ge(m1_stored, 16)
                act.wait_ge(m2_stored, 8 * 16)
                act.wait_ge(rows_free, half + START)
                turn_u(0, set_a_emptied)
                for q in range(5, 8):
                    heads(Q_U + q)
                heads(Q_ZS)
                multiplied(Q_ZS)
                turn_u(1, set_b_emptied)
                heads(Q_ZS + 1)
                state_inputs(act, nc.scalar, half, 0)
                for q in range(2, 4):
                    heads(Q_ZS + q)
                heads(Q_ZS + 4)
                multiplied(Q_ZS + 4)
                for n in range(4):
                    nc.scalar.activation(z_s[:, n, :], psum[:, n, :], ACT.Silu).then_inc(set_a_emptied, 1)
                for q in range(5, 8):
                    heads(Q_ZS + q)
                act.wait_ge(scan_done, (half + 1) * SCAN + START)
                shift_states(act, nc.scalar, half, 0, 1)
                shift_states(act, nc.scalar, half, 1, 1)
                heads(Q_GLU)
                multiplied(Q_GLU)
                for n in range(4):
                    nc.scalar.activation(z_s[:, 4 + n, :], psum[:, 4 + n, :], ACT.Silu).then_inc(set_b_emptied, 1)
                def g_heads(j):
                    act.wait_ge(g_loaded[j], (half + 1) * 16)
                    act.wait_ge(y_full, half * 8 + (3 + j // 4))
                    nc.scalar.activation(y_hi[:, j, :].rearrange("p (c t) -> p c t", t=STEP), g_tile(j),
                                         ACT.Copy).then_inc(g_head, 1)

                for j in range(8):
                    if j + 2 < 8:
                        shift_states(act, nc.scalar, half, j + 2, 1)
                    act.wait_ge(y_full, half * 8 + j + 1)
                    if j >= 2:
                        act.wait_ge(g_stored[j - 2], (half + 1) * 16)
                    nc.scalar.activation(g_step[:, j % 2, :], psum[:, j % 4, :], ACT.Gelu_apprx_tanh).then_inc(gelu_done, 1)
                    act.wait_ge(gelu_done, half * 8 + j + 1)
                    act.dma_start(turned[KT_MID + j].rearrange("(p n) -> p n", p=P), g_step[:, j % 2, :]).then_inc(g_stored[j], 16)
                    if j >= 4:
                        g_heads(j - 4)
                for j in range(4, 8):
                    g_heads(j)
                heads(Q_GLU + 1)
                heads(Q_GLU + 2)
                multiplied(Q_GLU + 2)
                for n in range(4):
                    nc.scalar.activation(gate[:, n, :], psum[:, n, :], ACT.Sigmoid,
                                         bias=bglu_sb[:, n:n + 1]).then_inc(set_a_emptied, 1)
                heads(Q_GLU + 3)
                heads(Q_Q)
                multiplied(Q_Q)
                act.wait_ge(glu_step, half * 24 + 12)
                for n in range(4):
                    nc.scalar.activation(gate[:, n, :], psum[:, 4 + n, :], ACT.Sigmoid,
                                         bias=bglu_sb[:, 4 + n:5 + n]).then_inc(set_b_emptied, 1)
                heads(Q_Q + 1)
                act.wait_ge(glu_step, (half + 1) * 24)
                for n in range(2):
                    nc.scalar.activation(y_hi[:, 4 * n:4 * n + 4, :], z_s[:, 4 * n:4 * n + 4, :],
                                         ACT.Copy).then_inc(ys_head, 1)
                for q in range(2, 4):
                    heads(Q_Q + q)
                for q in range(4):
                    heads(Q_K + q)
                for q in range(8):
                    heads(Q_V + q)
                for q in range(4):
                    heads(Q_ZR + q)
                heads(Q_ZR + 4)
                multiplied(Q_ZR + 4)
                act.wait_ge(rope_done, (half + 1) * 32)
                for n in range(4):
                    nc.scalar.activation(z_r[:, n, :], psum[:, n, :], ACT.Silu).then_inc(set_a_emptied, 1)
                for q in range(5, 8):
                    heads(Q_ZR + q)
                heads(Q_S)
                multiplied(Q_S)
                for n in range(4):
                    nc.scalar.activation(z_r[:, 4 + n, :], psum[:, 4 + n, :], ACT.Silu).then_inc(set_b_emptied, 1)
                for t in range(BLOCKS):
                    before = half * 2 * BLOCKS + 2 * t
                    for par in range(2):
                        act.wait_ge(o_full, before + par + 1)
                        if t >= 2 and par == 0:
                            act.wait_ge(z_scaled, before - 2)
                        nc.scalar.activation(o_t[t % 2][:, par], psum[:, 3 + par, :].rearrange("p (a n) -> p a n", a=4),
                                             ACT.Copy).then_inc(o_copied, 1)
                    for par in range(2):
                        act.wait_ge(o_copied, before + par + 1)
                        if t:
                            act.wait_ge(o_scaled, before - 1 + par)
                        nc.scalar.activation(o_sq[:, par], o_t[t % 2][:, par], ACT.Square).then_inc(o_squared, 1)
                    for par in range(2):
                        act.wait_ge(osum_full, before + par + 1)
                        nc.scalar.activation(o_sq[:, par], psum[:, 6 + par, :].rearrange("p (a n) -> p a n", a=4),
                                             ACT.Sqrt, scale=1.0 / V_HEAD, bias=eps_sb[:, 0:1]).then_inc(ostd_ready, 1)
                act.wait_ge(kv_full, (half + 1) * BLOCKS)
                with act.Fori(0, MERGES) as b:
                    q0 = Q_S + b * Q_MERGE
                    for q in range(1, 5):
                        heads(q0 + q)
                    multiplied(q0 + 4)
                    act.wait_ge(set_b_emptied, (half * BLOCKS_SET + B_S + b) * 4 + START)
                    for n in range(4):
                        nc.scalar.activation(gate[:, n, :], psum[:, n, :], ACT.Sigmoid).then_inc(set_a_emptied, 1)
                    heads(q0 + 5)
                    heads(q0 + 6)
                multiplied(Q_R)
                act.wait_ge(z_scaled, (half + 1) * BLOCKS * 2)
                for n in range(2):
                    nc.scalar.activation(y_hi[:, 4 * n:4 * n + 4, :], z_r[:, 4 * n:4 * n + 4, :],
                                         ACT.Copy).then_inc(yr_head, 1)
                def merge_gates(b):
                    q0 = Q_R + b * Q_MERGE
                    for q in range(1, 5):
                        heads(q0 + q)
                    multiplied(q0 + 4)
                    act.wait_ge(m_added, half * 16 + b * 4 + START)
                    for n in range(4):
                        nc.scalar.activation(gate[:, n, :], psum[:, n, :], ACT.Sigmoid).then_inc(set_a_emptied, 1)
                    heads(q0 + 5)

                def m_heads(n):
                    act.wait_ge(m_added, half * 16 + 4 * n + 4 + START)
                    nc.scalar.activation(h_hi[:, 4 * n:4 * n + 4, :], m_t[:, 4 * n:4 * n + 4, :],
                                         ACT.Copy).then_inc(m_head, 1)

                with act.Fori(0, MERGES - 1) as b:
                    merge_gates(b)
                    heads(Q_R + b * Q_MERGE + 6)
                merge_gates(MERGES - 1)
                for n in range(MERGES - 1):
                    m_heads(n)
                heads(Q_OUT)
                m_heads(MERGES - 1)
                for c in range(3):
                    for q in range(1, 5):
                        heads(Q_OUT + 4 * c + q)
                    multiplied(Q_OUT + 4 * c + 4)
                    first = 4 * (c % 2)
                    for i in range(4):
                        if c or i:
                            act.wait_ge(out_squared, half * 16 + 4 * c + i + START)
                        nc.scalar.activation(tmp[:, 0, :], psum[:, first + i, :], ACT.Square,
                                             accum_out=ssq[:, i, c:c + 1]).then_inc(out_squared, 1)
                for q in range(1, 4):
                    heads(Q_OUT + 12 + q)
                for i in range(4):
                    if i < 3:
                        act.wait_ge(row_block_full, half * 3 + i + 1)
                    else:
                        multiplied(QUADS)
                    act.wait_ge(out_squared, half * 16 + 12 + i + START)
                    nc.scalar.activation(tmp[:, 0, :], psum[:, 4 + i, :], ACT.Square,
                                         accum_out=ssq[:, i, 3:4]).then_inc(out_squared, 1)
                    act.wait_ge(out_stat, half * 8 + 2 * i + 1)
                    nc.scalar.activation(rstd_out[:, i:i + 1], rstd_out[:, i:i + 1], ACT.Sqrt, scale=1.0 / D_MODEL,
                                         bias=eps_sb[:, 0:1]).then_inc(out_std, 1)
                    if 1 <= i <= 2:
                        act.wait_ge(out_stat, half * 8 + 2 * i)
                        act.wait_ge(set_b_emptied, (half * BLOCKS_SET + B_OUT + 1) * 4 + i + START)
                        nc.scalar.activation(o_row[:, i - 1, :], o_row[:, i - 1, :], ACT.Copy,
                                             scale=rstd_out[:, i - 1:i]).then_inc(rows_scaled, 1)

                for i in range(2):
                    act.wait_ge(out_ready, half * 2 + i + 1 + START)
                    act.dma_start(out[half * 4 + 2 + i], o_row[:, 2 + i, :]).then_inc(bottom_stored, 16)
            act.wait_ge(bottom_stored, PASSES * 2 * 16 + START)

        @block.vector
        def _(dve):
            V = nc.vector
            steps = [0]

            def then(ins):
                steps[0] += 1
                ins.then_inc(setup_step, 1)
                dve.wait_ge(setup_step, steps[0])

            def ts(dst, src, a, op, b=None, op2=ALU.bypass):
                if b is None:
                    then(V.tensor_scalar(dst, src, a, None, op))
                else:
                    then(V.tensor_scalar(dst, src, a, b, op, op2))

            def tt(dst, a, b, op):
                then(V.tensor_tensor(dst, a, b, op))

            MAGIC = 12582912.0

            def rint(dst, src):
                ts(dst, src, MAGIC, ALU.add)
                ts(dst, dst, -MAGIC, ALU.add)

            def poly(dst, z, coefs):
                ts(dst, z, coefs[0], ALU.mult, coefs[1], ALU.add)
                for c in coefs[2:]:
                    tt(dst, dst, z, ALU.mult)
                    ts(dst, dst, c, ALU.add)

            def exp(dst, arg, n, r, bits):
                ts(r, arg, 89.0, ALU.min, -110.0, ALU.max)
                ts(n, r, 1.0 / math.log(2.0), ALU.mult)
                rint(n, n)
                then(V.scalar_tensor_tensor(r, n, -0.693359375, r, ALU.mult, ALU.add))
                then(V.scalar_tensor_tensor(r, n, 2.12194440e-4, r, ALU.mult, ALU.add))
                poly(dst, r, [1 / 5040, 1 / 720, 1 / 120, 1 / 24, 1 / 6, 0.5, 1.0, 1.0])
                ts(n, n, 127.0, ALU.add, 0.0, ALU.max)
                ts(n, n, 255.0, ALU.min, 8388608.0, ALU.mult)
                then(V.tensor_copy(bits.bitcast(I32), n))
                tt(dst, dst, bits, ALU.mult)

            V.memset(eps_sb[:, :], EPS).then_inc(eps_ready, 1)
            then(V.memset(carry[:, :, :], 0.0))
            then(V.memset(ret_state[:, :, :], 0.0))
            dve.wait_ge(rates_loaded, 3 * 16)
            exp(s0, step_sb, s1, s2, s3)
            tt(s4, lam_r, s0, ALU.mult)
            exp(par_re, s4, s1, s2, s3)
            tt(s4, lam_i, s0, ALU.mult)
            ts(s1, s4, 2.0 / math.pi, ALU.mult)
            rint(s1, s1)
            half_pi = [1.5703125, 4.8351287841796875e-4, -3.1385570764541626e-7, 6.077100506506192e-11]
            then(V.scalar_tensor_tensor(s2, s1, -half_pi[0], s4, ALU.mult, ALU.add))
            for c in half_pi[1:]:
                then(V.scalar_tensor_tensor(s2, s1, -c, s2, ALU.mult, ALU.add))
            ts(s3, s1, 0.25, ALU.mult, -0.375, ALU.add)
            rint(s3, s3)
            then(V.scalar_tensor_tensor(s1, s3, -4.0, s1, ALU.mult, ALU.add))
            tt(s5, s2, s2, ALU.mult)
            poly(s6, s5, [2.7557319e-6, -1.98412698e-4, 8.33333333e-3, -1.66666667e-1, 1.0])
            tt(s6, s6, s2, ALU.mult)
            poly(s7, s5, [2.48015873e-5, -1.38888889e-3, 4.16666667e-2, -0.5, 1.0])
            ts(s3, s1, 1.0, ALU.is_equal)
            ts(s4, s1, 3.0, ALU.is_equal)
            tt(s3, s3, s4, ALU.add)
            ts(s4, s3, -1.0, ALU.mult, 1.0, ALU.add)
            tt(s8, s6, s4, ALU.mult)
            tt(s9, s7, s3, ALU.mult)
            tt(s8, s8, s9, ALU.add)
            tt(s7, s7, s4, ALU.mult)
            tt(s6, s6, s3, ALU.mult)
            tt(s7, s7, s6, ALU.add)
            ts(s3, s1, 2.0, ALU.is_ge, -2.0, ALU.mult)
            ts(s3, s3, 1.0, ALU.add)
            tt(s8, s8, s3, ALU.mult)
            ts(s3, s1, 1.0, ALU.is_equal)
            ts(s4, s1, 2.0, ALU.is_equal)
            tt(s3, s3, s4, ALU.add)
            ts(s3, s3, -2.0, ALU.mult, 1.0, ALU.add)
            tt(s7, s7, s3, ALU.mult)
            then(V.memset(pow_re[:, 0, :], 1.0))
            then(V.memset(pow_im[:, 0, :], 0.0))
            tt(pow_im[:, 1, :], par_re, s8, ALU.mult)
            tt(pow_re[:, 1, :], par_re, s7, ALU.mult)
            def bunch(a, first, count):
                return a[:, first:first + count, :]

            for m in (1, 2, 4):
                re_m = pow_re[:, m:m + 1, :].broadcast_to([P, m, GROUPS])
                im_m = pow_im[:, m:m + 1, :].broadcast_to([P, m, GROUPS])
                p_rr, p_ii, p_ri, p_ir = [powers_tmp[:, 4 * n:4 * n + m, :] for n in range(4)]
                V.tensor_tensor(p_rr, bunch(pow_re, 1, m), re_m, ALU.mult).then_inc(setup_step, 1)
                V.tensor_tensor(p_ii, bunch(pow_im, 1, m), im_m, ALU.mult).then_inc(setup_step, 1)
                V.tensor_tensor(p_ri, bunch(pow_re, 1, m), im_m, ALU.mult).then_inc(setup_step, 1)
                V.tensor_tensor(p_ir, bunch(pow_im, 1, m), re_m, ALU.mult).then_inc(setup_step, 1)
                steps[0] += 4
                dve.wait_ge(setup_step, steps[0])
                V.tensor_tensor(bunch(pow_re, m + 1, m), p_rr, p_ii, ALU.subtract).then_inc(setup_step, 1)
                steps[0] += 1
                tt(bunch(pow_im, m + 1, m), p_ri, p_ir, ALU.add)
            dve.wait_ge(params_loaded, 6 * 16)
            V.tensor_scalar(cc_p, cc_p, sign_sb[:, 0:1], None, ALU.mult).then_inc(powers_ready, 1)
            tt(s1, lam_r, lam_r, ALU.mult)
            tt(s2, lam_i, lam_i, ALU.mult)
            tt(s1, s1, s2, ALU.add)
            then(V.reciprocal(s1, s1))
            ts(s0, pow_re[:, 1, :], -1.0, ALU.add)
            tt(s2, s0, lam_r, ALU.mult)
            tt(s3, pow_im[:, 1, :], lam_i, ALU.mult)
            tt(s2, s2, s3, ALU.add)
            tt(par_re, s2, s1, ALU.mult)
            tt(s2, pow_im[:, 1, :], lam_r, ALU.mult)
            tt(s3, s0, lam_i, ALU.mult)
            tt(s2, s2, s3, ALU.subtract)
            tt(par_im, s2, s1, ALU.mult)

            def by_group(a):
                return a.unsqueeze(2).broadcast_to([P, GROUPS, GROUP])

            then(V.tensor_scalar(bb_q, bb_q, sign_sb[:, 1:2], None, ALU.mult))
            tt(b_tmp, bb_p, by_group(par_im), ALU.mult)
            tt(bb_p, bb_p, by_group(par_re), ALU.mult)
            tt(b_tmp2, bb_q, by_group(par_im), ALU.mult)
            tt(bb_p, bb_p, b_tmp2, ALU.add)
            tt(bb_q, bb_q, by_group(par_re), ALU.mult)
            tt(bb_q, bb_q, b_tmp, ALU.subtract)
            for par in range(2):
                half_rows = slice(64 * par, 64 * par + 64)
                for r in range(2):
                    then(V.tensor_copy(scan_re[half_rows, r, :], pow_re[half_rows, 8, par::2]))
                    ts(scan_im[half_rows, r, :], pow_im[half_rows, 8, par::2], -1.0 if r else 1.0, ALU.mult)
            for part in range(8):
                gs = slice(8 * part, 8 * part + 8)

                def powers(a):
                    return a[:, 0:8, gs][:, ::-1, :].rearrange("p i g -> p g i").unsqueeze(3).broadcast_to([P, 8, STEP, GROUP])

                def coefs(a):
                    return a[:, gs, :].unsqueeze(2).broadcast_to([P, 8, STEP, GROUP])

                tt(window[:, gs], coefs(bb_p), powers(pow_re), ALU.mult)
                tt(win_tmp, coefs(bb_q), powers(pow_im), ALU.mult)
                V.tensor_tensor(window[:, gs], window[:, gs], win_tmp, ALU.add).then_inc(window_ready, 1)
                dve.wait_ge(window_ready, part + 1)
            dve.wait_ge(std_ready, 2)
            V.reciprocal(rstd_stage, rstd_stage).then_inc(rstd_ready, 1)
            dve.wait_ge(consts_loaded, CONSTS * 16)
            lags_3d = lags.rearrange("p (g h) -> p g h", h=GROUP)
            tt(lags_3d, ident[:, P - GROUP:P].unsqueeze(1).broadcast_to([P, GROUPS, GROUP]),
               d_sb.unsqueeze(2).broadcast_to([P, GROUPS, GROUP]), ALU.mult)
            dve.wait_ge(lags_full, 1)
            V.tensor_tensor(lags, lags, psum[:, 0:2, :].rearrange("p b n -> p (b n)"), ALU.add).then_inc(lags_ready, 1)
            m1_banks(dve, V, 1)

            with dve.Fori(0, PASSES) as half:
                def rests(q):
                    for s in range(SLOTS):
                        rest(q, s)

                def rest(q, s):
                    dve.wait_ge(head_split, (half * QUADS + q) * SLOTS + s + 1)
                    V.tensor_tensor(w_lo[:, s, :], raw[:, s, :], w_hi[:, s, :].bitcast(F32),
                                    ALU.subtract).then_inc(rest_split, 1)

                def multiplied(q):
                    dve.wait_ge(unit_multiplied, (half * QUADS + q) * SLOTS + SLOTS)

                def scan_step(c):
                    now = half * SCAN + c * 4 + 1 + START
                    dve.wait_ge(scan_done, now)
                    V.tensor_tensor(scan_t[:, 0], state[:, c], scan_re[:, :, :], ALU.mult).then_inc(scan_done, 1)
                    V.tensor_tensor(scan_t[:, 1], state[:, c], scan_im[:, :, :], ALU.mult).then_inc(scan_done, 1)
                    dve.wait_ge(scan_done, now + 1)
                    V.tensor_tensor(state[:, c + 1], state[:, c + 1], scan_t[:, 0], ALU.add).then_inc(scan_done, 1)
                    dve.wait_ge(scan_done, now + 3)
                    V.tensor_tensor(state[:, c + 1], state[:, c + 1], scan_t[:, 1, ::-1, :], ALU.add).then_inc(scan_done, 1)

                def scale_h(k):
                    dve.wait_ge(xt_loaded[k], (half + 1) * 16)
                    if k >= 2:
                        dve.wait_ge(h_ready, half * KT_IN + k - 1)
                    else:
                        dve.wait_ge(rstd_loaded, (half + 1) * 16)
                    V.scalar_tensor_tensor(tmp[:, k % 2, :], xt_slot(k), gain_sb[:, k:k + 1],
                                           rstd_in, ALU.mult, ALU.mult).then_inc(h_scaled, 1)

                scale_h(0)
                for k in range(KT_IN):
                    if k + 1 < KT_IN:
                        scale_h(k + 1)
                    dve.wait_ge(h_head, half * KT_IN + k + 1)
                    V.tensor_tensor(h_lo[:, k, :], tmp[:, k % 2, :], h_hi[:, k, :].bitcast(F32),
                                    ALU.subtract).then_inc(h_ready, 1)
                    rest(Q_U + k // 4, k % 4)
                for q in range(4, 8):
                    rests(Q_U + q)
                rests(Q_ZS)
                rests(Q_ZS + 1)
                state_inputs(dve, V, half, 1)
                dve.wait_ge(state_in_act, (half + 1) * 16)
                dve.wait_ge(state_in_dve, (half + 1) * 16)
                V.tensor_copy(state[:, 0], carry[:, :, :]).then_inc(scan_done, 1)
                with dve.Fori(0, STEPS // 8) as i:
                    for c in range(8):
                        scan_step(i * 8 + c)
                dve.wait_ge(scan_done, half * SCAN + 4 * STEPS + 1 + START)
                V.tensor_copy(carry[:, :, :], state[:, STEPS]).then_inc(scan_done, 1)
                shift_states(dve, V, half, 0, 0)
                shift_states(dve, V, half, 1, 0)
                for j in range(8):
                    if j + 2 < 8:
                        shift_states(dve, V, half, j + 2, 0)
                for j in range(8):
                    dve.wait_ge(g_head, half * 8 + j + 1)
                    dve.wait_ge(y_full, half * 8 + (5 + j // 4))
                    V.tensor_tensor(y_lo[:, j, :].rearrange("p (c t) -> p c t", t=STEP), g_tile(j),
                                    y_hi[:, j, :].rearrange("p (c t) -> p c t", t=STEP).bitcast(F32),
                                    ALU.subtract).then_inc(g_ready, 1)
                dve.wait_ge(rest_split, (half * QUADS + Q_GLU + 1) * SLOTS + SLOTS)
                rests(Q_GLU + 1)

                def glu(b):
                    emptied = set_b_emptied if b else set_a_emptied
                    base = half * 24 + 12 * b
                    for n in range(4):
                        k = 4 * b + n
                        dve.wait_ge(emptied, (half * BLOCKS_SET + B_GLU) * 4 + n + 1 + START)
                        if n or b:
                            dve.wait_ge(glu_step, base + 3 * n)
                        V.tensor_tensor(tmp[:, 0, :], y_hi[:, k, :].bitcast(F32), y_lo[:, k, :].bitcast(F32),
                                        ALU.add).then_inc(glu_step, 1)
                        dve.wait_ge(glu_step, base + 3 * n + 1)
                        V.tensor_tensor(tmp[:, 0, :], tmp[:, 0, :], gate[:, n, :], ALU.mult).then_inc(glu_step, 1)
                        dve.wait_ge(glu_step, base + 3 * n + 2)
                        V.tensor_tensor(z_s[:, k, :], z_s[:, k, :], tmp[:, 0, :], ALU.mult).then_inc(glu_step, 1)

                rests(Q_GLU + 2)
                glu(0)
                rests(Q_GLU + 3)
                rests(Q_Q)
                multiplied(Q_Q)
                glu(1)
                rests(Q_Q + 1)
                for n in range(2):
                    dve.wait_ge(ys_head, half * 2 + n + 1)
                    V.tensor_tensor(y_lo[:, 4 * n:4 * n + 4, :], z_s[:, 4 * n:4 * n + 4, :],
                                    y_hi[:, 4 * n:4 * n + 4, :].bitcast(F32), ALU.subtract).then_inc(ys_ready, 1)
                for q in range(2, 4):
                    rests(Q_Q + q)

                def rotate(dst, b, emptied, first, j):
                    dve.wait_ge(rope_loaded, (half + 1) * 16)
                    base = half * 32 + 16 * b + 8 * j
                    if j or b:
                        dve.wait_ge(rope_done, base)
                    cos, sin = rope_sb[:, 0, :], rope_sb[:, 1, :]
                    one, two = psum[:, first + j, :], psum[:, first + 2 + j, :]
                    V.tensor_tensor(gate[:, 0, :], one, cos, ALU.mult).then_inc(rope_step, 1)
                    V.tensor_tensor(gate[:, 1, :], two, sin, ALU.mult).then_inc(rope_step, 1)
                    V.tensor_tensor(gate[:, 2, :], one, sin, ALU.mult).then_inc(emptied, 1)
                    V.tensor_tensor(gate[:, 3, :], two, cos, ALU.mult).then_inc(emptied, 1)
                    dve.wait_ge(rope_step, half * 8 + 4 * b + 2 * j + 2)
                    dve.wait_ge(emptied, (half * BLOCKS_SET + B_QK) * 4 + 2 * j + 2 + START)
                    for hh in range(4):
                        pair, par = (4 * j + hh) // 2, hh % 2
                        rows = slice(32 * hh, 32 * hh + 32)
                        V.tensor_tensor(dst[64 * par:64 * par + 32, pair, :], gate[rows, 0, :], gate[rows, 1, :],
                                        ALU.subtract).then_inc(rope_done, 1)
                        V.tensor_tensor(dst[64 * par + 32:64 * par + 64, pair, :], gate[rows, 2, :], gate[rows, 3, :],
                                        ALU.add).then_inc(rope_done, 1)

                rests(Q_K)
                multiplied(Q_K)
                for j in range(2):
                    rotate(q_t, 0, set_a_emptied, 0, j)
                    rests(Q_K + 1 + j)
                rests(Q_K + 3)
                rests(Q_V)
                multiplied(Q_V)
                for j in range(2):
                    rotate(k_t, 1, set_b_emptied, 4, j)
                    rests(Q_V + 1 + j)
                rests(Q_V + 3)
                rests(Q_V + 4)
                multiplied(Q_V + 4)
                for i in range(4):
                    V.tensor_copy(v_row[:, i, 0:512], psum[:, i, :]).then_inc(set_a_emptied, 1)
                for q in range(5, 8):
                    rests(Q_V + q)
                rests(Q_ZR)
                multiplied(Q_ZR)
                for i in range(4):
                    V.tensor_copy(v_row[:, i, 512:1024], psum[:, 4 + i, :]).then_inc(set_b_emptied, 1)
                for q in range(1, 8):
                    rests(Q_ZR + q)
                rests(Q_S)
                dve.wait_ge(tables_loaded, (half + 1) * 3 * 16)
                dve.wait_ge(rope_done, (half + 1) * 32)

                def inverse(t):
                    for par in range(2):
                        dve.wait_ge(ostd_ready, half * 2 * BLOCKS + 2 * t + par + 1)
                        V.reciprocal(o_sq[:, par], o_sq[:, par]).then_inc(o_inverse, 1)

                for t in range(BLOCKS):
                    n = half * BLOCKS + t
                    tok = slice(BLOCK * t, BLOCK * t + BLOCK)
                    if t:
                        dve.wait_ge(o_full, 2 * n)
                    V.tensor_tensor(q_xi, q_t[:, :, tok], xi_sb.rearrange("p (a n) -> p a n", a=4),
                                    ALU.mult).then_inc(q_xi_ready, 1)
                    for par in range(2):
                        dve.wait_ge(scores_full, 2 * n + par + 1)
                        V.tensor_tensor(s_dec[:, par, :], psum[:, 1 + par, :], dmat_sb[:, par, :],
                                        ALU.mult).then_inc(scores_decayed, 1)
                    dve.wait_ge(k_turned, n + 1)
                    if t:
                        dve.wait_ge(kv_full, n)
                    V.tensor_tensor(k_zeta, psum[:, 0, :], zeta_sb, ALU.mult).then_inc(k_zeta_ready, 1)
                    if t:
                        inverse(t - 1)
                    dve.wait_ge(kv_full, n + 1)
                    for a in range(4):
                        V.scalar_tensor_tensor(ret_state[:, a, :], ret_state[:, a, :], gdec_sb[:, a:a + 1],
                                               psum[:, 5, 128 * a:128 * a + 128], ALU.mult, ALU.add
                                               ).then_inc(state_ready, 1)
                inverse(BLOCKS - 1)
                with dve.Fori(0, MERGES) as b:
                    q0 = Q_S + b * Q_MERGE
                    for q in range(1, 7):
                        rests(q0 + q)
                    multiplied(q0 + 6)
                    dve.wait_ge(set_a_emptied, (half * BLOCKS_SET + B_S + 1 + b) * 4 + START)
                    for n in range(4):
                        V.tensor_tensor(m_t[:, b * 4 + n, :], gate[:, n, :], psum[:, 4 + n, :],
                                        ALU.mult).then_inc(set_b_emptied, 1)
                for n in range(2):
                    dve.wait_ge(yr_head, half * 2 + n + 1)
                    V.tensor_tensor(y_lo[:, 4 * n:4 * n + 4, :], z_r[:, 4 * n:4 * n + 4, :],
                                    y_hi[:, 4 * n:4 * n + 4, :].bitcast(F32), ALU.subtract).then_inc(yr_ready, 1)
                def m_rests(n):
                    dve.wait_ge(m_head, half * 4 + n + 1)
                    V.tensor_tensor(h_lo[:, 4 * n:4 * n + 4, :], m_t[:, 4 * n:4 * n + 4, :],
                                    h_hi[:, 4 * n:4 * n + 4, :].bitcast(F32), ALU.subtract).then_inc(m_ready, 1)

                def merge_sums(b):
                    multiplied(Q_R + b * Q_MERGE + 6)
                    dve.wait_ge(set_a_emptied, (half * BLOCKS_SET + B_R + 1 + b) * 4 + START)
                    for n in range(4):
                        V.tensor_tensor(gate[:, n, :], gate[:, n, :], psum[:, 4 + n, :],
                                        ALU.mult).then_inc(set_b_emptied, 1)
                    for n in range(4):
                        dve.wait_ge(set_b_emptied, (half * BLOCKS_SET + B_R + b) * 4 + n + 1 + START)
                        V.tensor_tensor(m_t[:, b * 4 + n, :], m_t[:, b * 4 + n, :], gate[:, n, :],
                                        ALU.add).then_inc(m_added, 1)

                with dve.Fori(0, MERGES - 1) as b:
                    for q in range(1, 7):
                        rests(Q_R + b * Q_MERGE + q)
                    merge_sums(b)
                for q in range(1, 6):
                    rests(Q_R + (MERGES - 1) * Q_MERGE + q)
                for n in range(MERGES - 1):
                    m_rests(n)
                rests(Q_OUT)
                merge_sums(MERGES - 1)
                rests(Q_OUT + 1)
                m_rests(MERGES - 1)
                dve.wait_ge(m_ready, (half + 1) * 4)
                dve.wait_ge(gain_row_loaded, (half + 1) * 16)

                def gained(c, i, emptied):
                    dve.wait_ge(out_squared, half * 16 + 4 * c + i + 1 + START)
                    cols = slice(COLS * c, COLS * c + COLS)
                    V.tensor_tensor(o_row[:, i, cols], psum[:, 4 * (c % 2) + i, :], gain_row[:, cols],
                                    ALU.mult).then_inc(emptied, 1)

                for c in range(3):
                    for q in range(2 if c == 0 else 1, 5):
                        rests(Q_OUT + 4 * c + q)
                    multiplied(Q_OUT + 4 * c + 4)
                    for i in range(4):
                        gained(c, i, set_b_emptied if c % 2 else set_a_emptied)
                for q in range(1, 4):
                    rests(Q_OUT + 12 + q)
                dve.wait_ge(x_loaded, (half + 1) * 4 * 16)

                def finish(i):
                    dve.wait_ge(out_std, half * 4 + i + 1)
                    V.reciprocal(rstd_out[:, i:i + 1], rstd_out[:, i:i + 1]).then_inc(out_stat, 1)
                    if i < 2:
                        return
                    dve.wait_ge(out_stat, half * 8 + 2 * i + 2)
                    dve.wait_ge(set_b_emptied, (half * BLOCKS_SET + B_OUT + 1) * 4 + i + 1 + START)
                    V.scalar_tensor_tensor(o_row[:, i, :], o_row[:, i, :], rstd_out[:, i:i + 1],
                                           x_rows_2[:, i - 2, :],
                                           ALU.mult, ALU.add).then_inc(out_ready, 1)

                for i in range(4):
                    dve.wait_ge(out_squared, half * 16 + 12 + i + 1 + START)
                    V.tensor_reduce(rstd_out[:, i:i + 1], ssq[:, i, :], AX_X, ALU.add).then_inc(out_stat, 1)
                    gained(3, i, set_b_emptied)
                    finish(i)

        @block.tensor
        def _(pe):
            T = nc.tensor
            pe.sem_inc(unit_multiplied, SLOTS)
            pe.wait_ge(consts_loaded, CONSTS * 16)
            for n in range(PASSES * KT_IN):
                pe.wait_ge(squared, n + 1 + SLOTS)
                T.matmul(psum[:, 6 + n // KT_IN, :], ones_sb[:, :], plain("w_lo", COLS * (n % SLOTS), COLS),
                         start=(n % KT_IN == 0), stop=(n % KT_IN == KT_IN - 1)).then_inc(square_added, 1)
            for b in range(16):
                if b % 2 == 0:
                    pe.wait_ge(window_ready, b // 2 + 1)
                if b >= 4:
                    pe.wait_ge(m2_copied, b - 3)
                for a in range(4):
                    g = 4 * b + a
                    w = window[:, g].rearrange("p i h -> p (i h)")
                    m2 = T.transpose(psum[:, 2 + b % 4, 128 * a:128 * a + 128], w, ident)
                    lag = T.matmul(psum[:, g // 32, GROUP * (g % 32):GROUP * (g % 32) + GROUP], w, cc_p[:, g, :],
                                   start=True, stop=True)
                    if a == 3:
                        m2.then_inc(m2_full, 1)
            lag.then_inc(lags_full, 1)
            pe.wait_ge(lags_ready, 1)
            for n in range(16):
                t = n // 2
                if n >= 8:
                    pe.wait_ge(m1_dve if n % 2 else m1_act, (n - 8) // 2 + 1)
                elif 2 <= n < 6:
                    pe.wait_ge(m2_copied, 16)
                elif n >= 6:
                    pe.wait_ge(std_ready, 2)
                move = GROUP * (STEP - 1 - t)
                T.matmul(psum[:, n % 8, :], eye_sb[:, move:move + P], lags[:, COLS * (n % 2):COLS * (n % 2) + COLS],
                         start=True, stop=True).then_inc(m1_full, 1)
            pe.wait_ge(m1_act, 8)
            pe.wait_ge(m1_dve, 8)

            with pe.Fori(0, PASSES) as half:
                def unit_ready(q, s):
                    pe.wait_ge(rest_split, (half * QUADS + q) * SLOTS + s + 1 + SLOTS)

                def columns_out(q, first, x_hi, x_lo, tiles, ready=None):
                    for k in range(tiles):
                        if ready is not None:
                            ready(k)
                        s = k % SLOTS
                        unit_ready(q + k // SLOTS, s)
                        for n in range(4):
                            cols = slice(P * n, P * n + P)
                            bank = psum[:, first + n, :]
                            T.matmul(bank, w_hi[:, s, cols], x_hi[:, k, :], start=(k == 0), stop=False)
                            T.matmul(bank, w_lo[:, s, cols], x_hi[:, k, :], start=False, stop=False)
                            last = T.matmul(bank, w_hi[:, s, cols], x_lo[:, k, :], start=False, stop=(k == tiles - 1))
                        last.then_inc(unit_multiplied, 1)

                def rows_out(q, first, x_hi, x_lo, pick, ready=None, tiles=KT_IN):
                    for k in range(tiles):
                        if ready is not None:
                            ready(k)
                        s = k % SLOTS
                        unit_ready(q + k // SLOTS, s)
                        for n in range(4):
                            bank = psum[:, first + n, :]
                            T.matmul(bank, pick(x_hi, k, n), w_hi[:, s, :], start=(k == 0), stop=False)
                            T.matmul(bank, pick(x_hi, k, n), w_lo[:, s, :], start=False, stop=False)
                            last = T.matmul(bank, pick(x_lo, k, n), w_hi[:, s, :], start=False, stop=(k == KT_IN - 1))
                        last.then_inc(unit_multiplied, 1)

                def empty(which, b):
                    pe.wait_ge(which, (half * BLOCKS_SET + b) * 4 + START)

                def block_tokens(a, k, n):
                    return a[:, k, P * n:P * n + P]

                empty(set_a_emptied, 0)
                columns_out(Q_U, 0, h_hi, h_lo, KT_IN, lambda k: pe.wait_ge(h_ready, half * KT_IN + k + 1))
                empty(set_b_emptied, 0)
                columns_out(Q_U + 4, 4, h_hi, h_lo, KT_IN)

                def step_inputs():
                    empty(set_b_emptied, B_U + 1)
                    for j in range(8):
                        if j >= 4:
                            pe.wait_ge(state_in_dve if j % 2 else state_in_act, half * 16 + 4 * ((j - 4) // 2 + 1))
                        pe.wait_ge(m2_loaded[j // 4], (half + 1) * 64)
                        pe.wait_ge(u_loaded[j // 4], (half + 1) * 64)
                        for a in range(8):
                            last = T.matmul(psum[:, 4 + j % 4, 64 * a:64 * a + 64], m2_tile(j)[:, 128 * a:128 * a + 128],
                                            u_step[:, 8 * j + a, :], start=True, stop=True)
                        last.then_inc(step_in_full, 1)

                empty(set_a_emptied, B_U + 1)
                columns_out(Q_ZS, 0, h_hi, h_lo, KT_IN, lambda k: step_inputs() if k == 4 else None)
                pe.wait_ge(state_in_act, (half + 1) * 16)
                pe.wait_ge(state_in_dve, (half + 1) * 16)
                columns_out(Q_ZS + 4, 4, h_hi, h_lo, KT_IN)
                empty(set_a_emptied, B_ZS + 1)
                for j in range(8):
                    if j >= 4:
                        pe.wait_ge(gelu_done, half * 8 + j - 3)
                    pe.wait_ge(shifted_act, half * 16 + 2 * j + 2)
                    pe.wait_ge(shifted_dve, half * 16 + 2 * j + 2)
                    pe.wait_ge(mat_loaded[j], (half + 1) * 32)
                    for a in range(8):
                        bank = psum[:, j % 4, 64 * a:64 * a + 64]
                        cols = slice(128 * a, 128 * a + 128)
                        T.matmul(bank, mat_tile(j, 0)[:, cols], u_step[:, 8 * j + a, :], start=True, stop=False)
                        last = T.matmul(bank, mat_tile(j, 1)[:, cols], sc_ring[:, j % 2, a, :], start=False, stop=True)
                    last.then_inc(y_full, 1)
                pe.wait_ge(gelu_done, (half + 1) * 8)
                columns_out(Q_GLU, 0, y_hi, y_lo, KT_MID, lambda k: pe.wait_ge(g_ready, half * 8 + k + 1))
                empty(set_b_emptied, B_ZS + 1)
                columns_out(Q_GLU + 2, 4, y_hi, y_lo, KT_MID)
                empty(set_a_emptied, B_QK)
                columns_out(Q_Q, 0, h_hi, h_lo, KT_IN)
                empty(set_b_emptied, B_QK)
                columns_out(Q_K, 4, h_hi, h_lo, KT_IN)
                empty(set_a_emptied, B_V)
                rows_out(Q_V, 0, h_hi, h_lo, block_tokens)
                empty(set_b_emptied, B_V)
                rows_out(Q_V + 4, 4, h_hi, h_lo, block_tokens)
                empty(set_a_emptied, B_ZR)
                columns_out(Q_ZR, 0, h_hi, h_lo, KT_IN)
                empty(set_b_emptied, B_ZR)
                columns_out(Q_ZR + 4, 4, h_hi, h_lo, KT_IN)
                empty(set_a_emptied, B_ZR + 1)
                pe.wait_ge(rope_done, (half + 1) * 32)
                def square_sums(t):
                    n = half * BLOCKS + t
                    for par in range(2):
                        pe.wait_ge(o_squared, 2 * n + par + 1)
                        if t:
                            pe.wait_ge(ostd_ready, 2 * n + par - 1)
                        T.matmul(psum[:, 6 + par, :], ones_sb[:, :],
                                 o_sq[:, par].rearrange("p a n -> p (a n)"), start=True, stop=True).then_inc(osum_full, 1)

                def scores(t):
                    n = half * BLOCKS + t
                    tok = slice(BLOCK * t, BLOCK * t + BLOCK)
                    if t:
                        pe.wait_ge(scores_decayed, 2 * n)
                    for a in range(4):
                        for par in range(2):
                            rows = slice(64 * par, 64 * par + 64)
                            last = T.matmul(psum[:, 1 + par, 128 * a:128 * a + 128], k_t[rows, a, tok], q_t[rows, a, tok],
                                            start=True, stop=True)
                            if a == 3:
                                last.then_inc(scores_full, 1)
                    if t:
                        pe.wait_ge(k_zeta_ready, n)
                    for a in range(4):
                        last = T.transpose(psum[:, 0, 128 * a:128 * a + 128], k_t[:, a, tok], ident)
                    last.then_inc(k_turned, 1)

                scores(0)
                empty(set_b_emptied, B_ZR + 1)
                for t in range(BLOCKS):
                    n = half * BLOCKS + t
                    pe.wait_ge(q_xi_ready, n + 1)
                    pe.wait_ge(state_ready, 4 * n + START)
                    for par in range(2):
                        rows = slice(64 * par, 64 * par + 64)
                        pe.wait_ge(scores_decayed, 2 * n + par + 1)
                        if t:
                            pe.wait_ge(o_copied, 2 * n + par - 1)
                        for a in range(4):
                            head = 2 * a + par
                            bank = psum[:, 3 + par, 128 * a:128 * a + 128]
                            T.matmul(bank, v_row[:, t, V_HEAD * head:V_HEAD * head + V_HEAD],
                                     s_dec[:, par, 128 * a:128 * a + 128], start=True, stop=False)
                            last = T.matmul(bank, ret_state[rows, a, :], q_xi[rows, a, :], start=False, stop=True)
                        last.then_inc(o_full, 1)
                    pe.wait_ge(k_zeta_ready, n + 1)
                    for a in range(4):
                        for par in range(2):
                            head = 2 * a + par
                            last = T.matmul(psum[64 * par:64 * par + 64, 5, 128 * a:128 * a + 128],
                                            k_zeta[:, 64 * head:64 * head + 64],
                                            v_row[:, t, V_HEAD * head:V_HEAD * head + V_HEAD], start=True, stop=True)
                    last.then_inc(kv_full, 1)
                    if t + 1 < BLOCKS:
                        scores(t + 1)
                    square_sums(t)
                pe.wait_ge(ostd_ready, (half + 1) * BLOCKS * 2)
                pe.wait_ge(state_ready, (half + 1) * BLOCKS * 4 + START)
                pe.wait_ge(o_copied, (half + 1) * BLOCKS * 2)
                pe.wait_ge(ys_ready, (half + 1) * 2)
                pe.sem_inc(pe_waited, 1)
                with pe.Fori(0, MERGES) as b:
                    q0 = Q_S + b * Q_MERGE
                    columns_out(q0, 0, h_hi, h_lo, KT_IN)
                    empty(set_b_emptied, B_S + b)
                    columns_out(q0 + 4, 4, y_hi, y_lo, KT_MID)
                    empty(set_a_emptied, B_S + 1 + b)
                    pe.sem_inc(pe_waited, 1)
                with pe.Fori(0, MERGES) as b:
                    q0 = Q_R + b * Q_MERGE
                    columns_out(q0, 0, h_hi, h_lo, KT_IN)
                    empty(set_b_emptied, B_R + b)
                    pe.wait_ge(yr_ready, (half + 1) * 2)
                    columns_out(q0 + 4, 4, y_hi, y_lo, KT_MID)
                    empty(set_a_emptied, B_R + 1 + b)
                    pe.sem_inc(pe_waited, 1)
                for c in range(4):
                    which, first = (set_a_emptied, 0) if c % 2 == 0 else (set_b_emptied, 4)
                    empty(which, B_OUT + c // 2)
                    ready = (lambda k: pe.wait_ge(m_ready, half * 4 + k // 4 + 1)) if c == 0 else None
                    rows_out(Q_OUT + 4 * c, first, h_hi, h_lo, block_tokens, ready, KT_IN if c < 3 else KT_IN - SLOTS)
                for s in range(SLOTS):
                    unit_ready(QUADS - 1, s)
                for n in range(4):
                    for s in range(SLOTS):
                        k = KT_IN - SLOTS + s
                        bank = psum[:, 4 + n, :]
                        T.matmul(bank, block_tokens(h_hi, k, n), w_hi[:, s, :], start=False, stop=False)
                        T.matmul(bank, block_tokens(h_hi, k, n), w_lo[:, s, :], start=False, stop=False)
                        last = T.matmul(bank, block_tokens(h_lo, k, n), w_hi[:, s, :], start=False, stop=(s == SLOTS - 1))
                        if n == 3:
                            last.then_inc(unit_multiplied, 1)
                        elif s == SLOTS - 1:
                            last.then_inc(row_block_full, 1)


def retention_tables():
    log_g = np.log1p(-np.exp2(-5.0 - np.arange(HEADS)))
    idx = np.arange(BLOCK)
    scale = QK_HEAD ** -0.5
    ahead = (idx[:, None] // CHUNK) > (idx[None, :] // CHUNK)
    dist = np.abs(idx[None, :] - idx[:, None])
    dmat = np.where(ahead, 0.0, np.exp(dist[None] * log_g[:, None, None])) * scale
    dmat = dmat.reshape(4, 2, BLOCK, BLOCK).transpose(2, 1, 0, 3).reshape(BLOCK, -1)
    zeta = np.exp((BLOCK - 1 - idx)[:, None] * log_g[None, :]) * scale
    zeta = np.repeat(zeta, QK_HEAD, axis=1)
    xi = np.exp((idx + 1.0)[None, :] * log_g[:, None])
    xi = np.repeat(xi.reshape(4, 2, 1, BLOCK), QK_HEAD, axis=2).transpose(1, 2, 0, 3).reshape(P, -1)
    gdec = np.repeat(np.exp(BLOCK * log_g).reshape(4, 2).T, QK_HEAD, axis=0)
    return [np.ascontiguousarray(a, dtype=np.float32) for a in (dmat, zeta, xi, gdec)]


def rope_table():
    half = QK_HEAD // 2
    inv = np.float32(ROPE_BASE) ** (-np.arange(0, QK_HEAD, 2, dtype=np.float32) / np.float32(QK_HEAD))
    angle = (np.arange(SEQ, dtype=np.float32)[None, :] * inv.astype(np.float32)[:, None]).astype(np.float32)
    both = np.stack([np.cos(angle.astype(np.float64)), np.sin(angle.astype(np.float64))], 1)
    both = np.tile(both, (P // half, 1, 1)).reshape(P, 2, PASSES, TOK).transpose(2, 0, 1, 3)
    return np.ascontiguousarray(both, dtype=np.float32)


def layouts(x, norm_pre, w_in, lam_re, lam_im, log_step, s5_b_re, s5_b_im, s5_c_re, s5_c_im,
            s5_d, w_glu, b_glu, w_proj_s5, w_proj_ret, w_out, norm_post):
    def units(w):
        r, c = w.shape
        return w.reshape(r // P, P, c // COLS, COLS).transpose(2, 0, 1, 3)

    w = w_in[0]
    at = np.cumsum([0, S5_WIDTH, S5_WIDTH, 512, 512, S5_WIDTH, S5_WIDTH, D_MODEL, D_MODEL])
    part = [w[:, a:b] for a, b in zip(at[:-1], at[1:])]
    turn = (P * np.arange(KT_MID)[:, None] + np.arange(P).reshape(8, GROUP).T.reshape(1, -1)).reshape(-1)
    rot = np.arange(512).reshape(HEADS, 2, QK_HEAD // 2).transpose(1, 0, 2).reshape(-1)
    runs = [units(part[0][:, turn]), units(part[1][:, turn]), units(w_glu[0][turn][:, turn]), units(part[2][:, rot]), units(part[3][:, rot]),
            units(part[4]), units(part[5])]
    for gate, proj in ((part[6], w_proj_s5[0][turn]), (part[7], w_proj_ret[0])):
        g, p = units(gate), units(proj)
        for b in range(MERGES):
            runs += [g[b:b + 1], p[b:b + 1]]
    runs.append(units(w_out[0]))
    stream = np.concatenate([r.reshape(-1, P, COLS) for r in runs], axis=0)

    def states(a):
        return np.ascontiguousarray(np.concatenate([a.T, a.T], axis=0))

    def stack(a, b):
        both = np.concatenate([a.transpose(1, 0, 2), b.transpose(1, 0, 2)], axis=0)
        return np.ascontiguousarray(both.reshape(P, -1))

    br, bi = s5_b_re[0], s5_b_im[0]
    cr, ci = s5_c_re[0].transpose(0, 2, 1), s5_c_im[0].transpose(0, 2, 1)
    d = np.tile(s5_d[0].reshape(GROUPS, GROUP).T, (STEP, 1))
    signs = np.ones((P, 2), np.float32)
    signs[64:, 0] = -1.0
    signs[:64, 1] = -1.0
    dmat, zeta, xi, gdec = retention_tables()
    xs = x[0]
    arrays = {
        "x": xs.reshape(SEQ // P, P, D_MODEL),
        "xT": xs.reshape(PASSES, TOK, KT_IN, P).transpose(0, 2, 3, 1).reshape(PASSES * KT_IN, P, TOK),
        "wstream": stream,
        "gain_in": norm_pre[0].reshape(KT_IN, P).T,
        "gain_out": np.broadcast_to(norm_post[0], (P, D_MODEL)),
        "b_glu": b_glu[0][turn].reshape(KT_MID, P).T,
        "lam_re": states(lam_re[0]),
        "lam_im": states(lam_im[0]),
        "log_step": np.broadcast_to(log_step[0], (P, GROUPS)),
        "b_ri": stack(br, bi), "b_ir": stack(bi, br),
        "c_ri": stack(cr, ci), "c_ir": stack(ci, cr),
        "d_rep": d, "signs": signs, "eye": np.eye(P, 2 * P - GROUP, dtype=np.float32),
        "ones": np.ones((P, P), np.float32),
        "dmat": dmat, "zeta": zeta, "xi": xi, "gdec": gdec, "rope": rope_table(),
    }
    return {n: np.ascontiguousarray(a) for n, a in arrays.items()}


def kernel(**inputs):
    import concourse.bacc as bacc
    from concourse.bass_utils import run_bass_kernel_spmd

    arrays = layouts(**{n: np.asarray(a) for n, a in inputs.items()})
    nc = bacc.Bacc("TRN2", target_bir_lowering=False, num_devices=1)
    args = {n: nc.dram_tensor(f"in_{n}", a.shape, F32, kind="ExternalInput").ap() for n, a in arrays.items()}
    args["mats"] = nc.dram_tensor("mats", (3, 8, P, 1024), F32, kind="Internal").ap()
    args["rstd"] = nc.dram_tensor("rstd", (PASSES, P, TOK), F32, kind="Internal").ap()
    args["turned"] = nc.dram_tensor("turned", (2 * KT_MID, P * TOK), F32, kind="Internal").ap()
    args["out"] = nc.dram_tensor("out_rows", (SEQ // P, P, D_MODEL), F32, kind="ExternalOutput").ap()
    build_program(nc, **args)
    r = run_bass_kernel_spmd(nc, [{f"in_{n}": a for n, a in arrays.items()}], core_ids=[0])
    return r.results[0]["out_rows"].reshape(1, SEQ, D_MODEL)
```
